# Optimizing a Trainium2 kernel written in Bass

```python
import jax, jax.numpy as jnp
from jax import lax
import numpy as np

D_MODEL = 1024
BATCH = 1
SEQ = 512
DEPTH = 2
DEC_BATCH = 8
DEC_SEQ = 1
PAST_LEN = 4096
PAGE_SIZE = 128

N_AB = (DEPTH + 1) // 2
N_C = DEPTH // 2
EPS = 1e-6
D_A = D_MODEL // 2
CONV_W = 31
H_B = 4
D_BV = D_MODEL // 2
D_BK = D_BV // 2
DK_B = D_BK // H_B
DV_B = D_BV // H_B
GATE_RANK = 16
GATE_TAU = 16.0
GLA_CHUNK = 64
D_IN_AB = 2 * D_A + 2 * D_BK + 2 * D_BV + GATE_RANK
H_C = 16
D_NOPE = 64
D_ROPE = 32
D_V = 64
R_Q = 384
R_KV = 256
D_IN_C = R_Q + R_KV + D_ROPE
ROPE_BASE = 10000.0
MLA_SCALE = (D_NOPE + D_ROPE) ** -0.5
Q_BLOCK = 128
H_P = 8
N_KEYS = 128
N_EXPERTS = N_KEYS * N_KEYS
D_KEY = 256
D_HALF = D_KEY // 2
TOPK = 16
PEER_BLOCK = 128

kernel_name = 'hybrid_conv_gla_mla_peer_step'

def rms_norm(x, g):
    xf = x.astype(jnp.float32)
    y = xf * lax.rsqrt(jnp.mean(xf * xf, axis=-1, keepdims=True) + EPS)
    return (y * g.astype(jnp.float32)).astype(x.dtype)

def layer_norm(x, g, b):
    xf = x.astype(jnp.float32)
    mu = jnp.mean(xf, axis=-1, keepdims=True)
    xc = xf - mu
    y = xc * lax.rsqrt(jnp.mean(xc * xc, axis=-1, keepdims=True) + EPS)
    return (y * g.astype(jnp.float32) + b.astype(jnp.float32)).astype(x.dtype)

def rope(x, pos):
    half = D_ROPE // 2
    inv = jnp.power(ROPE_BASE, -jnp.arange(half, dtype=jnp.float32) / half)
    ang = pos.astype(jnp.float32)[:, None] * inv[None, :]
    shape = (ang.shape[0],) + (1,) * (x.ndim - 3) + (half,)
    cos = jnp.cos(ang).reshape(shape)
    sin = jnp.sin(ang).reshape(shape)
    xf = x.astype(jnp.float32)
    x1, x2 = xf[..., :half], xf[..., half:]
    return jnp.concatenate([x1 * cos - x2 * sin, x1 * sin + x2 * cos], axis=-1).astype(x.dtype)

def gla_scan(q, k, v, log_a, s0):
    B, T, H, _ = q.shape
    DV = v.shape[-1]
    c = min(GLA_CHUNK, T)
    nc = -(-T // c)
    pad = nc * c - T

    def chunks(a):
        a = jnp.pad(a.astype(jnp.float32), ((0, 0), (0, pad), (0, 0), (0, 0)))
        return jnp.moveaxis(a.reshape(B, nc, c, H, a.shape[-1]), 1, 0)

    idx = jnp.arange(c)
    causal = (idx[:, None] >= idx[None, :])[None, :, :, None, None]

    def step(s, inp):
        qc, kc, vc, gc = inp
        b = jnp.cumsum(gc, axis=1)
        o_inter = jnp.einsum('bihk,bhkv->bihv', qc * jnp.exp(b), s)
        decay = jnp.exp(jnp.where(causal, b[:, :, None] - b[:, None, :], -jnp.inf))
        attn = jnp.einsum('bihk,bijhk->bhij', qc, decay * kc[:, None])
        o_intra = jnp.einsum('bhij,bjhv->bihv', attn, vc)
        b_end = b[:, -1]
        s_new = jnp.exp(b_end)[..., None] * s + jnp.einsum(
            'bjhk,bjhv->bhkv', kc * jnp.exp(b_end[:, None] - b), vc)
        return s_new, o_inter + o_intra

    s_fin, o = lax.scan(step, s0.astype(jnp.float32),
                        (chunks(q), chunks(k), chunks(v), chunks(log_a)))
    o = jnp.moveaxis(o, 0, 1).reshape(B, nc * c, H, DV)[:, :T]
    return o, s_fin

def even_layer(x, conv_buf, s0, norm_g, w_in, conv_w, conv_b, ln_g, ln_b,
               w_gate, b_gate, head_g, w_out):
    B, T, _ = x.shape
    z = rms_norm(x, norm_g) @ w_in
    offs = [D_A, 2 * D_A, 2 * D_A + D_BK, 2 * D_A + 2 * D_BK,
            2 * D_A + 2 * D_BK + D_BV, 2 * D_A + 2 * D_BK + 2 * D_BV]
    a_val, a_gate, q, k, v, r, g_low = jnp.split(z, offs, axis=-1)
    u = a_val * jax.nn.sigmoid(a_gate)
    ubuf = jnp.concatenate([conv_buf.astype(u.dtype), u], axis=1)
    c = lax.conv_general_dilated(ubuf, conv_w.astype(u.dtype)[:, None, :], (1,), 'VALID',
                                 dimension_numbers=('NWC', 'WIO', 'NWC'),
                                 feature_group_count=D_A) + conv_b
    a_out = jax.nn.silu(layer_norm(c, ln_g, ln_b))
    new_buf = ubuf[:, ubuf.shape[1] - (CONV_W - 1):]
    log_a = jax.nn.log_sigmoid((g_low @ w_gate + b_gate).astype(jnp.float32)) / GATE_TAU
    o, s_new = gla_scan(q.reshape(B, T, H_B, DK_B) * DK_B ** -0.5,
                        k.reshape(B, T, H_B, DK_B),
                        v.reshape(B, T, H_B, DV_B),
                        log_a.reshape(B, T, H_B, DK_B), s0)
    b_out = rms_norm(o, head_g).astype(x.dtype).reshape(B, T, D_BV) * jax.nn.silu(r)
    y = jnp.concatenate([a_out, b_out], axis=-1) @ w_out
    return x + y, new_buf, s_new.astype(x.dtype)

def mla_attend(q_lat, q_pe, ckv, kpe, ckv_past, kpe_past):
    B, T, H, R = q_lat.shape
    qb = min(Q_BLOCK, T)
    nb = -(-T // qb)
    pad = nb * qb - T

    def blocks(a):
        a = jnp.pad(a, ((0, 0), (0, pad)) + ((0, 0),) * (a.ndim - 2))
        return jnp.moveaxis(a.reshape((B, nb, qb) + a.shape[2:]), 1, 0)

    starts = jnp.arange(nb, dtype=jnp.int32) * qb
    kidx = jnp.arange(T, dtype=jnp.int32)

    def block(args):
        ql, qp, start = args
        qidx = start + jnp.arange(qb, dtype=jnp.int32)
        s = (jnp.einsum('bqhr,bkr->bhqk', ql, ckv)
             + jnp.einsum('bqhd,bkd->bhqk', qp, kpe)).astype(jnp.float32) * MLA_SCALE
        s = jnp.where(kidx[None, :] <= qidx[:, None], s, -jnp.inf)
        if ckv_past is None:
            p = jax.nn.softmax(s, axis=-1).astype(ckv.dtype)
            return jnp.einsum('bhqk,bkr->bqhr', p, ckv)
        sp = (jnp.einsum('bqhr,bkr->bhqk', ql, ckv_past)
              + jnp.einsum('bqhd,bkd->bhqk', qp, kpe_past)).astype(jnp.float32) * MLA_SCALE
        p = jax.nn.softmax(jnp.concatenate([sp, s], axis=-1), axis=-1).astype(ckv.dtype)
        n_past = ckv_past.shape[1]
        return (jnp.einsum('bhqk,bkr->bqhr', p[..., :n_past], ckv_past)
                + jnp.einsum('bhqk,bkr->bqhr', p[..., n_past:], ckv))

    o = lax.map(block, (blocks(q_lat), blocks(q_pe), starts))
    return jnp.moveaxis(o, 0, 1).reshape(B, nb * qb, H, R)[:, :T]

def odd_layer(x, pos, ckv_past, kpe_past, norm_g, w_in, q_norm_g, kv_norm_g,
              w_q_b, w_uk, w_uv, w_out):
    B, T, _ = x.shape
    z = rms_norm(x, norm_g) @ w_in
    c_q, c_kv, k_pe = jnp.split(z, [R_Q, R_Q + R_KV], axis=-1)
    q = (rms_norm(c_q, q_norm_g) @ w_q_b).reshape(B, T, H_C, D_NOPE + D_ROPE)
    q_nope = q[..., :D_NOPE]
    q_pe = rope(q[..., D_NOPE:], pos)
    ckv = rms_norm(c_kv, kv_norm_g)
    kpe = rope(k_pe, pos)
    q_lat = jnp.einsum('bthn,rhn->bthr', q_nope, w_uk)
    o_lat = mla_attend(q_lat, q_pe, ckv, kpe, ckv_past, kpe_past)
    o = jnp.einsum('bthr,rhv->bthv', o_lat, w_uv).reshape(B, T, H_C * D_V)
    return x + o @ w_out, ckv, kpe

def peer(h, w_q, sub_keys, u_tab, v_tab):
    lead = h.shape[:-1]
    xf = h.reshape(-1, D_MODEL)
    n = xf.shape[0]
    q = (xf @ w_q).reshape(n, H_P, 2, D_HALF)
    s = jnp.einsum('nhcd,hckd->nhck', q, sub_keys).astype(jnp.float32)
    s_top, i_top = lax.top_k(s, TOPK)
    cand = (s_top[:, :, 0, :, None] + s_top[:, :, 1, None, :]).reshape(n, H_P, TOPK * TOPK)
    c_top, c_idx = lax.top_k(cand, TOPK)
    i1 = jnp.take_along_axis(i_top[:, :, 0], c_idx // TOPK, axis=-1)
    i2 = jnp.take_along_axis(i_top[:, :, 1], c_idx % TOPK, axis=-1)
    ids = i1 * N_KEYS + i2
    gates = jax.nn.softmax(c_top, axis=-1).astype(h.dtype)
    blk = min(PEER_BLOCK, n)
    nb = -(-n // blk)
    pad = nb * blk - n

    def blocks(a):
        a = jnp.pad(a, ((0, pad),) + ((0, 0),) * (a.ndim - 1))
        return a.reshape((nb, blk) + a.shape[1:])

    def block(args):
        xb, ib, gb = args
        act = jax.nn.gelu(jnp.einsum('td,thkd->thk', xb, u_tab[ib]), approximate=False) * gb
        return jnp.einsum('thk,thkd->td', act, v_tab[ib])

    out = lax.map(block, (blocks(xf), blocks(ids), blocks(gates)))
    return out.reshape(nb * blk, D_MODEL)[:n].reshape(lead + (D_MODEL,))

def setup_inputs(seed: int = 0) -> dict:
    key = jax.random.key(seed)
    keys = list(jax.random.split(key, 48))

    def nrm(shape, scale):
        return jax.random.normal(keys.pop(), shape, jnp.float32) * scale

    def gain(shape):
        return 1.0 + nrm(shape, 0.02)

    n_pages = PAST_LEN // PAGE_SIZE
    n_used = DEC_BATCH * n_pages
    n_pool = n_used + max(1, n_used // 4)
    page_table = jax.random.permutation(keys.pop(), n_pool)[:n_used].reshape(
        DEC_BATCH, n_pages).astype(jnp.int32)
    return {
        'x_prompt': nrm((BATCH, SEQ, D_MODEL), 1.0),
        'x_sample': nrm((DEC_BATCH, DEC_SEQ, D_MODEL), 1.0),
        'cache_ckv': nrm((N_C, n_pool, PAGE_SIZE, R_KV), 1.0),
        'cache_kpe': nrm((N_C, n_pool, PAGE_SIZE, D_ROPE), 1.0),
        'state_conv': nrm((N_AB, DEC_BATCH, CONV_W - 1, D_A), 0.5),
        'state_gla': nrm((N_AB, DEC_BATCH, H_B, DK_B, DV_B), 0.5),
        'page_table': page_table,
        'ab_norm': gain((N_AB, D_MODEL)),
        'ab_w_in': nrm((N_AB, D_MODEL, D_IN_AB), D_MODEL ** -0.5),
        'conv_w': nrm((N_AB, CONV_W, D_A), CONV_W ** -0.5),
        'conv_b': nrm((N_AB, D_A), 0.02),
        'conv_ln_g': gain((N_AB, D_A)),
        'conv_ln_b': nrm((N_AB, D_A), 0.02),
        'gla_w_gate': nrm((N_AB, GATE_RANK, D_BK), GATE_RANK ** -0.5),
        'gla_b_gate': nrm((N_AB, D_BK), 0.1),
        'gla_head_g': gain((N_AB, DV_B)),
        'ab_w_out': nrm((N_AB, D_A + D_BV, D_MODEL), (D_A + D_BV) ** -0.5),
        'c_norm': gain((N_C, D_MODEL)),
        'c_w_in': nrm((N_C, D_MODEL, D_IN_C), D_MODEL ** -0.5),
        'c_q_norm': gain((N_C, R_Q)),
        'c_kv_norm': gain((N_C, R_KV)),
        'c_w_q_b': nrm((N_C, R_Q, H_C * (D_NOPE + D_ROPE)), R_Q ** -0.5),
        'c_w_uk': nrm((N_C, R_KV, H_C, D_NOPE), R_KV ** -0.5),
        'c_w_uv': nrm((N_C, R_KV, H_C, D_V), R_KV ** -0.5),
        'c_w_out': nrm((N_C, H_C * D_V, D_MODEL), (H_C * D_V) ** -0.5),
        'ffn_norm': gain((DEPTH, D_MODEL)),
        'peer_w_q': nrm((DEPTH, D_MODEL, H_P * D_KEY), D_MODEL ** -0.5),
        'peer_keys': nrm((DEPTH, H_P, 2, N_KEYS, D_HALF), D_HALF ** -0.5),
        'peer_u': nrm((DEPTH, N_EXPERTS, D_MODEL), D_MODEL ** -0.5),
        'peer_v': nrm((DEPTH, N_EXPERTS, D_MODEL), (H_P * TOPK) ** -0.5),
        'final_norm': gain((D_MODEL,)),
    }

def reference(x_prompt, x_sample, cache_ckv, cache_kpe, state_conv, state_gla, page_table,
              ab_norm, ab_w_in, conv_w, conv_b, conv_ln_g, conv_ln_b, gla_w_gate, gla_b_gate,
              gla_head_g, ab_w_out, c_norm, c_w_in, c_q_norm, c_kv_norm, c_w_q_b, c_w_uk,
              c_w_uv, c_w_out, ffn_norm, peer_w_q, peer_keys, peer_u, peer_v, final_norm):
    xp, xs = x_prompt, x_sample
    bp, tp = xp.shape[0], xp.shape[1]
    bs, ts = xs.shape[0], xs.shape[1]
    pos_p = jnp.arange(tp, dtype=jnp.int32)
    pos_s = PAST_LEN + jnp.arange(ts, dtype=jnp.int32)
    ckv_p, kpe_p, ckv_s, kpe_s = [], [], [], []
    conv_p, conv_s, gla_p, gla_s = [], [], [], []
    for l in range(DEPTH):
        j = l // 2
        if l % 2 == 0:
            prm = (ab_norm[j], ab_w_in[j], conv_w[j], conv_b[j], conv_ln_g[j], conv_ln_b[j],
                   gla_w_gate[j], gla_b_gate[j], gla_head_g[j], ab_w_out[j])
            zero_buf = jnp.zeros((bp, CONV_W - 1, D_A), xp.dtype)
            zero_s = jnp.zeros((bp, H_B, DK_B, DV_B), xp.dtype)
            xp, cb, sb = even_layer(xp, zero_buf, zero_s, *prm)
            conv_p.append(cb)
            gla_p.append(sb)
            xs, cb, sb = even_layer(xs, state_conv[j], state_gla[j], *prm)
            conv_s.append(cb)
            gla_s.append(sb)
        else:
            prm = (c_norm[j], c_w_in[j], c_q_norm[j], c_kv_norm[j], c_w_q_b[j],
                   c_w_uk[j], c_w_uv[j], c_w_out[j])
            xp, ck, kp = odd_layer(xp, pos_p, None, None, *prm)
            ckv_p.append(ck)
            kpe_p.append(kp)
            ckv_past = cache_ckv[j][page_table].reshape(bs, -1, R_KV)
            kpe_past = cache_kpe[j][page_table].reshape(bs, -1, D_ROPE)
            xs, ck, kp = odd_layer(xs, pos_s, ckv_past, kpe_past, *prm)
            ckv_s.append(ck)
            kpe_s.append(kp)
        xp = xp + peer(rms_norm(xp, ffn_norm[l]), peer_w_q[l], peer_keys[l], peer_u[l], peer_v[l])
        xs = xs + peer(rms_norm(xs, ffn_norm[l]), peer_w_q[l], peer_keys[l], peer_u[l], peer_v[l])
    y_prompt = rms_norm(xp, final_norm)
    y_sample = rms_norm(xs, final_norm)
    return (y_prompt, y_sample,
            jnp.stack(ckv_p), jnp.stack(kpe_p), jnp.stack(ckv_s), jnp.stack(kpe_s),
            jnp.stack(conv_p), jnp.stack(conv_s), jnp.stack(gla_p), jnp.stack(gla_s))


_drawn_inputs = setup_inputs


def setup_inputs(seed=0):
    import zlib

    import numpy as np

    out = dict(_drawn_inputs(seed))
    spreads = {}
    factors = {'cache_kpe': 4.465,
     'conv_ln_g': 5.049,
     'conv_ln_b': 5.49,
     'gla_head_g': 6.041,
     'c_q_norm': 8.0,
     'c_kv_norm': 2.782,
     'ffn_norm': 6.445,
     'final_norm': 2.873}
    for name, (base, spread) in spreads.items():
        noise = np.random.default_rng([zlib.crc32(name.encode()), seed]).standard_normal(out[name].shape)
        drawn = base * np.exp(spread * noise) if base else spread * noise
        out[name] = __import__('jax').numpy.asarray(drawn.astype(out[name].dtype))
    for name, factor in factors.items():
        out[name] = (out[name] * factor).astype(out[name].dtype)
    return out
```

```python
from contextlib import ExitStack

import numpy as np

import concourse.bass as bass
from concourse import mybir

F32 = mybir.dt.float32
I32 = mybir.dt.int32
U32 = mybir.dt.uint32
ALU = mybir.AluOpType
ACT = mybir.ActivationFunctionType
AX = mybir.AxisListType

D_MODEL, SEQ, DEC_BATCH, PAST_LEN, PAGE = 1024, 512, 8, 4096, 128
EPS = 1e-6
D_A, CONV_W, H_B, D_BV, D_BK, DK_B, DV_B, GATE_RANK = 512, 31, 4, 512, 256, 64, 128, 16
GATE_TAU = 16.0
D_IN_AB = 2 * D_A + 2 * D_BK + 2 * D_BV + GATE_RANK
H_C, D_NOPE, D_ROPE, D_V, R_Q, R_KV = 16, 64, 32, 64, 384, 256
D_IN_C = R_Q + R_KV + D_ROPE
ROPE_BASE = 10000.0
MLA_SCALE = (D_NOPE + D_ROPE) ** -0.5
H_P, N_KEYS, D_KEY, D_HALF, TOPK = 8, 128, 256, 128, 16
N_EXPERTS = N_KEYS * N_KEYS

KC = D_MODEL // 128
TOK = SEQ + DEC_BATCH
NT = SEQ // 128
PAD = CONV_W - 1
NEG_MASK = -1.0e30
LEVELS = 7
NP = PAST_LEN // PAGE


def rows_of(t):
    return 128 if t < NT else DEC_BATCH


def cols_of(t):
    return slice(128 * t, 128 * t + rows_of(t))


def bc(ap, shape):
    return ap.to_broadcast(shape)


def signals(nc, ctx, prefix):
    made = []

    def done():
        nc.clear_and_free_semaphores(made)
        nc.all_engine_barrier()

    def sem(name):
        made.append(nc.alloc_semaphore(prefix + name))
        return made[-1]

    ctx.callback(done)
    return sem


GLOW, K0, K1, Q0, Q1, L0, L1 = range(7)
JOB_COLS = {GLOW: 2 * D_A + 2 * D_BK + 2 * D_BV, K0: 2 * D_A + D_BK, K1: 2 * D_A + D_BK + 128,
            Q0: 2 * D_A, Q1: 2 * D_A + 128}
for _c in range(4):
    JOB_COLS[7 + 2 * _c] = D_A + 128 * _c
    JOB_COLS[8 + 2 * _c] = 128 * _c
N_JOBS = 15
ON_DVE = [j in (L0, L1) or (j >= 8 and j % 2 == 0) for j in range(N_JOBS)]


def evacuated(j):
    return ON_DVE[j], sum(1 for i in range(j + 1) if ON_DVE[i] == ON_DVE[j])


def even_layer(nc, w, out, ident, x_sb):
    with ExitStack() as ctx:
        def sb(name, shape, dt=F32):
            return ctx.enter_context(nc.sbuf_tensor("a_" + name, shape, dt))

        sem = signals(nc, ctx, "a_")

        arena = sb("arena", [128, KC * D_IN_AB])
        w_in = arena[:, :].rearrange("p (k n) -> p k n", k=KC)
        w_out = arena[:, 0:KC * D_MODEL].rearrange("p (k n) -> p k n", k=KC)
        cursor = [KC * D_MODEL]

        def carve(*dims):
            n = int(np.prod(dims))
            ap = arena[:, cursor[0]:cursor[0] + n]
            cursor[0] += n
            names = "abcd"[:len(dims)]
            return ap.rearrange(f"p ({' '.join(names)}) -> p {' '.join(names)}", **dict(zip(names, dims))) if len(dims) > 1 else ap

        qE = carve(2, 2, SEQ)
        kE = carve(2, 2, SEQ)
        attn = carve(2, 2, 2, 2 * 128)
        qB = carve(2, SEQ)
        kD = carve(2, SEQ)
        kDT = carve(NT, 2, 128)
        state = carve(NT + 1, 2, DV_B)
        assert cursor[0] <= KC * D_IN_AB

        norm_col = sb("norm_col", [128, KC])
        conv_wc = sb("conv_wc", [128, 4, CONV_W])
        chan = sb("chan", [128, 3, 4])
        w_gate = sb("w_gate", [GATE_RANK, D_BK])
        gate_b = sb("gate_b", [128, 2])
        head_gain = sb("head_gain", [128, DV_B])
        mean_w = sb("mean_w", [128, 128])
        ones = sb("ones", [128, 128])
        eps = sb("eps", [128, 1])
        masks = sb("masks", [128, LEVELS + 1, 128], I32)
        own_seq = sb("own_seq", [DEC_BATCH, DEC_BATCH])
        ms = sb("ms", [128, NT + 1])
        rstd = sb("rstd", [128, NT + 1])
        scratch = sb("scratch", [128, 4 * TOK])
        xs = scratch[:, 0:2 * D_MODEL].rearrange("p (b n) -> p b n", b=2)
        sig = scratch[:, 0:2 * TOK].rearrange("p (b n) -> p b n", b=2)
        absl = scratch[:, 2 * TOK:4 * TOK].rearrange("p (b n) -> p b n", b=2)
        dec = xs
        xT = sb("xT", [128, KC, TOK])
        u = sb("u", [128, 4, PAD + TOK])
        conv = sb("conv", [128, 4, TOK])
        qT = sb("qT", [128, 2, TOK])
        kT = sb("kT", [128, 2, TOK])
        glow = sb("glow", [GATE_RANK, TOK])
        la = sb("la", [128, 2, TOK])
        cum = sb("cum", [128, 2, SEQ])
        bend = sb("bend", [128, 2, NT])
        v = sb("v", [128, NT + 1, D_BV])
        r = sb("r", [128, NT + 1, D_BV])
        st_conv = sb("st_conv", [128, 4, DEC_BATCH, PAD])
        ubuf = sb("ubuf", [128, 4, DEC_BATCH, CONV_W])
        u_rows = sb("u_rows", [PAD, D_A])
        us_rows = sb("us_rows", [DEC_BATCH, D_A])
        hms = sb("hms", [128, NT + 1, H_B])
        hrs = sb("hrs", [128, NT + 1, H_B])
        k_rows = sb("k_rows", [DEC_BATCH, D_BK])
        s_smp = conv[:, :, :].rearrange("p a b -> p (a b)")[:, 0:2 * DEC_BATCH * DV_B].rearrange(
            "p (g b v) -> p g b v", g=2, b=DEC_BATCH)
        vblk = u[:, :, :].rearrange("p a b -> p (a b)")[0:DEC_BATCH, 0:2 * DEC_BATCH * DV_B].rearrange(
            "p (i b v) -> p i b v", i=2, b=DEC_BATCH)
        o_smp = sb("o_smp", [DEC_BATCH, H_B, DV_B])
        b_rows = sb("b_rows", [128, 2, D_BV])

        ps = [ctx.enter_context(nc.psum_tensor(f"a_ps{i}", [128, 1024], F32)) for i in range(4)]
        half = TOK // 2

        def pair(t, rows=128):
            return t[0:rows, :].rearrange("p (b n) -> p b n", b=2)[:, :, 0:half]

        def halves(ap):
            return ap.rearrange("p (b n) -> p b n", b=2)

        def by_head(t, c, h):
            at = 512 * (h % 2) + 256 * (c % 2) + 128 * (h // 2)
            return ps[t][:, at:at + 128]

        def o_heads(t, n=128):
            return ps[1 + 2 * (t % 2)][0:n, :].rearrange("p (b c a v) -> p c a b v", b=2, c=2, a=2)[:, 0]

        def kv_bank(c):
            return (ps[3] if c < 2 else ps[0])[:, 512 * (c % 2):512 * (c % 2) + 512]

        w_in_in, w_out_in, small_in = sem("w_in_in"), sem("w_out_in"), sem("small_in")
        masks_in, state_in, stores = sem("masks_in"), sem("state_in"), sem("stores")
        consts, pool_step, r_gained = sem("consts"), sem("pool_step"), sem("r_gained")
        ms_ready, root_ready, xs_ready = sem("ms_ready"), sem("root_ready"), sem("xs_ready")
        xT_ps, xT_ready = sem("xT_ps"), sem("xT_ready")
        job_ps, job_act, job_dve = sem("job_ps"), sem("job_act"), sem("job_dve")
        row_ps, row_act = sem("row_ps"), sem("row_act")
        act_step, dve_step = sem("act_step"), sem("dve_step")
        log_ready, la_ready = sem("log_ready"), sem("la_ready")
        ubuf_ready, conv_ready = sem("ubuf_ready"), sem("conv_ready")
        mean_ps, xc_ready, sq_ready, var_ps = sem("mean_ps"), sem("xc_ready"), sem("sq_ready"), sem("var_ps")
        lnroot_ready, ln_ready, conv_out = sem("lnroot_ready"), sem("ln_ready"), sem("conv_out")
        tail_ps, tail_ready = sem("tail_ps"), sem("tail_ready")
        dec_ready, exp_ready, lev_ready, lev_ps, lev_used = (sem("dec_ready"), sem("exp_ready"), sem("lev_ready"),
                                                             sem("lev_ps"), sem("lev_used"))
        kdt_ps, kdt_ready, kv_ps, st_ready = sem("kdt_ps"), sem("kdt_ready"), sem("kv_ps"), sem("st_ready")
        o_ps, osq_ready, hms_ready, hroot_ready, b_ready, bT_ps, bT_ready = (
            sem("o_ps"), sem("osq_ready"), sem("hms_ready"), sem("hroot_ready"), sem("b_ready"), sem("bT_ps"), sem("bT_ready"))
        krow_ps, krow_ready, vblk_ready, skv_ps, skv_used, s_decayed, so_ps, so_used = (
            sem("krow_ps"), sem("krow_ready"), sem("vblk_ready"), sem("skv_ps"), sem("skv_used"), sem("s_decayed"),
            sem("so_ps"), sem("so_used"))
        y_ps, y_used, dve_lev, qk_dec = sem("y_ps"), sem("y_used"), sem("dve_lev"), sem("qk_dec")
        N_SMALL = 7

        block = ctx.enter_context(nc.Block())

        @block.sync
        def _(sp):
            for k in range(KC):
                sp.dma_start(w_in[:, k, :], w["ab_w_in"][0, 128 * k:128 * k + 128, :]).then_inc(w_in_in, 16)
            sp.dma_start(masks[:], w["level_masks"]).then_inc(masks_in, 16)
            sp.wait_ge(row_ps, NT + 1)
            sp.dma_start(w_out, w["ab_w_out"][0].rearrange("(k p) n -> p k n", p=128)).then_inc(w_out_in, 16)
            sp.wait_ge(tail_ready, 2)
            sp.dma_start(out["new_conv_prompt"][0, 0], u_rows[:]).then_inc(stores, 16)
            sp.dma_start(out["new_conv_sample"][0, :, PAD - 1, :], us_rows[:]).then_inc(stores, 16)
            sp.dma_start(out["new_conv_sample"][0, :, 0:PAD - 1, :], w["state_conv"][0, :, 1:PAD, :]).then_inc(stores, 16)
            sp.wait_ge(st_ready, NT)
            for g in range(2):
                sp.dma_start(out["new_gla_prompt"][0, 0, 2 * g:2 * g + 2].rearrange("h k v -> (h k) v"),
                             state[:, NT, g, :]).then_inc(stores, 16)
            sp.wait_ge(skv_used, H_B)
            for g in range(2):
                sp.dma_start(out["new_gla_sample"][0, :, 2 * g:2 * g + 2].rearrange("b h k v -> (h k) b v"),
                             s_smp[:, g]).then_inc(stores, 16)
            sp.wait_ge(stores, 16 * 7)

        @block.gpsimd
        def _(pool):
            nc.gpsimd.memset(mean_w[:], 1.0 / D_A).then_inc(consts, 1)
            nc.gpsimd.memset(ones[:], 1.0).then_inc(consts, 1)
            nc.gpsimd.memset(eps[:], EPS).then_inc(consts, 1)
            nc.gpsimd.memset(u[:, :, 0:PAD], 0.0).then_inc(consts, 1)
            nc.gpsimd.memset(ms[:], 1.0).then_inc(consts, 1)
            pool.wait_ge(state_in, 16)
            nc.gpsimd.tensor_copy(ubuf[:, :, :, 0:PAD].rearrange("p c b t -> p (c b) t"), st_conv[:].rearrange("p c b t -> p (c b) t")).then_inc(ubuf_ready, 1)
            pool.wait_ge(row_ps, NT + 1)
            nc.gpsimd.memset(attn[:], 0.0).then_inc(consts, 1)
            pool.wait_ge(small_in, 16 * N_SMALL)
            for t in range(NT + 1):
                pool.wait_ge(row_act, 2 * (t + 1))
                n = rows_of(t)
                nc.gpsimd.tensor_tensor(r[0:n, t, :].rearrange("p (h v) -> p h v", h=H_B),
                                        r[0:n, t, :].rearrange("p (h v) -> p h v", h=H_B),
                                        bc(head_gain[0:n, :].unsqueeze(1), [n, H_B, DV_B]), ALU.mult).then_inc(r_gained, 1)

        @block.scalar
        def _(act):
            act.dma_start(norm_col[:], w["ab_norm_cols"]).then_inc(small_in, 16)
            act.dma_start(conv_wc[:], w["conv_w_cols"]).then_inc(small_in, 16)
            act.dma_start(chan[:], w["chan_cols"]).then_inc(small_in, 16)
            act.dma_start(w_gate[:], w["gla_w_gate"][0]).then_inc(small_in, 16)
            act.dma_start(gate_b[:], w["gate_b_cols"]).then_inc(small_in, 16)
            act.dma_start(head_gain[:], w["gla_head_g"].to_broadcast([128, DV_B])).then_inc(small_in, 16)
            act.dma_start(own_seq[:], w["own_seq"]).then_inc(small_in, 16)
            act.dma_start(st_conv[:], w["state_conv_cols"]).then_inc(state_in, 16)
            act.wait_ge(consts, 3)
            act.wait_ge(ms_ready, NT + 1)
            nc.scalar.activation(rstd[:], ms[:], ACT.Sqrt, bias=eps[:]).then_inc(root_ready, 1)
            for j in range(N_JOBS):
                if ON_DVE[j]:
                    continue
                src = ps[j % 2]
                act.wait_ge(job_ps, j + 1)
                if j == GLOW:
                    ins = nc.scalar.copy(halves(glow[:]), pair(src, GATE_RANK))
                elif j in (K0, K1):
                    ins = nc.scalar.copy(halves(kT[:, j - K0, :]), pair(src))
                elif j in (Q0, Q1):
                    ins = nc.scalar.mul(halves(qT[:, j - Q0, :]), pair(src), DK_B ** -0.5)
                else:
                    c = (j - 7) // 2
                    if c == 0:
                        act.wait_ge(job_dve, 2)
                        nc.scalar.activation(absl, la[:], ACT.Abs).then_inc(act_step, 1)
                        act.wait_ge(act_step, 1)
                        nc.scalar.activation(absl, absl, ACT.Exp, scale=-1.0).then_inc(act_step, 1)
                        act.wait_ge(act_step, 2)
                        nc.scalar.activation(absl, absl, ACT.Ln, bias=1.0).then_inc(log_ready, 1)
                    if c >= 2:
                        act.wait_ge(job_dve, 2 + c - 1)
                    ins = nc.scalar.activation(halves(sig[:, c % 2, :]), pair(src), ACT.Sigmoid)
                ins.then_inc(job_act, 1)
            for t in range(NT + 1):
                n = rows_of(t)
                act.wait_ge(row_ps, t + 1)
                nc.scalar.copy(v[0:n, t, :], ps[2 + t % 2][0:n, 0:512]).then_inc(row_act, 1)
                nc.scalar.activation(r[0:n, t, :], ps[2 + t % 2][0:n, 512:1024], ACT.Silu).then_inc(row_act, 1)
            act.wait_ge(xc_ready, 1)
            nc.scalar.activation(xT[:, 0:4, :], conv[:], ACT.Square).then_inc(sq_ready, 1)
            act.wait_ge(var_ps, 1)
            nc.scalar.activation(halves(sig[:, 0, :]), pair(ps[0]), ACT.Sqrt, bias=eps[:]).then_inc(lnroot_ready, 1)
            act.wait_ge(ln_ready, 1)
            for c in range(4):
                nc.scalar.activation(xT[:, c, :], conv[:, c, :], ACT.Silu, scale=chan[:, 1, c:c + 1],
                                     bias=chan[:, 2, c:c + 1]).then_inc(conv_out, 1)
            act.wait_ge(conv_out, 4)
            for g in range(2):
                act.dma_start(s_smp[:, g], w["state_gla"][0, :, 2 * g:2 * g + 2].rearrange("b h k v -> (h k) b v")).then_inc(state_in, 16)
            act.wait_ge(tail_ps, 1)
            nc.scalar.copy(u_rows[:], ps[0][0:PAD, 0:512]).then_inc(tail_ready, 1)
            nc.scalar.copy(us_rows[:], ps[0][0:DEC_BATCH, 512:1024]).then_inc(tail_ready, 1)
            for l in range(LEVELS):
                act.wait_ge(dec_ready, 2 * (l + 1))
                nc.scalar.activation(dec[:, l % 2, :], dec[:, l % 2, :], ACT.Exp).then_inc(exp_ready, 1)
            act.wait_ge(lev_ready, LEVELS)
            nc.scalar.activation(dec[:, 0, :], cum[:].rearrange("p g t -> p (g t)"), ACT.Exp).then_inc(exp_ready, 1)
            act.wait_ge(dec_ready, 2 * LEVELS + 1)
            nc.scalar.activation(dec[:, 1, :], dec[:, 1, :], ACT.Exp).then_inc(exp_ready, 1)
            nc.scalar.activation(bend[:], cum[:].rearrange("p g (c t) -> p g c t", c=NT)[:, :, :, 127], ACT.Exp).then_inc(exp_ready, 1)
            nc.scalar.activation(la[:, :, SEQ:TOK], la[:, :, SEQ:TOK], ACT.Exp).then_inc(exp_ready, 1)
            act.wait_ge(kdt_ps, 1)
            nc.scalar.copy(kDT[:].rearrange("p c g i -> p (c g i)"), ps[2][:, :]).then_inc(kdt_ready, 1)
            act.wait_ge(krow_ps, 1)
            nc.scalar.copy(k_rows[:], ps[2][0:DEC_BATCH, 0:D_BK]).then_inc(krow_ready, 1)
            for t in range(NT + 1):
                n = rows_of(t)
                if t < NT:
                    act.wait_ge(o_ps, t + 1)
                    src = o_heads(t)
                else:
                    act.wait_ge(so_used, H_B)
                    src = o_smp[:].rearrange("p (a b) v -> p a b v", b=2)
                if t >= 1:
                    act.wait_ge(hms_ready, t)
                nc.scalar.activation(dec[0:n, 0, 0:512].rearrange("p (a b v) -> p a b v", a=2, b=2), src, ACT.Square, scale=DV_B ** -0.5).then_inc(osq_ready, 1)
                act.wait_ge(hms_ready, t + 1)
                nc.scalar.activation(hrs[0:n, t, :], hms[0:n, t, :], ACT.Sqrt, bias=eps[0:n, :]).then_inc(hroot_ready, 1)
                act.wait_ge(bT_ps, t + 1)
                nc.scalar.copy(xT[:, 4:8, cols_of(t)], ps[2][:, 0:4 * n].rearrange("p (c n) -> p c n", c=4)).then_inc(bT_ready, 1)

        @block.vector
        def _(dve):
            steps = [0]

            def step(ins):
                steps[0] += 1
                ins.then_inc(dve_step, 1)
                dve.wait_ge(dve_step, steps[0])

            dve.wait_ge(consts, 5)
            for t in range(NT + 1):
                n = rows_of(t)
                nc.vector.tensor_tensor_reduce(u[0:n, 2 * (t % 2):2 * (t % 2) + 2, PAD:PAD + 512], x_sb[0:n, t, :].rearrange("p (a b) -> p a b", a=2),
                                               x_sb[0:n, t, :].rearrange("p (a b) -> p a b", a=2), 1.0 / D_MODEL, 0.0,
                                               ALU.mult, ALU.add, ms[0:n, t:t + 1]).then_inc(ms_ready, 1)
                dve.wait_ge(ms_ready, t + 1)
            dve.wait_ge(root_ready, 1)
            step(nc.vector.reciprocal(rstd[:], rstd[:]))
            dve.wait_ge(small_in, 16 * N_SMALL)

            def xT_out(t):
                n = rows_of(t)
                dve.wait_ge(xT_ps, t + 1)
                nc.vector.tensor_tensor(xT[:, :, cols_of(t)], ps[2 + t % 2][:, :].rearrange("p (k n) -> p k n", k=KC)[:, :, 0:n],
                                        bc(norm_col[:].unsqueeze(2), [128, KC, n]), ALU.mult).then_inc(xT_ready, 1)

            for t in range(NT + 1):
                n = rows_of(t)
                if t >= 2:
                    dve.wait_ge(xT_ps, t - 1)
                nc.vector.tensor_scalar(xs[0:n, t % 2, :], x_sb[0:n, t, :], rstd[0:n, t:t + 1], None, ALU.mult).then_inc(xs_ready, 1)
                if t:
                    xT_out(t - 1)
            xT_out(NT)
            for g in range(2):
                dve.wait_ge(job_ps, L0 + g + 1)
                nc.vector.tensor_scalar(halves(la[:, g, :]), pair(ps[(L0 + g) % 2]), gate_b[:, g:g + 1], None, ALU.add).then_inc(job_dve, 1)
            dve.wait_ge(log_ready, 1)
            step(nc.vector.scalar_tensor_tensor(out=la[:], in0=la[:], scalar=0.0, in1=absl, op0=ALU.min, op1=ALU.subtract))
            step(nc.vector.tensor_scalar(la[:], la[:], 1.0 / GATE_TAU, None, ALU.mult))
            for g in range(2):
                for c in range(NT):
                    last = nc.vector.tensor_tensor_scan(cum[:, g, 128 * c:128 * c + 128], ones[:], la[:, g, 128 * c:128 * c + 128],
                                                        0.0, ALU.mult, ALU.add)
                last.then_inc(la_ready, 1)
            for c0 in (0, 2):
                for c in (c0, c0 + 1):
                    dve.wait_ge(job_act, evacuated(7 + 2 * c)[1])
                    dve.wait_ge(job_ps, 8 + 2 * c + 1)
                    nc.vector.tensor_tensor(halves(u[:, c, PAD:PAD + TOK]), pair(ps[(8 + 2 * c) % 2]), halves(sig[:, c % 2, :]), ALU.mult).then_inc(job_dve, 1)
                dve.wait_ge(job_dve, 2 + c0 + 2)
                for tap in range(CONV_W):
                    for c in (c0, c0 + 1):
                        if tap == 0:
                            ins = nc.vector.tensor_scalar(conv[:, c, 0:SEQ], u[:, c, 0:SEQ], conv_wc[:, c, 0:1], chan[:, 0, c:c + 1], ALU.mult, ALU.add)
                        else:
                            dve.wait_ge(conv_ready, c0 * CONV_W + 2 * (tap - 1) + (c - c0) + 1)
                            ins = nc.vector.scalar_tensor_tensor(out=conv[:, c, 0:SEQ], in0=u[:, c, tap:tap + SEQ], scalar=conv_wc[:, c, tap:tap + 1],
                                                                 in1=conv[:, c, 0:SEQ], op0=ALU.mult, op1=ALU.add)
                        ins.then_inc(conv_ready, 1)
            dve.wait_ge(ubuf_ready, 1)
            step(nc.vector.tensor_copy(ubuf[:, :, :, PAD], u[:, :, PAD + SEQ:PAD + TOK]))
            for c in range(4):
                last = nc.vector.tensor_tensor(ubuf[:, c], ubuf[:, c], bc(conv_wc[:, c, :].unsqueeze(1), [128, DEC_BATCH, CONV_W]), ALU.mult)
            step(last)
            step(nc.vector.tensor_reduce(conv[:, :, SEQ:TOK], ubuf[:], AX.X, ALU.add))
            nc.vector.tensor_tensor(conv[:, :, SEQ:TOK], conv[:, :, SEQ:TOK], bc(chan[:, 0, :].unsqueeze(2), [128, 4, DEC_BATCH]), ALU.add).then_inc(conv_ready, 1)
            dve.wait_ge(conv_ready, 4 * CONV_W + 1)
            dve.wait_ge(mean_ps, 1)
            for c in range(4):
                last = nc.vector.tensor_tensor(halves(conv[:, c, :]), halves(conv[:, c, :]), pair(ps[1]), ALU.subtract)
            last.then_inc(xc_ready, 1)
            dve.wait_ge(lnroot_ready, 1)
            step(nc.vector.reciprocal(sig[:, 0, :], sig[:, 0, :]))
            last = nc.vector.tensor_tensor(conv[:], conv[:], bc(sig[:, 0:1, :], [128, 4, TOK]), ALU.mult)
            last.then_inc(ln_ready, 1)
            dve.wait_ge(masks_in, 16)
            dve.wait_ge(consts, 6)
            qk = (qT[:, :, 0:SEQ], kT[:, :, 0:SEQ])
            dve.wait_ge(job_act, evacuated(Q1)[1])

            def level_decay(l):
                hf = 64 >> l
                b4 = cum[:].rearrange("p g (n s) -> p (g n) s", s=2 * hf)
                d4 = dec[:, l % 2, :].rearrange("p (n s) -> p n s", s=2 * hf)
                edge = bc(b4[:, :, hf - 1:hf], [128, SEQ // hf, hf])
                if l >= 2:
                    dve.wait_ge(lev_ready, l - 1)
                nc.vector.tensor_tensor(d4[:, :, hf:], b4[:, :, hf:], edge, ALU.subtract).then_inc(dec_ready, 1)
                nc.vector.tensor_tensor(d4[:, :, 0:hf], edge, b4[:, :, 0:hf], ALU.subtract).then_inc(dec_ready, 1)

            def level_scale(l):
                dve.wait_ge(exp_ready, l + 1)
                if l >= 2:
                    dve.wait_ge(lev_ps, 2 * (l - 1))
                d3 = dec[:, l % 2, :].rearrange("p (g t) -> p g t", g=2)
                nc.vector.tensor_tensor(qE[:, l % 2], qk[0], d3, ALU.mult).then_inc(dve_lev, 1)
                nc.vector.tensor_tensor(kE[:, l % 2], qk[1], d3, ALU.mult).then_inc(lev_ready, 1)

            def level_keep(l):
                for cp in range(2):
                    i = 2 * l + cp
                    dve.wait_ge(lev_ps, i + 1)
                    if l:
                        dve.wait_ge(lev_used, i - 1)
                    nc.vector.copy_predicated(attn[:, cp].rearrange("p b c n -> p (b c n)").rearrange("p (n i) -> p n i", i=128),
                                              bc(masks[:, l, :].unsqueeze(1), [128, 8, 128]),
                                              ps[i % 2][:, :].rearrange("p (n i) -> p n i", i=128)).then_inc(lev_used, 1)

            dve.wait_ge(la_ready, 2)
            dve.wait_ge(ln_ready, 1)
            level_decay(0)
            for l in range(LEVELS):
                if l + 1 < LEVELS:
                    level_decay(l + 1)
                level_scale(l)
                if l:
                    level_keep(l - 1)
            level_keep(LEVELS - 1)
            level_keep(LEVELS)
            c4 = cum[:].rearrange("p g (c t) -> p (g c) t", c=NT)
            nc.vector.tensor_tensor(dec[:, 1, :].rearrange("p (n t) -> p n t", t=128), bc(c4[:, :, 127:128], [128, 2 * NT, 128]), c4, ALU.subtract).then_inc(dec_ready, 1)
            dve.wait_ge(exp_ready, LEVELS + 4)
            nc.vector.tensor_tensor(qB, qk[0], dec[:, 0, :].rearrange("p (g t) -> p g t", g=2), ALU.mult).then_inc(qk_dec, 1)
            nc.vector.tensor_tensor(kD, qk[1], dec[:, 1, :].rearrange("p (g t) -> p g t", g=2), ALU.mult).then_inc(qk_dec, 1)
            for c in range(NT):
                dve.wait_ge(kv_ps, c + 1)
                if c:
                    dve.wait_ge(st_ready, c)
                for g in range(2):
                    for h in range(2):
                        rows = slice(64 * h, 64 * h + 64)
                        src = kv_bank(c)[rows, 256 * g + 128 * h:256 * g + 128 * h + 128]
                        if c == 0:
                            last = nc.vector.tensor_copy(state[rows, 1, g, :], src)
                        else:
                            last = nc.vector.scalar_tensor_tensor(out=state[rows, c + 1, g, :], in0=state[rows, c, g, :], scalar=bend[rows, g, c:c + 1],
                                                                  in1=src, op0=ALU.mult, op1=ALU.add)
                last.then_inc(st_ready, 1)

            def head_norm(t):
                n = rows_of(t)
                src = o_heads(t) if t < NT else o_smp[:].rearrange("p (a b) v -> p a b v", b=2)
                dve.wait_ge(osq_ready, t + 1)
                nc.vector.tensor_reduce(hms[0:n, t, :], dec[0:n, 0, 0:512].rearrange("p (h v) -> p h v", h=H_B), AX.X, ALU.add).then_inc(hms_ready, 1)
                dve.wait_ge(hroot_ready, t + 1)
                step(nc.vector.reciprocal(hrs[0:n, t, :], hrs[0:n, t, :]))
                if t >= 2:
                    dve.wait_ge(bT_ps, t - 1)
                dst = b_rows[0:n, t % 2, :].rearrange("p (a b v) -> p a b v", a=2, b=2)
                step(nc.vector.tensor_tensor(dst, src, bc(hrs[0:n, t, :].rearrange("p (a b) -> p a b", b=2).unsqueeze(3), [n, 2, 2, DV_B]), ALU.mult))
                dve.wait_ge(r_gained, t + 1)
                nc.vector.tensor_tensor(b_rows[0:n, t % 2, :], b_rows[0:n, t % 2, :], r[0:n, t, :], ALU.mult).then_inc(b_ready, 1)

            for t in range(NT):
                head_norm(t)
            dve.wait_ge(state_in, 48)
            dve.wait_ge(tail_ps, 1)
            for g in range(2):
                nc.vector.tensor_tensor(s_smp[:, g], s_smp[:, g], bc(la[:, g, SEQ:TOK].unsqueeze(2), [128, DEC_BATCH, DV_B]), ALU.mult).then_inc(s_decayed, 1)

            def v_block(h):
                if h >= 2:
                    dve.wait_ge(skv_ps, h - 1)
                nc.vector.tensor_tensor(vblk[:, h % 2], bc(v[0:DEC_BATCH, NT, DV_B * h:DV_B * h + DV_B].unsqueeze(1), [DEC_BATCH, DEC_BATCH, DV_B]),
                                        bc(own_seq[:].unsqueeze(2), [DEC_BATCH, DEC_BATCH, DV_B]), ALU.mult).then_inc(vblk_ready, 1)

            v_block(0)
            v_block(1)
            for h in range(H_B):
                rows = slice(64 * (h % 2), 64 * (h % 2) + 64)
                dve.wait_ge(skv_ps, h + 1)
                dve.wait_ge(s_decayed, 2)
                nc.vector.tensor_tensor(s_smp[rows, h // 2], s_smp[rows, h // 2], ps[0][rows, :].rearrange("p (b v) -> p b v", b=DEC_BATCH), ALU.add).then_inc(skv_used, 1)
                if h + 2 < H_B:
                    v_block(h + 2)
            for h in range(H_B):
                dve.wait_ge(so_ps, h + 1)
                step(nc.vector.tensor_tensor(vblk[:, 0], ps[3][0:DEC_BATCH, :].rearrange("p (b v) -> p b v", b=DEC_BATCH),
                                             bc(own_seq[:].unsqueeze(2), [DEC_BATCH, DEC_BATCH, DV_B]), ALU.mult))
                nc.vector.tensor_reduce(o_smp[:, h, :], vblk[:, 0].rearrange("p b v -> p v b"), AX.X, ALU.add).then_inc(so_used, 1)
                dve.wait_ge(so_used, h + 1)
            head_norm(NT)
            for t in range(NT + 1):
                n = rows_of(t)
                dve.wait_ge(y_ps, t + 1)
                nc.vector.tensor_tensor(x_sb[0:n, t, :], x_sb[0:n, t, :], ps[t % 2][0:n, :], ALU.add).then_inc(y_used, 1)

        @block.tensor
        def _(pe):
            for t in range(NT + 1):
                n = rows_of(t)
                pe.wait_ge(xs_ready, t + 1)
                if t >= 2:
                    pe.wait_ge(xT_ready, t - 1)
                for k in range(KC):
                    last = nc.tensor.transpose(ps[2 + t % 2][:, 128 * k:128 * k + n], xs[0:n, t % 2, 128 * k:128 * k + 128], ident[0:n, 0:n])
                last.then_inc(xT_ps, 1)
            pe.wait_ge(xT_ready, NT + 1)
            pe.wait_ge(w_in_in, 16 * KC)
            for j in range(N_JOBS):
                if j >= 2:
                    on_dve, n = evacuated(j - 2)
                    pe.wait_ge(job_dve if on_dve else job_act, n)
                rows = GATE_RANK if j == GLOW else 128
                if j in (L0, L1):
                    pe.wait_ge(job_act, evacuated(GLOW)[1])
                for b in range(2):
                    dst = ps[j % 2][0:rows, 512 * b:512 * b + half]
                    if j in (L0, L1):
                        last = nc.tensor.matmul(dst, w_gate[:, 128 * (j - L0):128 * (j - L0) + 128], glow[:, half * b:half * b + half], start=True, stop=True)
                        continue
                    for k in range(KC):
                        last = nc.tensor.matmul(dst, w_in[:, k, JOB_COLS[j]:JOB_COLS[j] + rows], xT[:, k, half * b:half * b + half],
                                                start=(k == 0), stop=(k == KC - 1))
                last.then_inc(job_ps, 1)
            V_COL = 2 * D_A + 2 * D_BK
            for t in range(NT + 1):
                n = rows_of(t)
                if t >= 2:
                    pe.wait_ge(row_act, 2 * (t - 1))
                for b in range(2):
                    for k in range(KC):
                        last = nc.tensor.matmul(ps[2 + t % 2][0:n, 512 * b:512 * b + 512], xT[:, k, cols_of(t)],
                                                w_in[:, k, V_COL + 512 * b:V_COL + 512 * b + 512], start=(k == 0), stop=(k == KC - 1))
                last.then_inc(row_ps, 1)
            pe.wait_ge(job_dve, evacuated(14)[1])
            pe.wait_ge(conv_ready, 4 * CONV_W + 1)
            for b in range(2):
                for c in range(4):
                    last = nc.tensor.matmul(ps[1][:, 512 * b:512 * b + half], mean_w[:], conv[:, c, half * b:half * b + half], start=(c == 0), stop=(c == 3))
            last.then_inc(mean_ps, 1)
            pe.wait_ge(sq_ready, 1)
            for b in range(2):
                for c in range(4):
                    last = nc.tensor.matmul(ps[0][:, 512 * b:512 * b + half], mean_w[:], xT[:, c, half * b:half * b + half], start=(c == 0), stop=(c == 3))
            last.then_inc(var_ps, 1)
            pe.wait_ge(lnroot_ready, 1)
            for c in range(4):
                nc.tensor.transpose(ps[0][0:PAD, 128 * c:128 * c + 128], u[:, c, SEQ:SEQ + PAD], ident[:])
                last = nc.tensor.transpose(ps[0][0:DEC_BATCH, 512 + 128 * c:512 + 128 * c + 128], u[:, c, PAD + SEQ:PAD + TOK], ident[:])
            last.then_inc(tail_ps, 1)
            pe.wait_ge(tail_ready, 2)
            pe.wait_ge(xc_ready, 1)
            for l in range(LEVELS + 1):
                if l < LEVELS:
                    pe.wait_ge(lev_ready, l + 1)
                    pe.wait_ge(dve_lev, l + 1)
                    q_, k_ = qE[:, l % 2], kE[:, l % 2]
                else:
                    q_, k_ = qT, kT
                for cp in range(2):
                    i = 2 * l + cp
                    if i >= 2:
                        pe.wait_ge(lev_used, i - 1)
                    for c in (2 * cp, 2 * cp + 1):
                        for h in range(H_B):
                            rows = slice(64 * (h % 2), 64 * (h % 2) + 64)
                            last = nc.tensor.matmul(by_head(i % 2, c, h), k_[rows, h // 2, 128 * c:128 * c + 128],
                                                    q_[rows, h // 2, 128 * c:128 * c + 128], start=True, stop=True)
                    last.then_inc(lev_ps, 1)
            pe.wait_ge(qk_dec, 2)
            pe.wait_ge(row_act, 2 * (NT + 1))
            for c in range(NT):
                for g in range(2):
                    last = nc.tensor.transpose(ps[2][:, 256 * c + 128 * g:256 * c + 128 * g + 128], kD[:, g, 128 * c:128 * c + 128], ident[:])
            last.then_inc(kdt_ps, 1)
            pe.wait_ge(kdt_ready, 1)
            for g in range(2):
                last = nc.tensor.transpose(ps[2][0:DEC_BATCH, 128 * g:128 * g + 128], kT[:, g, SEQ:TOK], ident[:])
            last.then_inc(krow_ps, 1)
            pe.wait_ge(lev_used, 2 * (LEVELS + 1))
            for c in range(NT):
                for g in range(2):
                    last = nc.tensor.matmul(kv_bank(c)[:, 256 * g:256 * g + 256], kDT[:, c, g, :], v[:, c, 256 * g:256 * g + 256], start=True, stop=True)
                last.then_inc(kv_ps, 1)

            def b_transposed(t):
                n = rows_of(t)
                pe.wait_ge(b_ready, t + 1)
                if t:
                    pe.wait_ge(bT_ready, t)
                else:
                    pe.wait_ge(krow_ready, 1)
                for c in range(4):
                    last = nc.tensor.transpose(ps[2][:, n * c:n * c + n], b_rows[0:n, t % 2, 128 * c:128 * c + 128], ident[0:n, 0:n])
                last.then_inc(bT_ps, 1)

            for t in range(NT):
                if t:
                    pe.wait_ge(st_ready, max(t, 2))
                if t >= 2:
                    pe.wait_ge(b_ready, t - 1)
                for h in range(H_B):
                    rows = slice(64 * (h % 2), 64 * (h % 2) + 64)
                    dst = by_head(1 + 2 * (t % 2), 0, h)
                    last = nc.tensor.matmul(dst, attn[:, t // 2, h % 2, t % 2, 128 * (h // 2):128 * (h // 2) + 128], v[:, t, 128 * h:128 * h + 128], start=True, stop=(t == 0))
                    if t:
                        last = nc.tensor.matmul(dst, qB[rows, h // 2, 128 * t:128 * t + 128], state[rows, t, h // 2, :], start=False, stop=True)
                last.then_inc(o_ps, 1)
                if t:
                    b_transposed(t - 1)
            b_transposed(NT - 1)
            pe.wait_ge(krow_ready, 1)
            pe.wait_ge(st_ready, NT)
            for h in range(H_B):
                rows = slice(64 * (h % 2), 64 * (h % 2) + 64)
                pe.wait_ge(vblk_ready, h + 1)
                if h:
                    pe.wait_ge(skv_used, h)
                for b in range(2):
                    last = nc.tensor.matmul(ps[0][rows, 512 * b:512 * b + 512], k_rows[:, 64 * h:64 * h + 64],
                                            vblk[:, h % 2, 4 * b:4 * b + 4, :].rearrange("p b v -> p (b v)"), start=True, stop=True)
                last.then_inc(skv_ps, 1)
            pe.wait_ge(skv_used, H_B)
            for h in range(H_B):
                rows = slice(64 * (h % 2), 64 * (h % 2) + 64)
                if h:
                    pe.wait_ge(so_used, h)
                for b in range(2):
                    last = nc.tensor.matmul(ps[3][0:DEC_BATCH, 512 * b:512 * b + 512], qT[rows, h // 2, SEQ:TOK],
                                            s_smp[rows, h // 2, 4 * b:4 * b + 4, :].rearrange("p b v -> p (b v)"), start=True, stop=True)
                last.then_inc(so_ps, 1)
            b_transposed(NT)
            pe.wait_ge(w_out_in, 16)
            pe.wait_ge(conv_out, 4)
            pe.wait_ge(bT_ready, NT + 1)
            for t in range(NT + 1):
                n = rows_of(t)
                if t >= 2:
                    pe.wait_ge(y_used, t - 1)
                for b in range(2):
                    for k in range(KC):
                        last = nc.tensor.matmul(ps[t % 2][0:n, 512 * b:512 * b + 512], xT[:, k, cols_of(t)], w_out[:, k, 512 * b:512 * b + 512],
                                                start=(k == 0), stop=(k == KC - 1))
                last.then_inc(y_ps, 1)


RING = 8
GROUP = 2
GROUPS = TOPK // GROUP
NEG = -3.0e38


def peer_layer(nc, w, layer, ident, x_sb):
    with ExitStack() as ctx:
        def sb(name, shape, dt=F32):
            return ctx.enter_context(nc.sbuf_tensor(f"p{layer}_{name}", shape, dt))

        def psum(name, shape):
            return ctx.enter_context(nc.psum_tensor(f"p{layer}_{name}", shape, F32))

        sem = signals(nc, ctx, f"p{layer}_")

        rows = sb("rows", [128, RING, 2 * D_MODEL])
        w_q = sb("w_q", [128, KC, H_P * D_KEY])
        keysT = sb("keysT", [128, 2 * H_P * N_KEYS])
        gain = sb("gain", [128, D_MODEL])
        zero = sb("zero", [128, 128])
        eps = sb("eps", [128, 1])
        iota16 = sb("iota16", [128, TOPK])
        spread = sb("spread", [DEC_BATCH, 128])
        gatherT = sb("gatherT", [128, DEC_BATCH])
        own_k = sb("own_k", [128, TOPK])
        x_cur = sb("x_cur", [128, D_MODEL])
        x_next = sb("x_next", [128, D_MODEL])
        xT = sb("xT", [128, KC, 128])
        sq = sb("sq", [128, D_MODEL])
        rstd = sb("rstd", [128, 1])
        qT = sb("qT", [128, 2, 128])
        q_rows = sb("q_rows", [128, D_KEY])
        s = sb("s", [128, 2, N_KEYS])
        s2 = sb("s2", [128, 2, N_KEYS])
        top = sb("top", [128, 2, TOPK])
        topi = sb("topi", [128, 2, TOPK], U32)
        topf = sb("topf", [128, 2, TOPK])
        cand = sb("cand", [128, TOPK, TOPK])
        cand2 = sb("cand2", [128, TOPK, TOPK])
        best = sb("best", [128, TOPK])
        besti = sb("besti", [128, TOPK], U32)
        split = sb("split", [128, 2, TOPK], U32)
        splitf = sb("splitf", [128, 2, TOPK])
        hit = sb("hit", [128, 2, TOPK, TOPK])
        sel = sb("sel", [128, 2, TOPK])
        rel = sb("rel", [128, TOPK])
        ex = sb("ex", [128, TOPK])
        ex_sum = sb("ex_sum", [128, 1])
        ex_inv = sb("ex_inv", [128, 1])
        ids = sb("ids", [128, NT * H_P * TOPK], U32)
        gates = sb("gates", [128, NT * H_P * TOPK])
        smp = sb("smp", [DEC_BATCH, 2, H_P * TOPK])
        smp_hit = sb("smp_hit", [128, 2 * H_P, TOPK])
        smp_own = sb("smp_own", [128, 2 * H_P])
        ids_lo = sb("ids_lo", [128, TOPK // 2], U32)
        ids_hi = sb("ids_hi", [128, TOPK // 2], U32)
        gate = sb("gate", [128, TOPK])
        dots = sb("dots", [128, 4, GROUP])
        acts = sb("acts", [128, 4, GROUP])
        diag = sb("diag", [128, 4, GROUP, 128])

        acc = psum("acc", [128, D_MODEL])
        turn = psum("turn", [128, D_MODEL])
        q_bank = psum("q_bank", [128, 512])
        s_bank = psum("s_bank", [128, 512])

        loaded, w_q_in, zeroed, ident_used = sem("loaded"), sem("w_q_in"), sem("zeroed"), sem("ident_used")
        sq_ready, root_ready, xn_ready, xT_ps, xT_ready, xcur_ready = (sem("sq_ready"), sem("root_ready"), sem("xn_ready"), sem("xT_ps"), sem("xT_ready"), sem("xcur_ready"))
        q_ps, q_ready, s_ps, s_ready, routed, rel_ready, ex_ready = (sem("q_ps"), sem("q_ready"), sem("s_ps"), sem("s_ready"), sem("routed"), sem("rel_ready"), sem("ex_ready"))
        qT_ps, qT_ready, looked = sem("qT_ps"), sem("qT_ready"), sem("looked")
        rt, inv_ready, gates_ready, gate_copied = sem("rt"), sem("inv_ready"), sem("gates_ready"), sem("gate_copied")
        lo_ready, hi_ready, paced = sem("lo_ready"), sem("hi_ready"), sem("paced")
        paced_dve, paced_pe, paced_act = sem("paced_dve"), sem("paced_pe"), sem("paced_act")
        rows_in = [sem(f"rows_in{i}") for i in range(RING)]
        dotted, gelud, diag_ready, rows_used, acc_ready, acc_used = (sem("dotted"), sem("gelud"), sem("diag_ready"), sem("rows_used"), sem("acc_ready"), sem("acc_used"))
        spread_ps, smp_step = sem("spread_ps"), sem("smp_step")
        N_LOADED = 16 * 6
        R_STEPS = 18

        block = ctx.enter_context(nc.Block())

        @block.sync
        def _(sp):
            sp.dma_start(gain[:], w["ffn_norm"][layer:layer + 1, :].to_broadcast([128, D_MODEL])).then_inc(loaded, 16)
            sp.dma_start(iota16[:], w["iota16"]).then_inc(loaded, 16)
            sp.dma_start(spread[:], w["spread"]).then_inc(loaded, 16)
            sp.dma_start(gatherT[:], w["gatherT"]).then_inc(loaded, 16)
            sp.dma_start(own_k[:], w["own_k"]).then_inc(loaded, 16)
            sp.dma_start(keysT[:], w["keysT"][layer]).then_inc(loaded, 16)
            for k in range(KC):
                sp.dma_start(w_q[:, k, :], w["peer_w_q"][layer, 128 * k:128 * k + 128, :]).then_inc(w_q_in, 16)

        @block.gpsimd
        def _(pool):
            nc.gpsimd.memset(zero[:], 0.0).then_inc(zeroed, 1)
            nc.gpsimd.memset(eps[:], EPS).then_inc(zeroed, 1)

            def gather(k, table_ids):
                nc.gpsimd.indirect_dma_start(out=rows[:, k % RING, :], out_offset=None, in_=w[f"peer_uv{layer}"],
                                             in_offset=bass.IndirectOffsetOnAxis(ap=table_ids[:, k % 8:k % 8 + 1], axis=0)
                                             ).then_inc(rows_in[k % RING], 16)

            def slot_free(n, k):
                pool.wait_ge(rows_used, n * TOPK + k - RING + 1)
                pool.sem_inc(paced, 1)

            pool.wait_ge(lo_ready, 1)
            for k in range(TOPK):
                if k == 8:
                    pool.wait_ge(hi_ready, 1)
                if k >= RING:
                    pool.wait_ge(rows_used, k - RING + 1)
                gather(k, ids_lo if k < 8 else ids_hi)
            with pool.Fori(1, NT * H_P) as n:
                for k in range(TOPK):
                    if k % 8 == 0:
                        pool.wait_ge(lo_ready if k == 0 else hi_ready, n + 1)
                        pool.sem_inc(paced, 1)
                    slot_free(n, k)
                    gather(k, ids_lo if k < 8 else ids_hi)
            pool.wait_ge(lo_ready, NT * H_P + 1)
            for k in range(H_P):
                pool.wait_ge(rows_used, NT * H_P * TOPK + k - RING + 1)
                gather(k, ids_lo)

        @block.scalar
        def _(act):
            def prepare(t, first=False):
                n = rows_of(t) if isinstance(t, int) else 128
                if not first:
                    act.wait_ge(xn_ready, t)
                    act.sem_inc(paced_act, 1)
                nc.scalar.activation(sq[0:n, :], x_sb[0:n, t, :] if isinstance(t, int) else x_sb[:, bass.ds(t, 1), :].rearrange("p a n -> p (a n)"),
                                     ACT.Square, scale=D_MODEL ** -0.5, accum_out=rstd[0:n, :]).then_inc(sq_ready, 1)
                act.wait_ge(sq_ready, t + 1)
                nc.scalar.activation(rstd[0:n, :], rstd[0:n, :], ACT.Sqrt, bias=eps[0:n, :]).then_inc(root_ready, 1)
                act.wait_ge(xT_ps, t + 1)
                nc.scalar.copy(xT[:, :, 0:n], turn[:, :].rearrange("p (k n) -> p k n", k=KC)[:, :, 0:n]).then_inc(xT_ready, 1)

            def q_out(m, n):
                act.wait_ge(q_ps, m + 1)
                nc.scalar.copy(q_rows[0:n, :], q_bank[0:n, 0:D_KEY]).then_inc(q_ready, 1)

            def qT_out(m, n):
                act.wait_ge(qT_ps, m + 1)
                nc.scalar.copy(qT[:, :, 0:n], q_bank[:, 256:512].rearrange("p (c n) -> p c n", c=2)[:, :, 0:n]).then_inc(qT_ready, 1)

            def s_out(m, n, first=False):
                act.wait_ge(s_ps, m + 1)
                if not first:
                    act.wait_ge(routed, m)
                nc.scalar.copy(s[0:n].rearrange("p c n -> p (c n)"), s_bank[0:n, 0:256]).then_inc(s_ready, 1)

            def exps(m, n):
                act.wait_ge(rel_ready, m + 1)
                nc.scalar.activation(ex[0:n, :], rel[0:n, :], ACT.Exp, accum_out=ex_sum[0:n, :]).then_inc(ex_ready, 1)

            def gelu(i, g):
                act.wait_ge(dotted, i + 1)
                nc.scalar.activation(acts[:, g % 4, :], dots[:, g % 4, :], ACT.Gelu).then_inc(gelud, 1)

            def window(t, h, n):
                m = (t + 1) * H_P + h
                i = (t * H_P + h) * GROUPS
                q_out(m, n)
                gelu(i, 0)
                gelu(i + 1, 1)
                qT_out(m, n)
                gelu(i + 2, 2)
                s_out(m, n)
                for g in range(3, GROUPS - 1):
                    gelu(i + g, g)
                exps(m, n)
                gelu(i + GROUPS - 1, GROUPS - 1)

            act.wait_ge(zeroed, 2)
            prepare(0, first=True)
            q_out(0, 128)
            qT_out(0, 128)
            s_out(0, 128, first=True)
            exps(0, 128)
            with act.Fori(1, H_P) as h:
                q_out(h, 128)
                qT_out(h, 128)
                s_out(h, 128)
                exps(h, 128)
            with act.Fori(0, NT - 1) as t:
                prepare(t + 1)
                with act.Fori(0, H_P) as h:
                    window(t, h, 128)
            prepare(NT)
            with act.Fori(0, H_P) as h:
                window(NT - 1, h, DEC_BATCH)
            for g in range(H_P // GROUP):
                gelu(NT * H_P * GROUPS + g, g)

        @block.vector
        def _(dve):
            def after(sem_, value):
                dve.wait_ge(sem_, value)
                dve.sem_inc(paced_dve, 1)

            def prepare(t, first=False):
                n = rows_of(t) if isinstance(t, int) else 128
                dve.wait_ge(root_ready, t + 1)
                nc.vector.reciprocal(rstd[0:n, :], rstd[0:n, :]).then_inc(inv_ready, 1)
                dve.wait_ge(inv_ready, t * (H_P + 1) + 1)
                if not first:
                    dve.wait_ge(xcur_ready, t)
                nc.vector.scalar_tensor_tensor(out=x_next[0:n, :], in0=x_sb[0:n, t, :] if isinstance(t, int) else x_sb[:, bass.ds(t, 1), :].rearrange("p a n -> p (a n)"),
                                               scalar=rstd[0:n, :], in1=gain[0:n, :], op0=ALU.mult, op1=ALU.mult).then_inc(xn_ready, 1)

            def route(m, n, t, h):
                parts = []
                R = R_STEPS

                def need(i):
                    after(rt, m * R + i)

                def first8():
                    after(s_ready, m + 1)
                    for c in range(2):
                        nc.vector.max(top[0:n, c, 0:8], s[0:n, c, :]).then_inc(rt, 1)
                    for c in range(2):
                        need(1 + c)
                        nc.vector.max_index(topi[0:n, c, 0:8], top[0:n, c, 0:8], s[0:n, c, :]).then_inc(rt, 1)
                    for c in range(2):
                        nc.vector.match_replace(s2[0:n, c, :], top[0:n, c, 0:8], s[0:n, c, :], NEG).then_inc(rt, 1)

                def next8():
                    for c in range(2):
                        need(5 + c)
                        nc.vector.max(top[0:n, c, 8:16], s2[0:n, c, :]).then_inc(rt, 1)
                    for c in range(2):
                        need(7 + c)
                        nc.vector.max_index(topi[0:n, c, 8:16], top[0:n, c, 8:16], s2[0:n, c, :]).then_inc(rt, 1)

                def pairs():
                    nc.vector.tensor_tensor(cand[0:n], bc(top[0:n, 0, :].unsqueeze(2), [n, TOPK, TOPK]),
                                            bc(top[0:n, 1, :].unsqueeze(1), [n, TOPK, TOPK]), ALU.add).then_inc(rt, 1)
                    need(10)
                    nc.vector.tensor_copy(topf[0:n], topi[0:n]).then_inc(rt, 1)
                    need(11)
                    nc.vector.max(best[0:n, 0:8], cand[0:n]).then_inc(rt, 1)
                    need(13)
                    cflat, c2flat = cand[0:n].rearrange("p a b -> p (a b)"), cand2[0:n].rearrange("p a b -> p (a b)")
                    nc.vector.max_index(besti[0:n, 0:8], best[0:n, 0:8], cflat).then_inc(rt, 1)
                    nc.vector.match_replace(c2flat, best[0:n, 0:8], cflat, NEG).then_inc(rt, 1)
                    need(15)
                    nc.vector.max(best[0:n, 8:16], c2flat).then_inc(rt, 1)
                    need(16)
                    nc.vector.max_index(besti[0:n, 8:16], best[0:n, 8:16], c2flat).then_inc(rt, 1)
                    nc.vector.tensor_scalar(rel[0:n, :], best[0:n, :], best[0:n, 0:1], None, ALU.subtract).then_inc(rel_ready, 1)

                def lookup():
                    need(17)
                    nc.vector.tensor_scalar(split[0:n, 0, :], besti[0:n, :], 4, None, ALU.logical_shift_right)
                    nc.vector.tensor_scalar(split[0:n, 1, :], besti[0:n, :], 15, None, ALU.bitwise_and).then_inc(rt, 1)
                    dve.wait_ge(rt, m * R + 18)
                    nc.vector.tensor_copy(splitf[0:n], split[0:n]).then_inc(looked, 1)
                    dve.wait_ge(looked, 4 * m + 1)
                    nc.vector.tensor_tensor(hit[0:n].rearrange("p c k j -> p (c k) j"), bc(splitf[0:n].rearrange("p c k -> p (c k)").unsqueeze(2), [n, 2 * TOPK, TOPK]),
                                            bc(iota16[0:n, :].unsqueeze(1), [n, 2 * TOPK, TOPK]), ALU.is_equal).then_inc(looked, 1)
                    dve.wait_ge(looked, 4 * m + 2)
                    nc.vector.tensor_tensor(hit[0:n], hit[0:n], bc(topf[0:n].unsqueeze(2), [n, 2, TOPK, TOPK]), ALU.mult).then_inc(looked, 1)
                    dve.wait_ge(looked, 4 * m + 3)
                    nc.vector.tensor_reduce(sel[0:n].rearrange("p c k -> p (c k)"), hit[0:n].rearrange("p c k j -> p (c k) j"), AX.X, ALU.add).then_inc(looked, 1)
                    dve.wait_ge(looked, 4 * m + 4)
                    if n == 128:
                        dst = ids[:, bass.ds(m * TOPK, TOPK)] if not isinstance(m, int) else ids[:, m * TOPK:m * TOPK + TOPK]
                    else:
                        dst = smp[0:n, 0, bass.ds(h * TOPK, TOPK)]
                    nc.vector.scalar_tensor_tensor(out=dst, in0=sel[0:n, 0, :], scalar=float(N_KEYS), in1=sel[0:n, 1, :], op0=ALU.mult, op1=ALU.add).then_inc(routed, 1)

                def softmax():
                    dve.wait_ge(ex_ready, m + 1)
                    nc.vector.reciprocal(ex_inv[0:n, :], ex_sum[0:n, :]).then_inc(inv_ready, 1)
                    dve.wait_ge(inv_ready, t * (H_P + 1) + h + 2)
                    if n == 128:
                        dst = gates[:, bass.ds(m * TOPK, TOPK)] if not isinstance(m, int) else gates[:, m * TOPK:m * TOPK + TOPK]
                    else:
                        dst = smp[0:n, 1, bass.ds(h * TOPK, TOPK)]
                    nc.vector.tensor_scalar(dst, ex[0:n, :], ex_inv[0:n, :], None, ALU.mult).then_inc(gates_ready, 1)

                return [first8, next8, pairs, lookup], softmax

            def dot(n, g, table=TOPK // RING):
                for j in range(GROUP):
                    k = g * GROUP + j
                    dve.wait_ge(rows_in[k % RING], (n * table + k // RING + 1) * 16)
                    last = nc.vector.tensor_tensor_reduce(rows[:, k % RING, 0:D_MODEL], rows[:, k % RING, 0:D_MODEL], x_cur[:], 1.0, 0.0,
                                                          ALU.mult, ALU.add, dots[:, g % 4, j:j + 1])
                last.then_inc(dotted, 1)

            def weigh(i, g, wide=True):
                dve.wait_ge(gelud, i + 1)
                for j in range(GROUP):
                    k = g * GROUP + j
                    dst, unit = (diag[:, g % 4, j, :], ident[:]) if wide else (diag[:, g % 4, j, 0:DEC_BATCH], gatherT[:])
                    last = nc.vector.tensor_scalar(dst, unit, acts[:, g % 4, j:j + 1], gate[:, k:k + 1], ALU.mult, ALU.mult)
                last.then_inc(diag_ready, 1)

            def copy_ids(dst, n, at, sem_):
                if not isinstance(n, int):
                    dve.sem_inc(paced_dve, 1)
                src = ids[:, n * TOPK + at:n * TOPK + at + 8] if isinstance(n, int) else ids[:, bass.ds(n * TOPK + at, 8)]
                nc.vector.tensor_copy(dst[:], src).then_inc(sem_, 1)

            def window(t, h, rows_next, last_head=False):
                n = t * H_P + h
                m = n + H_P
                parts, softmax = route(m, rows_next, t + 1, h)
                dve.wait_ge(gates_ready, n + 1)
                after(diag_ready, n * GROUPS + 1)
                src = gates[:, n * TOPK:n * TOPK + TOPK] if isinstance(n, int) else gates[:, bass.ds(n * TOPK, TOPK)]
                nc.vector.tensor_copy(gate[:], src).then_inc(gate_copied, 1)
                dve.wait_ge(gate_copied, n + 1)
                for g in range(GROUPS):
                    dot(n, g)
                    if g == 0:
                        copy_ids(ids_hi, n, 8, hi_ready)
                    if g == 3 and not last_head:
                        dve.wait_ge(routed, n + 2)
                        copy_ids(ids_lo, n + 1, 0, lo_ready)
                    if g:
                        weigh(n * GROUPS + g - 1, g - 1)
                    if 3 <= g < 7:
                        parts[g - 3]()
                softmax()
                weigh(n * GROUPS + GROUPS - 1, GROUPS - 1)

            def next_x(t):
                dve.wait_ge(dotted, t * H_P * GROUPS)
                nc.vector.tensor_copy(x_cur[:], x_next[:]).then_inc(xcur_ready, 1)
                dve.wait_ge(xcur_ready, t + 1)

            def add_to_x(t):
                n = rows_of(t) if isinstance(t, int) else 128
                xt = x_sb[0:n, t, :] if isinstance(t, int) else x_sb[:, bass.ds(t, 1), :].rearrange("p a n -> p (a n)")
                dve.wait_ge(acc_ready, t + 1)
                nc.vector.tensor_tensor(xt, xt, acc[0:n, :], ALU.add).then_inc(acc_used, 1)

            dve.sem_inc(diag_ready, 1)
            dve.sem_inc(acc_used, 1)
            dve.wait_ge(loaded, N_LOADED)
            prepare(0, first=True)
            dve.wait_ge(xn_ready, 1)
            nc.vector.tensor_copy(x_cur[:], x_next[:]).then_inc(xcur_ready, 1)
            with dve.Fori(0, H_P) as h:
                parts, softmax = route(h, 128, 0, h)
                for part in parts:
                    part()
                softmax()
            dve.wait_ge(routed, H_P)
            copy_ids(ids_lo, 0, 0, lo_ready)
            with dve.Fori(0, NT - 1) as t:
                prepare(t + 1)
                with dve.Fori(0, H_P) as h:
                    window(t, h, 128)
                next_x(t + 1)
                add_to_x(t)
            prepare(NT)
            with dve.Fori(0, H_P - 1) as h:
                window(NT - 1, h, DEC_BATCH)
            window(NT - 1, H_P - 1, DEC_BATCH, last_head=True)
            dve.wait_ge(spread_ps, 1)
            nc.vector.tensor_tensor(smp_hit[:], q_bank[:, 0:256].rearrange("p (a k) -> p a k", k=TOPK), bc(own_k[:].unsqueeze(1), [128, 2 * H_P, TOPK]), ALU.mult).then_inc(smp_step, 1)
            dve.wait_ge(smp_step, 1)
            nc.vector.tensor_reduce(smp_own[:], smp_hit[:], AX.X, ALU.add).then_inc(smp_step, 1)
            dve.wait_ge(smp_step, 2)
            nc.vector.tensor_copy(ids_lo[:], smp_own[:, 0:H_P]).then_inc(lo_ready, 1)
            dve.wait_ge(diag_ready, NT * H_P * GROUPS + 1)
            nc.vector.tensor_copy(gate[:, 0:H_P], smp_own[:, H_P:2 * H_P]).then_inc(gate_copied, 1)
            dve.wait_ge(dotted, NT * H_P * GROUPS)
            nc.vector.tensor_copy(x_cur[:], turn[:, :]).then_inc(xcur_ready, 1)
            add_to_x(NT - 1)
            dve.wait_ge(xcur_ready, NT + 1)
            dve.wait_ge(gate_copied, NT * H_P + 1)
            for g in range(H_P // GROUP):
                dot(NT * H_P, g)
                if g:
                    weigh(NT * H_P * GROUPS + g - 1, g - 1, wide=False)
            weigh(NT * H_P * GROUPS + 3, 3, wide=False)
            add_to_x(NT)

        @block.tensor
        def _(pe):
            def transpose_x(t):
                n = rows_of(t) if isinstance(t, int) else 128
                pe.wait_ge(xn_ready, t + 1)
                for k in range(KC):
                    last = nc.tensor.transpose(turn[:, 128 * k:128 * k + n], x_next[0:n, 128 * k:128 * k + 128], ident[0:n, 0:n])
                last.then_inc(xT_ps, 1)
                pe.wait_ge(xT_ready, t + 1)

            def queries(m, h, n, first=False):
                if not first:
                    pe.wait_ge(qT_ready, m)
                for k in range(KC):
                    cols = w_q[:, k, bass.ds(h * D_KEY, D_KEY)]
                    last = nc.tensor.matmul(q_bank[0:n, 0:D_KEY], xT[:, k, 0:n], cols, start=(k == 0), stop=(k == KC - 1))
                last.then_inc(q_ps, 1)

            def transpose_q(m, n):
                pe.wait_ge(q_ready, m + 1)
                pe.sem_inc(paced_pe, 1)
                for c in range(2):
                    last = nc.tensor.transpose(q_bank[:, 256 + 128 * c:256 + 128 * c + n], q_rows[0:n, 128 * c:128 * c + 128], ident[0:n, 0:n])
                last.then_inc(qT_ps, 1)

            def scores(m, h, n, first=False):
                if not first:
                    pe.wait_ge(s_ready, m)
                pe.wait_ge(qT_ready, m + 1)
                for c in range(2):
                    last = nc.tensor.matmul(s_bank[0:n, 128 * c:128 * c + 128], qT[:, c, 0:n], keysT[:, bass.ds((2 * h + c) * N_KEYS, N_KEYS)], start=True, stop=True)
                last.then_inc(s_ps, 1)

            def open_acc(t, n):
                pe.wait_ge(acc_used, t + 1)
                for b in range(2):
                    nc.tensor.matmul(acc[0:n, 512 * b:512 * b + 512], zero[:, 0:n], keysT[:, 0:512], start=True, stop=False)

            def close_acc(n):
                for b in range(2):
                    last = nc.tensor.matmul(acc[0:n, 512 * b:512 * b + 512], zero[:, 0:n], keysT[:, 0:512], start=False, stop=True)
                last.then_inc(acc_ready, 1)

            def experts(i, g, n):
                pe.wait_ge(diag_ready, i + 2)
                for j in range(GROUP):
                    k = g * GROUP + j
                    for b in range(2):
                        last = nc.tensor.matmul(acc[0:n, 512 * b:512 * b + 512], diag[:, g % 4, j, 0:n], rows[:, k % RING, D_MODEL + 512 * b:D_MODEL + 512 * b + 512],
                                                start=False, stop=False)
                    last.then_inc(rows_used, 1)

            def window(t, h, n):
                m = (t + 1) * H_P + h
                i = (t * H_P + h) * GROUPS
                queries(m, h, n)
                experts(i, 0, 128)
                transpose_q(m, n)
                experts(i + 1, 1, 128)
                scores(m, h, n)
                for g in range(2, GROUPS):
                    experts(i + g, g, 128)

            pe.wait_ge(zeroed, 2)
            pe.wait_ge(loaded, N_LOADED)
            transpose_x(0)
            pe.wait_ge(w_q_in, 16 * KC)
            queries(0, 0, 128, first=True)
            transpose_q(0, 128)
            scores(0, 0, 128, first=True)
            with pe.Fori(1, H_P) as h:
                queries(h, h, 128)
                transpose_q(h, 128)
                scores(h, h, 128)
            with pe.Fori(0, NT - 1) as t:
                transpose_x(t + 1)
                open_acc(t, 128)
                with pe.Fori(0, H_P) as h:
                    window(t, h, 128)
                close_acc(128)
            transpose_x(NT)
            open_acc(NT - 1, 128)
            with pe.Fori(0, H_P) as h:
                window(NT - 1, h, DEC_BATCH)
            close_acc(128)
            pe.wait_ge(gates_ready, (NT + 1) * H_P)
            pe.wait_ge(routed, (NT + 1) * H_P)
            nc.tensor.matmul(q_bank[:, 0:256], spread[:], smp[:].rearrange("p c n -> p (c n)"), start=True, stop=True)
            for b in range(2):
                last = nc.tensor.matmul(turn[:, 512 * b:512 * b + 512], spread[:], x_next[0:DEC_BATCH, 512 * b:512 * b + 512], start=True, stop=True)
            last.then_inc(spread_ps, 1)
            open_acc(NT, DEC_BATCH)
            for g in range(H_P // GROUP):
                experts(NT * H_P * GROUPS + g, g, DEC_BATCH)
            close_acc(DEC_BATCH)


def latent_projections(nc, w, out, ident, x_sb, smp):
    with ExitStack() as ctx:
        def sb(name, shape, dt=F32):
            return ctx.enter_context(nc.sbuf_tensor("c_" + name, shape, dt))

        sem = signals(nc, ctx, "c_")

        w_in = sb("w_in", [128, KC, D_IN_C])
        w_qb = sb("w_qb", [128, 3, H_C * 96])
        w_uk = sb("w_uk", [128, 2, H_C * D_NOPE])
        w_uv = sb("w_uv", [128, 2, H_C * D_V])
        w_out = sb("w_out", [128, KC, D_MODEL])
        norm_col = sb("norm_col", [128, KC])
        qn_col = sb("qn_col", [128, 3])
        kv_gain = sb("kv_gain", [128, R_KV])
        cos2 = sb("cos2", [128, NT + 1, D_ROPE])
        sin2 = sb("sin2", [128, NT + 1, D_ROPE])
        eps = sb("eps", [128, 1])
        causal = sb("causal", [128, 128])
        sq = sb("sq", [128, D_MODEL])
        rstd = sb("rstd", [128, 1])
        rstd2 = sb("rstd2", [128, 2])
        xs = sb("xs", [128, D_MODEL])
        xT = sb("xT", [128, KC, 128])
        cqT = sb("cqT", [128, 3, 128])
        ckv = sb("ckv", [128, 2, R_KV])
        ckvT = sb("ckvT", [128, 2, 128])
        kz = sb("kz", [128, 2, 96])
        kraw = sb("kraw", [128, D_ROPE])
        q = sb("q", [128, H_C, 96])
        cq = q[:, :, :].rearrange("p h d -> p (h d)")[:, 0:R_Q]
        rot = sb("rot", [128, 2, H_C, D_ROPE])
        qT = sb("qT", [96, H_C, 128])
        kT = sb("kT", [96, H_C, SEQ])
        v = sb("v", [128, NT, H_C * D_V])
        nmax = sb("nmax", [128, 2, 2])
        prob = rot[:, :, :, :].rearrange("p b h d -> p b (h d)")
        probT = xs[:, :].rearrange("p (b n) -> p b n", b=2)
        sums = sb("sums", [128, H_C])
        o = sq
        oT = xT
        ps = [ctx.enter_context(nc.psum_tensor(f"c_ps{i}", [128, 1024], F32)) for i in range(4)]

        small_in, w_in_in, wqb_in, wuk_in, wout_in = sem("small_in"), sem("w_in_in"), sem("wqb_in"), sem("wuk_in"), sem("wout_in")
        consts, sq_ready, root_ready, dve_step, xs_ready, xT_ps, xT_ready, z_ps = (sem("consts"), sem("sq_ready"), sem("root_ready"), sem("dve_step"), sem("xs_ready"), sem("xT_ps"), sem("xT_ready"), sem("z_ps"))
        zsq_ready, zroot_ready, z_used, lat_ready, latT_ps, cqT_ready, ckvT_ready = (sem("zsq_ready"), sem("zroot_ready"), sem("z_used"), sem("lat_ready"), sem("latT_ps"), sem("cqT_ready"), sem("ckvT_ready"))
        q_ps, q_ready, k_ps, k_used, v_ps, v_ready, rope_ready, qT_ps, qT_act, qT_dve = (sem("q_ps"), sem("q_ready"), sem("k_ps"), sem("k_used"), sem("v_ps"), sem("v_ready"), sem("rope_ready"), sem("qT_ps"), sem("qT_act"), sem("qT_dve"))
        s_ps, max_ready, neg_ready, p_ready, pT_ps, pT_ready, o_ps, o_ready, oT_ps, oT_ready, y_ps, y_used = (sem(n) for n in (
            "s_ps", "max_ready", "neg_ready", "p_ready", "pT_ps", "pT_ready", "o_ps", "o_ready", "oT_ps", "oT_ready", "y_ps", "y_used"))
        stores = sem("stores")
        block = ctx.enter_context(nc.Block())
        N_SMALL = 6

        @block.sync
        def _(sp):
            for dst, name in ((norm_col, "c_norm_cols"), (qn_col, "q_norm_cols"), (cos2, "cos2"), (sin2, "sin2"), (causal, "causal")):
                sp.dma_start(dst[:], w[name]).then_inc(small_in, 16)
            sp.dma_start(kv_gain[:], w["c_kv_norm"].to_broadcast([128, R_KV])).then_inc(small_in, 16)
            sp.dma_start(w_in[:], w["c_w_in"][0].rearrange("(k p) n -> p k n", p=128)).then_inc(w_in_in, 16)
            sp.dma_start(w_qb[:], w["c_w_q_b"][0].rearrange("(k p) n -> p k n", p=128)).then_inc(wqb_in, 16)
            sp.dma_start(w_uk[:], w["c_w_uk"][0].rearrange("(k p) h n -> p k (h n)", p=128)).then_inc(wuk_in, 16)
            sp.dma_start(w_uv[:], w["c_w_uv"][0].rearrange("(k p) h n -> p k (h n)", p=128)).then_inc(wuk_in, 16)
            sp.dma_start(w_out[:], w["c_w_out"][0].rearrange("(k p) n -> p k n", p=128)).then_inc(wout_in, 16)
            for t in range(NT + 1):
                n = rows_of(t)
                sp.wait_ge(lat_ready, t + 1)
                if t < NT:
                    ckv_dst, kpe_dst = out["new_ckv_prompt"][0, 0, 128 * t:128 * t + 128, :], out["new_kpe_prompt"][0, 0, 128 * t:128 * t + 128, :]
                else:
                    ckv_dst, kpe_dst = out["new_ckv_sample"][0, :, 0, :], out["new_kpe_sample"][0, :, 0, :]
                sp.dma_start(ckv_dst, ckv[0:n, t % 2, :]).then_inc(stores, 16)
                sp.dma_start(kpe_dst, kz[0:n, t % 2, 64:96]).then_inc(stores, 16)
                sp.wait_ge(stores, 32 * (t + 1))

        @block.gpsimd
        def _(pool):
            nc.gpsimd.memset(eps[:], EPS).then_inc(consts, 1)
            nc.gpsimd.memset(kz[:], 0.0).then_inc(consts, 1)

        @block.scalar
        def _(act):
            act.wait_ge(consts, 2)
            for t in range(NT + 1):
                n = rows_of(t)
                if t:
                    act.wait_ge(xs_ready, t)
                    act.wait_ge(oT_ps, t)
                nc.scalar.activation(sq[0:n, :], x_sb[0:n, t, :], ACT.Square, scale=D_MODEL ** -0.5, accum_out=rstd[0:n, :]).then_inc(sq_ready, 1)
                act.wait_ge(sq_ready, t + 1)
                nc.scalar.activation(rstd[0:n, :], rstd[0:n, :], ACT.Sqrt, bias=eps[0:n, :]).then_inc(root_ready, 1)
                act.wait_ge(z_ps, t + 1)
                nc.scalar.activation(sq[0:n, 0:R_Q], ps[2][0:n, 0:R_Q], ACT.Square, scale=R_Q ** -0.5, accum_out=rstd2[0:n, 0:1])
                nc.scalar.activation(sq[0:n, 512:512 + R_KV], ps[2][0:n, 512:512 + R_KV], ACT.Square, scale=R_KV ** -0.5, accum_out=rstd2[0:n, 1:2]).then_inc(zsq_ready, 1)
                act.wait_ge(zsq_ready, t + 1)
                nc.scalar.activation(rstd2[0:n, :], rstd2[0:n, :], ACT.Sqrt, bias=eps[0:n, :]).then_inc(zroot_ready, 1)
                act.wait_ge(latT_ps, t + 1)
                if t < NT:
                    nc.scalar.copy(ckvT[:, :, 0:n], ps[3][:, 512:768].rearrange("p (c n) -> p c n", c=2))
                    nc.scalar.copy(kT[64:96, :, cols_of(t)], bc(ps[3][64:96, 768:896].unsqueeze(1), [32, H_C, 128])).then_inc(ckvT_ready, 1)
                else:
                    nc.scalar.copy(smp["ckvT"][:], ps[3][:, 512:768].rearrange("p (c n) -> p c n", c=2)[:, :, 0:n])
                    nc.scalar.copy(smp["kpeT"][64:96, :], ps[3][64:96, 768:768 + n]).then_inc(ckvT_ready, 1)
                act.wait_ge(q_ps, t + 1)
                if t:
                    act.wait_ge(qT_ps, t)
                q_flat = q[0:n].rearrange("p h d -> p (h d)")
                nc.scalar.copy(q_flat[:, 0:1024], ps[0][0:n, :]).then_inc(q_ready, 1)
                nc.scalar.copy(q_flat[:, 1024:1536], ps[1][0:n, 0:512]).then_inc(q_ready, 1)
                if t == NT:
                    break
                act.wait_ge(v_ps, t + 1)
                nc.scalar.copy(v[:, t, :], ps[3][:, :]).then_inc(v_ready, 1)
                act.wait_ge(qT_ps, t + 1)
                nc.scalar.copy(qT[:, 0:8, :], ps[0][0:96, :].rearrange("p (h n) -> p h n", h=8)).then_inc(qT_act, 1)
                keys = 128 * (t + 1)
                for h in range(H_C):
                    i = H_C * t + h
                    act.wait_ge(neg_ready, i + 1)
                    if i >= 2:
                        act.wait_ge(pT_ps, i - 1)
                    if h == 0 and t:
                        act.wait_ge(o_ready, t)
                    nc.scalar.activation(prob[:, i % 2, 0:keys], ps[0][:, 512 * (i % 2):512 * (i % 2) + keys], ACT.Exp, scale=MLA_SCALE,
                                         bias=nmax[:, 1, i % 2:i % 2 + 1], accum_out=sums[:, h:h + 1]).then_inc(p_ready, 1)
                act.wait_ge(oT_ps, t + 1)
                nc.scalar.copy(oT[:].rearrange("p k n -> p (k n)"), ps[3][:, :]).then_inc(oT_ready, 1)

        @block.vector
        def _(dve):
            steps = [0]

            def step(ins):
                steps[0] += 1
                ins.then_inc(dve_step, 1)
                dve.wait_ge(dve_step, steps[0])

            def rotate(dst, src, n, heads, t):
                c = bc(cos2[0:n, t, :].unsqueeze(1), [n, heads, D_ROPE])
                nc.vector.tensor_tensor(rot[0:n, 1, 0:heads, 0:16], src[:, :, 16:32], bc(sin2[0:n, t, 0:16].unsqueeze(1), [n, heads, 16]), ALU.mult)
                nc.vector.tensor_tensor(rot[0:n, 1, 0:heads, 16:32], src[:, :, 0:16], bc(sin2[0:n, t, 16:32].unsqueeze(1), [n, heads, 16]), ALU.mult)
                step(nc.vector.tensor_tensor(rot[0:n, 0, 0:heads, :], src, c, ALU.mult))
                return nc.vector.tensor_tensor(dst, rot[0:n, 0, 0:heads, :], rot[0:n, 1, 0:heads, :], ALU.add)

            dve.wait_ge(small_in, 16 * N_SMALL)
            dve.wait_ge(consts, 2)
            for t in range(NT + 1):
                n = rows_of(t)
                dve.wait_ge(root_ready, t + 1)
                step(nc.vector.reciprocal(rstd[0:n, :], rstd[0:n, :]))
                if t:
                    dve.wait_ge(xT_ps, t)
                nc.vector.tensor_scalar(xs[0:n, :], x_sb[0:n, t, :], rstd[0:n, :], None, ALU.mult).then_inc(xs_ready, 1)
                dve.wait_ge(xT_ps, t + 1)
                nc.vector.tensor_tensor(xT[:, :, 0:n], ps[3][:, :].rearrange("p (k n) -> p k n", k=KC)[:, :, 0:n], bc(norm_col[:].unsqueeze(2), [128, KC, n]), ALU.mult).then_inc(xT_ready, 1)
                dve.wait_ge(zroot_ready, t + 1)
                step(nc.vector.reciprocal(rstd2[0:n, :], rstd2[0:n, :]))
                if t:
                    dve.wait_ge(latT_ps, t)
                nc.vector.tensor_scalar(cq[0:n, :], ps[2][0:n, 0:R_Q], rstd2[0:n, 0:1], None, ALU.mult)
                if t >= 2:
                    dve.wait_ge(stores, 32 * (t - 1))
                nc.vector.scalar_tensor_tensor(out=ckv[0:n, t % 2, :], in0=ps[2][0:n, 512:512 + R_KV], scalar=rstd2[0:n, 1:2], in1=kv_gain[0:n, :], op0=ALU.mult, op1=ALU.mult)
                step(nc.vector.tensor_copy(kraw[0:n, :], ps[2][0:n, 512 + R_KV:512 + R_KV + D_ROPE]))
                rotate(kz[0:n, t % 2, 64:96].unsqueeze(1), kraw[0:n, :].unsqueeze(1), n, 1, t).then_inc(lat_ready, 1)
                dve.wait_ge(latT_ps, t + 1)
                nc.vector.tensor_tensor(cqT[:, :, 0:n], ps[3][:, 0:384].rearrange("p (c n) -> p c n", c=3)[:, :, 0:n], bc(qn_col[:].unsqueeze(2), [128, 3, n]), ALU.mult).then_inc(cqT_ready, 1)
                if t < NT:
                    dve.wait_ge(k_ps, t + 1)
                    nc.vector.tensor_copy(kT[0:64, 0:8, cols_of(t)], ps[3][0:64, :].rearrange("p (h n) -> p h n", h=8)).then_inc(k_used, 1)
                    nc.vector.tensor_copy(kT[0:64, 8:16, cols_of(t)], ps[2][0:64, :].rearrange("p (h n) -> p h n", h=8)).then_inc(k_used, 1)
                dve.wait_ge(q_ready, 2 * (t + 1))
                if t == NT:
                    dve.wait_ge(lat_ready, NT + 1)
                    nc.vector.tensor_copy(smp["ckv"][:], ckv[0:n, t % 2, :])
                    rotate(q[0:n, :, 64:96], q[0:n, :, 64:96], n, H_C, t).then_inc(rope_ready, 1)
                    dve.wait_ge(rope_ready, t + 1)
                    nc.vector.tensor_copy(smp["qn"][:], q[0:n, :, 0:64])
                    nc.vector.tensor_copy(smp["qp"][:], bc(q[0:n, :, 64:96].unsqueeze(2), [n, H_C, 4, D_ROPE]))
                    break
                rotate(q[0:n, :, 64:96], q[0:n, :, 64:96], n, H_C, t).then_inc(rope_ready, 1)
                dve.wait_ge(qT_ps, t + 1)
                nc.vector.tensor_copy(qT[:, 8:16, :], ps[1][0:96, :].rearrange("p (h n) -> p h n", h=8)).then_inc(qT_dve, 1)
                keys = 128 * (t + 1)

                def turn_out(i):
                    dve.wait_ge(pT_ps, i + 1)
                    if i >= 2:
                        dve.wait_ge(o_ps, i - 1)
                    nc.vector.tensor_copy(probT[:, i % 2, 0:keys], ps[1][:, 512 * (i % 2):512 * (i % 2) + keys]).then_inc(pT_ready, 1)

                for h in range(H_C):
                    i = H_C * t + h
                    dve.wait_ge(s_ps, i + 1)
                    if i >= 2:
                        dve.wait_ge(p_ready, i - 1)
                    nc.vector.tensor_reduce(nmax[:, 0, i % 2:i % 2 + 1], ps[0][:, 512 * (i % 2):512 * (i % 2) + keys], AX.X, ALU.max).then_inc(max_ready, 1)
                    dve.wait_ge(max_ready, i + 1)
                    nc.vector.tensor_scalar(nmax[:, 1, i % 2:i % 2 + 1], nmax[:, 0, i % 2:i % 2 + 1], -MLA_SCALE, None, ALU.mult).then_inc(neg_ready, 1)
                    if h:
                        turn_out(i - 1)
                turn_out(H_C * t + H_C - 1)
                dve.wait_ge(p_ready, H_C * (t + 1))
                step(nc.vector.reciprocal(sums[:], sums[:]))
                dve.wait_ge(o_ps, H_C * (t + 1))
                nc.vector.tensor_tensor(o[:].rearrange("p (h v) -> p h v", h=H_C), ps[2][:, :].rearrange("p (h v) -> p h v", h=H_C),
                                        bc(sums[:].unsqueeze(2), [128, H_C, D_V]), ALU.mult).then_inc(o_ready, 1)
                dve.wait_ge(y_ps, t + 1)
                nc.vector.tensor_tensor(x_sb[:, t, :], x_sb[:, t, :], ps[2][:, :], ALU.add).then_inc(y_used, 1)

        @block.tensor
        def _(pe):
            for t in range(NT + 1):
                n = rows_of(t)
                pe.wait_ge(xs_ready, t + 1)
                for k in range(KC):
                    last = nc.tensor.transpose(ps[3][:, 128 * k:128 * k + n], xs[0:n, 128 * k:128 * k + 128], ident[0:n, 0:n])
                last.then_inc(xT_ps, 1)
                pe.wait_ge(xT_ready, t + 1)
                pe.wait_ge(w_in_in, 16)
                if t:
                    pe.wait_ge(y_used, t)
                for at, lo, hi in ((0, 0, R_Q), (512, R_Q, D_IN_C)):
                    for k in range(KC):
                        last = nc.tensor.matmul(ps[2][0:n, at:at + hi - lo], xT[:, k, 0:n], w_in[:, k, lo:hi], start=(k == 0), stop=(k == KC - 1))
                last.then_inc(z_ps, 1)
                pe.wait_ge(lat_ready, t + 1)
                for c in range(3):
                    nc.tensor.transpose(ps[3][:, 128 * c:128 * c + n], cq[0:n, 128 * c:128 * c + 128], ident[0:n, 0:n])
                for c in range(2):
                    nc.tensor.transpose(ps[3][:, 512 + 128 * c:512 + 128 * c + n], ckv[0:n, t % 2, 128 * c:128 * c + 128], ident[0:n, 0:n])
                nc.tensor.transpose(ps[3][0:96, 768:768 + n], kz[0:n, t % 2, :], ident[0:n, 0:n]).then_inc(latT_ps, 1)
                pe.wait_ge(cqT_ready, t + 1)
                pe.wait_ge(wqb_in, 16)
                for b in range(3):
                    for k in range(3):
                        last = nc.tensor.matmul(ps[b // 2][0:n, 512 * (b % 2):512 * (b % 2) + 512], cqT[:, k, 0:n], w_qb[:, k, 512 * b:512 * b + 512], start=(k == 0), stop=(k == 2))
                last.then_inc(q_ps, 1)
                if t == NT:
                    break
                pe.wait_ge(ckvT_ready, t + 1)
                pe.wait_ge(wuk_in, 32)
                for h in range(H_C):
                    dst = ps[3 - h // 8][0:64, 128 * (h % 8):128 * (h % 8) + 128]
                    for c in range(2):
                        last = nc.tensor.matmul(dst, w_uk[:, c, 64 * h:64 * h + 64], ckvT[:, c, :], start=(c == 0), stop=(c == 1))
                last.then_inc(k_ps, 1)
                pe.wait_ge(k_used, 2 * (t + 1))
                for b in range(2):
                    for c in range(2):
                        last = nc.tensor.matmul(ps[3][:, 512 * b:512 * b + 512], ckvT[:, c, :], w_uv[:, c, 512 * b:512 * b + 512], start=(c == 0), stop=(c == 1))
                last.then_inc(v_ps, 1)
                pe.wait_ge(q_ready, 2 * (t + 1))
                pe.wait_ge(rope_ready, t + 1)
                for h in range(H_C):
                    last = nc.tensor.transpose(ps[h // 8][0:96, 128 * (h % 8):128 * (h % 8) + 128], q[:, h, :], ident[:])
                last.then_inc(qT_ps, 1)
                pe.wait_ge(qT_act, t + 1)
                pe.wait_ge(qT_dve, t + 1)
                pe.wait_ge(v_ready, t + 1)
                keys = 128 * (t + 1)

                def scores(h):
                    i = H_C * t + h
                    if h >= 2:
                        pe.wait_ge(p_ready, i - 1)
                    dst = ps[0][:, 512 * (i % 2):512 * (i % 2) + keys]
                    nc.tensor.matmul(dst, qT[:, h, :], kT[:, h, 0:keys], start=True, stop=False)
                    nc.tensor.matmul(dst[:, 128 * t:128 * t + 128], ident[:], causal[:], start=False, stop=True).then_inc(s_ps, 1)

                def turn(h):
                    i = H_C * t + h
                    pe.wait_ge(p_ready, i + 1)
                    if h >= 2:
                        pe.wait_ge(pT_ready, i - 1)
                    for b in range(t + 1):
                        last = nc.tensor.transpose(ps[1][:, 512 * (i % 2) + 128 * b:512 * (i % 2) + 128 * b + 128], prob[:, i % 2, 128 * b:128 * b + 128], ident[:])
                    last.then_inc(pT_ps, 1)

                def weighted(h):
                    i = H_C * t + h
                    pe.wait_ge(pT_ready, i + 1)
                    for b in range(t + 1):
                        last = nc.tensor.matmul(ps[2][:, 64 * h:64 * h + 64], probT[:, i % 2, 128 * b:128 * b + 128], v[:, b, 64 * h:64 * h + 64], start=(b == 0), stop=(b == t))
                    last.then_inc(o_ps, 1)

                scores(0)
                for h in range(H_C):
                    if h + 1 < H_C:
                        scores(h + 1)
                    turn(h)
                    if h:
                        weighted(h - 1)
                weighted(H_C - 1)
                pe.wait_ge(o_ready, t + 1)
                for k in range(KC):
                    last = nc.tensor.transpose(ps[3][:, 128 * k:128 * k + 128], o[:, 128 * k:128 * k + 128], ident[:])
                last.then_inc(oT_ps, 1)
                pe.wait_ge(oT_ready, t + 1)
                pe.wait_ge(wout_in, 16)
                for b in range(2):
                    for k in range(KC):
                        last = nc.tensor.matmul(ps[2][:, 512 * b:512 * b + 512], oT[:, k, :], w_out[:, k, 512 * b:512 * b + 512], start=(k == 0), stop=(k == KC - 1))
                last.then_inc(y_ps, 1)


def latent_sample(nc, w, ident, x_sb, smp):
    B, NQ = DEC_BATCH, 4
    with ExitStack() as ctx:
        def sb(name, shape, dt=F32):
            return ctx.enter_context(nc.sbuf_tensor("d_" + name, shape, dt))

        sem = signals(nc, ctx, "d_")

        w_ukT = sb("w_ukT", [128, H_C // 2, R_KV])
        w_uv = sb("w_uv", [128, 2, H_C * D_V])
        w_out = sb("w_out", [128, KC, D_MODEL])
        table = sb("table", [1, B * NP], I32)
        four = sb("four", [128, NQ])
        ones = sb("ones", [128, 128])
        pages = sb("pages", [128, 2, NP, R_KV])
        kpe = sb("kpe", [128, 2, NP, D_ROPE])
        qnT = sb("qnT", [128, H_C // 2, B])
        qlT = sb("qlT", [128, 2, B, H_C])
        qpT = sb("qpT", [128, B, NQ, H_C])
        qp_self = sb("qp_self", [32, B, H_C])
        kp_self = sb("kp_self", [32, B])
        self_s = sb("self_s", [1, B * H_C])
        self_row = sb("self_row", [1, B, R_KV])
        ckvT = sb("ckvT", [128, 2, NQ * 2 * 128])
        kpeT = sb("kpeT", [128, NP // NQ, 128])
        sc = sb("sc", [128, NP + 1, H_C])
        m1 = sb("m1", [128, H_C])
        mx = sb("mx", [H_C, 1])
        dmx = sb("dmx", [H_C, H_C])
        sums = sb("sums", [128, H_C])
        inv = sb("inv", [128, H_C])
        olT = sb("olT", [128, 2, H_C, B])
        oT = sb("oT", [128, KC, B])
        turn = [ctx.enter_context(nc.psum_tensor(f"d_turn{i}", [128, 1024], F32)) for i in range(2)]
        s_bank = ctx.enter_context(nc.psum_tensor("d_s", [128, 512], F32))
        m_bank = ctx.enter_context(nc.psum_tensor("d_m", [128, 512], F32))
        b_bank = ctx.enter_context(nc.psum_tensor("d_b", [128, 512], F32))
        o_bank = ctx.enter_context(nc.psum_tensor("d_o", [128, 512], F32))

        loaded, wout_in, table_in, consts = sem("loaded"), sem("wout_in"), sem("table_in"), sem("consts")
        pages_in = [sem("pages_in0"), sem("pages_in1")]
        qnT_ps, qnT_ready, ql_ps, ql_ready, qp_ps, qp_ready, self_ps, self_ready, row_in, kps_ready = (sem(n) for n in (
            "qnT_ps", "qnT_ready", "ql_ps", "ql_ready", "qp_ps", "qp_ready", "self_ps", "self_ready", "row_in", "kps_ready"))
        kpeT_ps, kpeT_ready, turn_ps, turn_act, turn_dve, turn_used, sc_ready = (sem(n) for n in (
            "kpeT_ps", "kpeT_ready", "turn_ps", "turn_act", "turn_dve", "turn_used", "sc_ready"))
        self_put, m1_ready, m1T_ps, mx_ready, dmx_ready, mb_ps, rel_ready, p_ready, sum_ready, sumb_ps, inv_ready, o_ps, o_used = (sem(n) for n in (
            "self_put", "m1_ready", "m1T_ps", "mx_ready", "dmx_ready", "mb_ps", "rel_ready", "p_ready", "sum_ready", "sumb_ps", "inv_ready", "o_ps", "o_used"))
        oT_ps, oT_ready, y_ps, y_used = sem("oT_ps"), sem("oT_ready"), sem("y_ps"), sem("y_used")
        block = ctx.enter_context(nc.Block())
        G = NP // NQ

        @block.sync
        def _(sp):
            sp.dma_start(table[:], w["page_table"].rearrange("b n -> (b n)").unsqueeze(0)).then_inc(table_in, 16)
            sp.wait_ge(table_in, 16)
            for b in range(B):
                if b >= 2:
                    sp.wait_ge(o_ps, b - 1)
                with sp.Fori(0, NP) as i:
                    page = sp.value_load(table[0:1, bass.ds(i + NP * b, 1)], min_val=0, max_val=w["cache_ckv"].shape[1] - 1)
                    sp.dma_start(pages[:, b % 2, bass.ds(i, 1), :], w["cache_ckv"][0, bass.ds(page, 1)].rearrange("a p r -> p a r")).then_inc(pages_in[b % 2], 16)
                    sp.dma_start(kpe[:, b % 2, bass.ds(i, 1), :], w["cache_kpe"][0, bass.ds(page, 1)].rearrange("a p r -> p a r")).then_inc(pages_in[b % 2], 16)

        @block.gpsimd
        def _(pool):
            pool.dma_start(self_row[:].rearrange("a b r -> a (b r)"), smp["ckv"][:]).then_inc(row_in, 16)
            nc.gpsimd.memset(ones[:], 1.0).then_inc(consts, 1)
            nc.gpsimd.memset(sc[:, NP, :], NEG_MASK).then_inc(consts, 1)

        @block.scalar
        def _(act):
            act.dma_start(w_ukT[:], w["w_ukT"]).then_inc(loaded, 16)
            act.dma_start(four[:], w["four"]).then_inc(loaded, 16)
            act.dma_start(w_uv[:], w["c_w_uv"][0].rearrange("(k p) h n -> p k (h n)", p=128)).then_inc(loaded, 16)
            act.dma_start(w_out[:], w["c_w_out"][0].rearrange("(k p) n -> p k n", p=128)).then_inc(wout_in, 16)
            nc.scalar.copy(kp_self[:], smp["kpeT"][64:96, :]).then_inc(kps_ready, 1)
            act.wait_ge(qnT_ps, 1)
            nc.scalar.copy(qnT[:].rearrange("p h b -> p (h b)"), m_bank[:, 0:64]).then_inc(qnT_ready, 1)
            act.wait_ge(ql_ps, 1)
            for odd in range(2):
                nc.scalar.copy(qlT[:].rearrange("p c b (a o) -> p o c a b", o=2)[:, odd], turn[0][:, 512 * odd:512 * odd + 128].rearrange("p (c a b) -> p c a b", c=2, a=8)).then_inc(ql_ready, 1)
            act.wait_ge(self_ps, 1)
            nc.scalar.copy(self_s[:], m_bank[0:1, 0:B * H_C]).then_inc(self_ready, 1)
            for b in range(B):
                act.wait_ge(kpeT_ps, b + 1)
                nc.scalar.copy(kpeT[:].rearrange("p g n -> p (g n)"), turn[0][:, :]).then_inc(kpeT_ready, 1)
                for g in range(1, G, 2):
                    i = b * G + g
                    act.wait_ge(turn_ps, i + 1)
                    if i >= 2:
                        act.wait_ge(turn_used, i - 1)
                    nc.scalar.copy(ckvT[:, i % 2, :], turn[1 - i % 2][:, :]).then_inc(turn_act, 1)
                act.wait_ge(rel_ready, b + 1)
                nc.scalar.activation(sc[:], sc[:], ACT.Exp, scale=MLA_SCALE).then_inc(p_ready, 1)
            act.wait_ge(oT_ps, 1)
            nc.scalar.copy(oT[:].rearrange("p k b -> p (k b)"), m_bank[:, 0:64]).then_inc(oT_ready, 1)

        @block.vector
        def _(dve):
            dve.wait_ge(loaded, 48)
            dve.wait_ge(qp_ps, 1)
            src = turn[1][:, 0:128].rearrange("p (h b) -> p b h", b=B)
            nc.vector.tensor_copy(qp_self[:], src[0:32]).then_inc(qp_ready, 1)
            nc.vector.tensor_tensor(qpT[:], bc(src.unsqueeze(2), [128, B, NQ, H_C]), bc(four[:].unsqueeze(1).unsqueeze(3), [128, B, NQ, H_C]), ALU.mult).then_inc(qp_ready, 1)
            dve.wait_ge(self_ready, 1)
            dve.wait_ge(consts, 2)
            for b in range(B):
                for g in range(0, G, 2):
                    i = b * G + g
                    dve.wait_ge(turn_ps, i + 1)
                    if i >= 2:
                        dve.wait_ge(turn_used, i - 1)
                    nc.vector.tensor_copy(ckvT[:, i % 2, :], turn[1 - i % 2][:, :]).then_inc(turn_dve, 1)
                dve.wait_ge(turn_used, G * (b + 1))
                if b:
                    dve.wait_ge(o_ps, b)
                nc.vector.tensor_copy(sc[:, 0:NP, :].rearrange("p g h -> p (g h)"), s_bank[:, :]).then_inc(sc_ready, 1)
                if b:
                    nc.vector.memset(sc[:, NP, :], NEG_MASK).then_inc(self_put, 1)
                    dve.wait_ge(self_put, 2 * b)
                nc.vector.tensor_copy(sc[0:1, NP, :], self_s[:, H_C * b:H_C * b + H_C]).then_inc(self_put, 1)
                dve.wait_ge(self_put, 2 * b + 1)
                dve.wait_ge(sc_ready, b + 1)
                nc.vector.tensor_reduce(m1[:], sc[:].rearrange("p g h -> p h g"), AX.X, ALU.max).then_inc(m1_ready, 1)
                dve.wait_ge(m1T_ps, b + 1)
                nc.vector.tensor_reduce(mx[:], m_bank[0:H_C, 0:128], AX.X, ALU.max).then_inc(mx_ready, 1)
                dve.wait_ge(mx_ready, b + 1)
                nc.vector.tensor_scalar(dmx[:], ident[0:H_C, 0:H_C], mx[:], None, ALU.mult).then_inc(dmx_ready, 1)
                dve.wait_ge(mb_ps, b + 1)
                nc.vector.tensor_tensor(sc[:], sc[:], bc(b_bank[:, 0:H_C].unsqueeze(1), [128, NP + 1, H_C]), ALU.subtract).then_inc(rel_ready, 1)
                dve.wait_ge(p_ready, b + 1)
                nc.vector.tensor_reduce(sums[:], sc[:].rearrange("p g h -> p h g"), AX.X, ALU.add).then_inc(sum_ready, 1)
                dve.wait_ge(sumb_ps, b + 1)
                nc.vector.reciprocal(inv[:], b_bank[:, H_C:2 * H_C]).then_inc(inv_ready, 1)
                dve.wait_ge(inv_ready, b + 1)
                dve.wait_ge(o_ps, b + 1)
                nc.vector.tensor_tensor(olT[:, :, :, b], o_bank[:, 0:2 * H_C].rearrange("p (c h) -> p c h", c=2), bc(inv[:].unsqueeze(1), [128, 2, H_C]), ALU.mult).then_inc(o_used, 1)
            dve.wait_ge(y_ps, 1)
            nc.vector.tensor_tensor(x_sb[0:B, NT, :], x_sb[0:B, NT, :], turn[0][0:B, :], ALU.add).then_inc(y_used, 1)

        @block.tensor
        def _(pe):
            qn = smp["qn"][:].rearrange("p h n -> p (h n)")
            for a in range(H_C // 2):
                last = nc.tensor.transpose(m_bank[:, 8 * a:8 * a + 8], qn[:, 128 * a:128 * a + 128], ident[0:B, 0:B])
            last.then_inc(qnT_ps, 1)
            for h in range(H_C):
                last = nc.tensor.transpose(turn[1][:, 8 * h:8 * h + 8], smp["qp"][:, h].rearrange("p a d -> p (a d)"), ident[0:B, 0:B])
            last.then_inc(qp_ps, 1)
            pe.wait_ge(qnT_ready, 1)
            pe.wait_ge(loaded, 48)
            for h in range(H_C):
                rows = slice(64 * (h % 2), 64 * (h % 2) + 64)
                for c in range(2):
                    at = 512 * (h % 2) + 64 * c + 8 * (h // 2)
                    last = nc.tensor.matmul(turn[0][:, at:at + 8], w_ukT[rows, h // 2, 128 * c:128 * c + 128], qnT[rows, h // 2, :], start=True, stop=True)
            last.then_inc(ql_ps, 1)
            pe.wait_ge(ql_ready, 2)
            pe.wait_ge(qp_ready, 2)
            pe.wait_ge(kps_ready, 1)
            for b in range(B):
                dst = m_bank[0:1, H_C * b:H_C * b + H_C]
                for c in range(2):
                    nc.tensor.matmul(dst, smp["ckvT"][:, c, b:b + 1], qlT[:, c, b, :], start=(c == 0), stop=False)
                last = nc.tensor.matmul(dst, kp_self[:, b:b + 1], qp_self[:, b, :], start=False, stop=True)
            last.then_inc(self_ps, 1)
            pe.wait_ge(self_ready, 1)
            pe.wait_ge(row_in, 16)
            pe.wait_ge(consts, 1)
            for b in range(B):
                pe.wait_ge(pages_in[b % 2], 16 * 2 * NP * (b // 2 + 1))

                def turn_pages(g):
                    i = b * G + g
                    if g >= 1 or b:
                        j = i - 2
                        if g == 1:
                            pe.wait_ge(kpeT_ready, b + 1)
                        if j >= 0:
                            pe.wait_ge(turn_act if j % 2 else turn_dve, j // 2 + 1)
                    for p in range(NQ):
                        for c in range(2):
                            last = nc.tensor.transpose(turn[1 - i % 2][:, 256 * p + 128 * c:256 * p + 128 * c + 128], pages[:, b % 2, NQ * g + p, 128 * c:128 * c + 128], ident[:])
                    last.then_inc(turn_ps, 1)

                def group_scores(g):
                    i = b * G + g
                    pe.wait_ge(turn_act if i % 2 else turn_dve, i // 2 + 1)
                    at = NQ * H_C * g
                    nc.tensor.matmul(s_bank[:, at:at + NQ * H_C], kpeT[:, g, :], qpT[:, b].rearrange("p a h -> p (a h)"), start=True, stop=False)
                    for p in range(NQ):
                        for c in range(2):
                            last = nc.tensor.matmul(s_bank[:, at + H_C * p:at + H_C * p + H_C], ckvT[:, i % 2, 256 * p + 128 * c:256 * p + 128 * c + 128], qlT[:, c, b, :],
                                                    start=False, stop=(c == 1 and p == NQ - 1))
                    last.then_inc(turn_used, 1)

                if b:
                    pe.wait_ge(turn_act, b * G // 2)
                for g in range(G):
                    last = nc.tensor.transpose(turn[0][:, 128 * g:128 * g + 128], kpe[:, b % 2, NQ * g:NQ * g + NQ, :].rearrange("p a d -> p (a d)"), ident[:])
                last.then_inc(kpeT_ps, 1)
                turn_pages(0)
                pe.wait_ge(kpeT_ready, b + 1)
                if b:
                    pe.wait_ge(sc_ready, b)
                for g in range(G):
                    if g + 1 < G:
                        turn_pages(g + 1)
                    group_scores(g)
                pe.wait_ge(m1_ready, b + 1)
                nc.tensor.transpose(m_bank[0:H_C, 0:128], m1[:], ident[:]).then_inc(m1T_ps, 1)
                pe.wait_ge(dmx_ready, b + 1)
                nc.tensor.matmul(b_bank[:, 0:H_C], ones[0:H_C, :], dmx[:], start=True, stop=True).then_inc(mb_ps, 1)
                pe.wait_ge(p_ready, b + 1)
                if b:
                    pe.wait_ge(o_used, b)
                for c in range(2):
                    for p in range(NP):
                        nc.tensor.matmul(o_bank[:, H_C * c:H_C * c + H_C], pages[:, b % 2, p, 128 * c:128 * c + 128], sc[:, p, :], start=(p == 0), stop=False)
                    last = nc.tensor.matmul(o_bank[:, H_C * c:H_C * c + H_C], self_row[:, b, 128 * c:128 * c + 128], sc[0:1, NP, :], start=False, stop=True)
                last.then_inc(o_ps, 1)
                pe.wait_ge(sum_ready, b + 1)
                nc.tensor.matmul(b_bank[:, H_C:2 * H_C], ones[:], sums[:], start=True, stop=True).then_inc(sumb_ps, 1)
            pe.wait_ge(o_used, B)
            for h in range(H_C):
                rows = slice(64 * (h % 2), 64 * (h % 2) + 64)
                for c in range(2):
                    last = nc.tensor.matmul(m_bank[rows, 8 * (h // 2):8 * (h // 2) + 8], w_uv[:, c, 64 * h:64 * h + 64], olT[:, c, h, :], start=(c == 0), stop=(c == 1))
            last.then_inc(oT_ps, 1)
            pe.wait_ge(oT_ready, 1)
            pe.wait_ge(wout_in, 16)
            for n in range(2):
                for k in range(KC):
                    last = nc.tensor.matmul(turn[0][0:B, 512 * n:512 * n + 512], oT[:, k, :], w_out[:, k, 512 * n:512 * n + 512], start=(k == 0), stop=(k == KC - 1))
            last.then_inc(y_ps, 1)


def sample_buffers(nc, ctx):
    def sb(name, shape):
        return ctx.enter_context(nc.sbuf_tensor("smp_" + name, shape, F32))

    return {"ckv": sb("ckv", [DEC_BATCH, R_KV]), "ckvT": sb("ckvT", [128, 2, DEC_BATCH]), "kpeT": sb("kpeT", [96, DEC_BATCH]),
            "qn": sb("qn", [DEC_BATCH, H_C, D_NOPE]), "qp": sb("qp", [DEC_BATCH, H_C, 4, D_ROPE])}


def final_norm(nc, w, out, x_sb):
    with ExitStack() as ctx:
        gain = ctx.enter_context(nc.sbuf_tensor("f_gain", [128, D_MODEL], F32))
        eps = ctx.enter_context(nc.sbuf_tensor("f_eps", [128, 1], F32))
        sq = ctx.enter_context(nc.sbuf_tensor("f_sq", [128, D_MODEL], F32))
        rstd = ctx.enter_context(nc.sbuf_tensor("f_rstd", [128, NT + 1], F32))
        sem = signals(nc, ctx, "f_")
        gain_in, eps_set, sq_ready, root_ready, inv_ready, y_ready, y_out = (sem(n) for n in (
            "gain_in", "eps_set", "sq_ready", "root_ready", "inv_ready", "y_ready", "y_out"))
        block = ctx.enter_context(nc.Block())

        @block.gpsimd
        def _(pool):
            nc.gpsimd.memset(eps[:], EPS).then_inc(eps_set, 1)

        @block.sync
        def _(sp):
            sp.dma_start(gain[:], w["final_norm"].unsqueeze(0).to_broadcast([128, D_MODEL])).then_inc(gain_in, 16)
            for t in range(NT + 1):
                sp.wait_ge(y_ready, t + 1)
                dst = out["y_prompt"][0, 128 * t:128 * t + 128, :] if t < NT else out["y_sample"][:, 0, :]
                sp.dma_start(dst, x_sb[0:rows_of(t), t, :]).then_inc(y_out, 16)
            sp.wait_ge(y_out, 16 * (NT + 1))

        @block.scalar
        def _(act):
            act.wait_ge(eps_set, 1)
            for t in range(NT + 1):
                n = rows_of(t)
                if t:
                    act.wait_ge(sq_ready, t)
                nc.scalar.activation(sq[0:n, :], x_sb[0:n, t, :], ACT.Square, scale=D_MODEL ** -0.5, accum_out=rstd[0:n, t:t + 1]).then_inc(sq_ready, 1)
                act.wait_ge(sq_ready, t + 1)
                nc.scalar.activation(rstd[0:n, t:t + 1], rstd[0:n, t:t + 1], ACT.Sqrt, bias=eps[0:n, :]).then_inc(root_ready, 1)

        @block.vector
        def _(dve):
            dve.wait_ge(gain_in, 16)
            for t in range(NT + 1):
                n = rows_of(t)
                dve.wait_ge(root_ready, t + 1)
                nc.vector.reciprocal(rstd[0:n, t:t + 1], rstd[0:n, t:t + 1]).then_inc(inv_ready, 1)
                dve.wait_ge(inv_ready, t + 1)
                nc.vector.scalar_tensor_tensor(out=x_sb[0:n, t, :], in0=x_sb[0:n, t, :], scalar=rstd[0:n, t:t + 1], in1=gain[0:n, :],
                                               op0=ALU.mult, op1=ALU.mult).then_inc(y_ready, 1)


def constants():
    p = np.arange(128)
    masks = np.zeros((128, LEVELS + 1, 128), np.int32)
    for l in range(LEVELS):
        hf = 64 >> l
        masks[:, l, :] = ((p[:, None] // (2 * hf) == p[None, :] // (2 * hf))
                          & (p[:, None] // hf % 2 == 0) & (p[None, :] // hf % 2 == 1))
    masks[:, LEVELS, :] = np.eye(128)
    pos = np.full((128, NT + 1), PAST_LEN, np.float32)
    pos[:, 0:NT] = 128 * np.arange(NT)[None, :] + p[:, None]
    inv = np.power(np.float32(ROPE_BASE), -np.arange(D_ROPE // 2, dtype=np.float32) / np.float32(D_ROPE // 2)).astype(np.float32)
    ang = (pos[:, :, None] * inv).astype(np.float32)
    cos, sin = np.cos(ang).astype(np.float32), np.sin(ang).astype(np.float32)
    return {"cos2": np.concatenate([cos, cos], axis=2), "sin2": np.concatenate([-sin, sin], axis=2),
            "causal": np.where(p[None, :] <= p[:, None], 0.0, NEG_MASK).astype(np.float32),
            "four": (p[:, None] // D_ROPE == np.arange(4)[None, :]).astype(np.float32),
            "ident": np.eye(128, dtype=np.float32), "level_masks": masks,
            "own_seq": np.eye(DEC_BATCH, dtype=np.float32),
            "iota16": np.tile(np.arange(TOPK, dtype=np.float32), (128, 1)),
            "spread": (p[None, :] // TOPK == np.arange(DEC_BATCH)[:, None]).astype(np.float32),
            "gatherT": (p[:, None] // TOPK == np.arange(DEC_BATCH)[None, :]).astype(np.float32),
            "own_k": (p[:, None] % TOPK == np.arange(TOPK)[None, :]).astype(np.float32)}


def laid_out(a):
    def cols(v):
        return np.ascontiguousarray(v.reshape(-1, 128).T)

    return {
        "ab_norm_cols": lambda: cols(a["ab_norm"][0]),
        "conv_w_cols": lambda: np.ascontiguousarray(a["conv_w"][0].reshape(CONV_W, 4, 128).transpose(2, 1, 0)),
        "chan_cols": lambda: np.ascontiguousarray(np.stack([cols(a[n][0]) for n in ("conv_b", "conv_ln_g", "conv_ln_b")], axis=1)),
        "gate_b_cols": lambda: cols(a["gla_b_gate"][0]),
        "c_norm_cols": lambda: cols(a["c_norm"][0]),
        "q_norm_cols": lambda: cols(a["c_q_norm"][0]),
        "w_ukT": lambda: np.ascontiguousarray(a["c_w_uk"][0].reshape(R_KV, H_C // 2, 128).transpose(2, 1, 0)),
        "keysT": lambda: np.ascontiguousarray(a["peer_keys"].transpose(0, 4, 1, 2, 3)).reshape(2, N_KEYS, -1),
        "peer_uv0": lambda: np.concatenate([a["peer_u"][0], a["peer_v"][0]], axis=1),
        "peer_uv1": lambda: np.concatenate([a["peer_u"][1], a["peer_v"][1]], axis=1),
        "state_conv_cols": lambda: np.ascontiguousarray(a["state_conv"][0].reshape(DEC_BATCH, PAD, 4, 128).transpose(3, 2, 0, 1)),
    }


def program(nc, w, out):
    with ExitStack() as ctx:
        ident = ctx.enter_context(nc.sbuf_tensor("ident", [128, 128], F32))
        x_sb = ctx.enter_context(nc.sbuf_tensor("x_sb", [128, NT + 1, D_MODEL], F32))
        x_in = ctx.enter_context(nc.semaphore("x_in"))
        with nc.Block() as block:
            @block.sync
            def _(sp):
                sp.dma_start(ident[:], w["ident"]).then_inc(x_in, 16)
                for t in range(NT):
                    sp.dma_start(x_sb[:, t, :], w["x_prompt"][0, 128 * t:128 * t + 128, :]).then_inc(x_in, 16)
                sp.dma_start(x_sb[0:DEC_BATCH, NT, :], w["x_sample"][:, 0, :]).then_inc(x_in, 16)
                sp.wait_ge(x_in, 16 * (NT + 2))
        even_layer(nc, w, out, ident, x_sb)
        peer_layer(nc, w, 0, ident, x_sb)
        with ExitStack() as odd:
            smp = sample_buffers(nc, odd)
            latent_projections(nc, w, out, ident, x_sb, smp)
            latent_sample(nc, w, ident, x_sb, smp)
        peer_layer(nc, w, 1, ident, x_sb)
        final_norm(nc, w, out, x_sb)


_USED = ['ab_norm_cols', 'ab_w_in', 'ab_w_out', 'c_kv_norm', 'c_norm_cols', 'c_w_in', 'c_w_out', 'c_w_q_b', 'c_w_uk', 'c_w_uv', 'cache_ckv', 'cache_kpe', 'causal', 'chan_cols', 'conv_w_cols', 'cos2', 'ffn_norm', 'final_norm', 'four', 'gate_b_cols', 'gatherT', 'gla_head_g', 'gla_w_gate', 'ident', 'iota16', 'keysT', 'level_masks', 'own_k', 'own_seq', 'page_table', 'peer_uv0', 'peer_uv1', 'peer_w_q', 'q_norm_cols', 'sin2', 'spread', 'state_conv', 'state_conv_cols', 'state_gla', 'w_ukT', 'x_prompt', 'x_sample']
_OUTS = {"y_prompt": (1, SEQ, D_MODEL), "y_sample": (DEC_BATCH, 1, D_MODEL),
         "new_ckv_prompt": (1, 1, SEQ, R_KV), "new_kpe_prompt": (1, 1, SEQ, D_ROPE),
         "new_ckv_sample": (1, DEC_BATCH, 1, R_KV), "new_kpe_sample": (1, DEC_BATCH, 1, D_ROPE),
         "new_conv_prompt": (1, 1, PAD, D_A), "new_conv_sample": (1, DEC_BATCH, PAD, D_A),
         "new_gla_prompt": (1, 1, H_B, DK_B, DV_B), "new_gla_sample": (1, DEC_BATCH, H_B, DK_B, DV_B)}


def kernel(**inputs):
    import concourse.bacc as _bacc
    from concourse import mybir as _mybir
    from concourse.bass_utils import run_bass_kernel_spmd as _run

    arrays = {name: np.ascontiguousarray(a) for name, a in inputs.items() if name in _USED}
    arrays.update((k, a) for k, a in constants().items() if k in _USED)
    arrays.update((k, f()) for k, f in laid_out({n: np.asarray(a) for n, a in inputs.items()}).items() if k in _USED)
    nc = _bacc.Bacc("TRN2", target_bir_lowering=False, num_devices=1)
    w = {n: nc.dram_tensor("in_" + n, a.shape, _mybir.dt.from_np(a.dtype), kind="ExternalInput").ap() for n, a in arrays.items()}
    out = {n: nc.dram_tensor("out_" + n, shape, F32, kind="ExternalOutput").ap() for n, shape in _OUTS.items()}
    program(nc, w, out)
    r = _run(nc, [{"in_" + n: a for n, a in arrays.items()}], core_ids=[0])
    return tuple(r.results[0]["out_" + n] for n in _OUTS)
```

```python
from contextlib import ExitStack

import numpy as np

import concourse.bass as bass
from concourse import mybir

F32 = mybir.dt.float32
I32 = mybir.dt.int32
U32 = mybir.dt.uint32
ALU = mybir.AluOpType
ACT = mybir.ActivationFunctionType
AX = mybir.AxisListType

D_MODEL, SEQ, DEC_BATCH, PAST_LEN, PAGE = 1024, 512, 8, 4096, 128
EPS = 1e-6
D_A, CONV_W, H_B, D_BV, D_BK, DK_B, DV_B, GATE_RANK = 512, 31, 4, 512, 256, 64, 128, 16
GATE_TAU = 16.0
D_IN_AB = 2 * D_A + 2 * D_BK + 2 * D_BV + GATE_RANK
H_C, D_NOPE, D_ROPE, D_V, R_Q, R_KV = 16, 64, 32, 64, 384, 256
D_IN_C = R_Q + R_KV + D_ROPE
ROPE_BASE = 10000.0
MLA_SCALE = (D_NOPE + D_ROPE) ** -0.5
H_P, N_KEYS, D_KEY, D_HALF, TOPK = 8, 128, 256, 128, 16
N_EXPERTS = N_KEYS * N_KEYS

KC = D_MODEL // 128
TOK = SEQ + DEC_BATCH
NT = SEQ // 128
PAD = CONV_W - 1
NEG_MASK = -1.0e30
LEVELS = 7
NP = PAST_LEN // PAGE


def rows_of(t):
    return 128 if t < NT else DEC_BATCH


def cols_of(t):
    return slice(128 * t, 128 * t + rows_of(t))


def bc(ap, shape):
    return ap.to_broadcast(shape)


def signals(nc, ctx, prefix):
    made = []

    def done():
        nc.clear_and_free_semaphores(made)
        nc.all_engine_barrier()

    def sem(name):
        made.append(nc.alloc_semaphore(prefix + name))
        return made[-1]

    ctx.callback(done)
    return sem


GLOW, K0, K1, Q0, Q1, L0, L1 = range(7)
JOB_COLS = {GLOW: 2 * D_A + 2 * D_BK + 2 * D_BV, K0: 2 * D_A + D_BK, K1: 2 * D_A + D_BK + 128,
            Q0: 2 * D_A, Q1: 2 * D_A + 128}
for _c in range(4):
    JOB_COLS[7 + 2 * _c] = D_A + 128 * _c
    JOB_COLS[8 + 2 * _c] = 128 * _c
N_JOBS = 15
W_IN_COLS = ((JOB_COLS[GLOW], D_IN_AB), (JOB_COLS[Q0], JOB_COLS[Q0] + 2 * D_BK), (0, 2 * D_A), (2 * D_A + 2 * D_BK, JOB_COLS[GLOW]))
GLU_SECOND, ROWS_FIRST = 11, 2
ON_DVE = [j in (L0, L1) or (j >= 8 and j % 2 == 0) for j in range(N_JOBS)]


def evacuated(j):
    return ON_DVE[j], sum(1 for i in range(j + 1) if ON_DVE[i] == ON_DVE[j])


def even_layer(nc, w, out, ident, x_sb):
    with ExitStack() as ctx:
        def sb(name, shape, dt=F32):
            return ctx.enter_context(nc.sbuf_tensor("a_" + name, shape, dt))

        sem = signals(nc, ctx, "a_")

        arena = sb("arena", [128, KC * D_IN_AB])
        w_in = arena[:, :].rearrange("p (k n) -> p k n", k=KC)
        w_out = arena[:, 0:KC * D_MODEL].rearrange("p (k n) -> p k n", k=KC)
        cursor = [KC * D_MODEL]

        def carve(*dims):
            n = int(np.prod(dims))
            ap = arena[:, cursor[0]:cursor[0] + n]
            cursor[0] += n
            names = "abcd"[:len(dims)]
            return ap.rearrange(f"p ({' '.join(names)}) -> p {' '.join(names)}", **dict(zip(names, dims))) if len(dims) > 1 else ap

        qE = carve(2, 2, SEQ)
        kE = carve(2, 2, SEQ)
        attn = carve(2, 2, 2, 2 * 128)
        qB = carve(2, SEQ)
        kD = carve(2, SEQ)
        kDT = carve(NT, 2, 128)
        state = carve(NT + 1, 2, DV_B)
        ln_inv = carve(TOK)
        assert cursor[0] <= KC * D_IN_AB

        norm_col = sb("norm_col", [128, KC])
        conv_wc = sb("conv_wc", [128, 4, CONV_W])
        chan = sb("chan", [128, 3, 4])
        w_gate = sb("w_gate", [GATE_RANK, D_BK])
        gate_b = sb("gate_b", [128, 2])
        head_gain = sb("head_gain", [128, DV_B])
        mean_w = sb("mean_w", [128, 128])
        ones = sb("ones", [128, 128])
        eps = sb("eps", [128, 1])
        masks = sb("masks", [128, LEVELS + 1, 128], I32)
        own_seq = sb("own_seq", [DEC_BATCH, DEC_BATCH])
        ms = sb("ms", [128, NT + 1])
        rstd = sb("rstd", [128, NT + 1])
        scratch = sb("scratch", [128, 4 * TOK])
        xs = scratch[:, 0:2 * D_MODEL].rearrange("p (b n) -> p b n", b=2)
        sig = scratch[:, 0:2 * TOK].rearrange("p (b n) -> p b n", b=2)
        absl = scratch[:, 2 * TOK:4 * TOK].rearrange("p (b n) -> p b n", b=2)
        dec = xs
        xT = sb("xT", [128, KC, TOK])
        u = sb("u", [128, 4, PAD + TOK])
        conv = sb("conv", [128, 4, TOK])
        qT = sb("qT", [128, 2, TOK])
        kT = sb("kT", [128, 2, TOK])
        glow = sb("glow", [GATE_RANK, TOK])
        la = sb("la", [128, 2, TOK])
        cum = sb("cum", [128, 2, SEQ])
        bend = sb("bend", [128, 2, NT])
        v = sb("v", [128, NT + 1, D_BV])
        r = sb("r", [128, NT + 1, D_BV])
        st_conv = sb("st_conv", [128, 4, DEC_BATCH, PAD])
        ubuf = sb("ubuf", [128, 4, DEC_BATCH, CONV_W])
        u_rows = sb("u_rows", [PAD, D_A])
        us_rows = sb("us_rows", [DEC_BATCH, D_A])
        hms = sb("hms", [128, NT + 1, H_B])
        hrs = sb("hrs", [128, NT + 1, H_B])
        k_rows = sb("k_rows", [DEC_BATCH, D_BK])
        s_smp = conv[:, :, :].rearrange("p a b -> p (a b)")[:, 0:2 * DEC_BATCH * DV_B].rearrange(
            "p (g b v) -> p g b v", g=2, b=DEC_BATCH)
        vblk = u[:, :, :].rearrange("p a b -> p (a b)")[0:DEC_BATCH, 0:2 * DEC_BATCH * DV_B].rearrange(
            "p (i b v) -> p i b v", i=2, b=DEC_BATCH)
        o_smp = sb("o_smp", [DEC_BATCH, H_B, DV_B])
        b_rows = sb("b_rows", [128, 2, D_BV])

        ps = [ctx.enter_context(nc.psum_tensor(f"a_ps{i}", [128, 1024], F32)) for i in range(4)]
        half = TOK // 2

        def pair(t, rows=128):
            return t[0:rows, :].rearrange("p (b n) -> p b n", b=2)[:, :, 0:half]

        def halves(ap):
            return ap.rearrange("p (b n) -> p b n", b=2)

        def by_head(t, c, h):
            at = 512 * (h % 2) + 256 * (c % 2) + 128 * (h // 2)
            return ps[t][:, at:at + 128]

        def o_heads(t, n=128):
            return ps[1 + 2 * (t % 2)][0:n, :].rearrange("p (b c a v) -> p c a b v", b=2, c=2, a=2)[:, 0]

        def kv_bank(c):
            return (ps[3] if c < 2 else ps[0])[:, 512 * (c % 2):512 * (c % 2) + 512]

        w_in_in = [sem("gates_in"), sem("qk_in"), sem("glu_in"), sem("vr_in")]
        w_out_in, small_in = sem("w_out_in"), sem("small_in")
        masks_in, state_in, stores = sem("masks_in"), sem("state_in"), sem("stores")
        consts, r_gained = sem("consts"), sem("r_gained")
        ms_ready, root_ready, xs_ready = sem("ms_ready"), sem("root_ready"), sem("xs_ready")
        xT_ps, xT_ready = sem("xT_ps"), sem("xT_ready")
        job_ps, job_act, job_dve = sem("job_ps"), sem("job_act"), sem("job_dve")
        row_ps, row_act = sem("row_ps"), sem("row_act")
        act_step, dve_step = sem("act_step"), sem("dve_step")
        log_ready, la_ready = sem("log_ready"), sem("la_ready")
        ubuf_ready, conv_ready = sem("ubuf_ready"), sem("conv_ready")
        mean_ps, xc_ready, sq_ready, var_ps = sem("mean_ps"), sem("xc_ready"), sem("sq_ready"), sem("var_ps")
        lnroot_ready, ln_ready, conv_out = sem("lnroot_ready"), sem("ln_ready"), sem("conv_out")
        tail_ps, tail_ready = sem("tail_ps"), sem("tail_ready")
        dec_ready, exp_ready, lev_ready, lev_ps, lev_used = (sem("dec_ready"), sem("exp_ready"), sem("lev_ready"),
                                                             sem("lev_ps"), sem("lev_used"))
        kdt_ps, kdt_ready, kv_ps, st_ready = sem("kdt_ps"), sem("kdt_ready"), sem("kv_ps"), sem("st_ready")
        o_ps, osq_ready, hms_ready, hroot_ready, b_ready, bT_ps, bT_ready = (
            sem("o_ps"), sem("osq_ready"), sem("hms_ready"), sem("hroot_ready"), sem("b_ready"), sem("bT_ps"), sem("bT_ready"))
        krow_ps, krow_ready, vblk_ready, skv_ps, skv_used, s_decayed, so_ps, so_used = (
            sem("krow_ps"), sem("krow_ready"), sem("vblk_ready"), sem("skv_ps"), sem("skv_used"), sem("s_decayed"),
            sem("so_ps"), sem("so_used"))
        y_ps, y_used, dve_lev, qk_dec = sem("y_ps"), sem("y_used"), sem("dve_lev"), sem("qk_dec")
        N_SMALL = 7

        block = ctx.enter_context(nc.Block())

        @block.sync
        def _(sp):
            for (lo, hi), arrived in zip(W_IN_COLS, w_in_in):
                for k in range(KC):
                    sp.dma_start(w_in[:, k, lo:hi], w["ab_w_in"][0, 128 * k:128 * k + 128, lo:hi]).then_inc(arrived, 16)
            sp.dma_start(masks[:], w["level_masks"]).then_inc(masks_in, 16)
            sp.wait_ge(row_ps, NT + 1)
            sp.dma_start(w_out, w["ab_w_out"][0].rearrange("(k p) n -> p k n", p=128)).then_inc(w_out_in, 16)
            sp.wait_ge(tail_ready, 2)
            sp.dma_start(out["new_conv_prompt"][0, 0], u_rows[:]).then_inc(stores, 16)
            sp.dma_start(out["new_conv_sample"][0, :, PAD - 1, :], us_rows[:]).then_inc(stores, 16)
            sp.dma_start(out["new_conv_sample"][0, :, 0:PAD - 1, :], w["state_conv"][0, :, 1:PAD, :]).then_inc(stores, 16)
            sp.wait_ge(st_ready, NT)
            for g in range(2):
                sp.dma_start(out["new_gla_prompt"][0, 0, 2 * g:2 * g + 2].rearrange("h k v -> (h k) v"),
                             state[:, NT, g, :]).then_inc(stores, 16)
            sp.wait_ge(skv_used, H_B)
            for g in range(2):
                sp.dma_start(out["new_gla_sample"][0, :, 2 * g:2 * g + 2].rearrange("b h k v -> (h k) b v"),
                             s_smp[:, g]).then_inc(stores, 16)
            sp.wait_ge(stores, 16 * 7)

        @block.gpsimd
        def _(pool):
            nc.gpsimd.memset(mean_w[:], 1.0 / D_A).then_inc(consts, 1)
            nc.gpsimd.memset(ones[:], 1.0).then_inc(consts, 1)
            nc.gpsimd.memset(eps[:], EPS).then_inc(consts, 1)
            nc.gpsimd.memset(u[:, :, 0:PAD], 0.0).then_inc(consts, 1)
            nc.gpsimd.memset(ms[:], 1.0).then_inc(consts, 1)
            pool.wait_ge(state_in, 16)
            nc.gpsimd.tensor_copy(ubuf[:, :, :, 0:PAD].rearrange("p c b t -> p (c b) t"), st_conv[:].rearrange("p c b t -> p (c b) t")).then_inc(ubuf_ready, 1)
            pool.wait_ge(row_ps, NT + 1)
            nc.gpsimd.memset(attn[:], 0.0).then_inc(consts, 1)
            pool.wait_ge(small_in, 16 * N_SMALL)
            for t in range(NT + 1):
                pool.wait_ge(row_act, 2 * (t + 1))
                n = rows_of(t)
                nc.gpsimd.tensor_tensor(r[0:n, t, :].rearrange("p (h v) -> p h v", h=H_B),
                                        r[0:n, t, :].rearrange("p (h v) -> p h v", h=H_B),
                                        bc(head_gain[0:n, :].unsqueeze(1), [n, H_B, DV_B]), ALU.mult).then_inc(r_gained, 1)

        @block.scalar
        def _(act):
            act.dma_start(norm_col[:], w["ab_norm_cols"]).then_inc(small_in, 16)
            act.dma_start(conv_wc[:], w["conv_w_cols"]).then_inc(small_in, 16)
            act.dma_start(chan[:], w["chan_cols"]).then_inc(small_in, 16)
            act.dma_start(w_gate[:], w["gla_w_gate"][0]).then_inc(small_in, 16)
            act.dma_start(gate_b[:], w["gate_b_cols"]).then_inc(small_in, 16)
            act.dma_start(head_gain[:], w["gla_head_g"].to_broadcast([128, DV_B])).then_inc(small_in, 16)
            act.dma_start(own_seq[:], w["own_seq"]).then_inc(small_in, 16)
            act.dma_start(st_conv[:], w["state_conv_cols"]).then_inc(state_in, 16)
            act.wait_ge(consts, 3)
            act.wait_ge(ms_ready, NT + 1)
            nc.scalar.activation(rstd[:], ms[:], ACT.Sqrt, bias=eps[:]).then_inc(root_ready, 1)
            def channel_out(j):
                if ON_DVE[j]:
                    return
                src = ps[j % 2]
                act.wait_ge(job_ps, j + 1)
                if j == GLOW:
                    ins = nc.scalar.copy(halves(glow[:]), pair(src, GATE_RANK))
                elif j in (K0, K1):
                    ins = nc.scalar.copy(halves(kT[:, j - K0, :]), pair(src))
                elif j in (Q0, Q1):
                    ins = nc.scalar.mul(halves(qT[:, j - Q0, :]), pair(src), DK_B ** -0.5)
                else:
                    c = (j - 7) // 2
                    if c == 0:
                        act.wait_ge(job_dve, 2)
                        nc.scalar.activation(absl, la[:], ACT.Abs).then_inc(act_step, 1)
                        act.wait_ge(act_step, 1)
                        nc.scalar.activation(absl, absl, ACT.Exp, scale=-1.0).then_inc(act_step, 1)
                        act.wait_ge(act_step, 2)
                        nc.scalar.activation(absl, absl, ACT.Ln, bias=1.0).then_inc(log_ready, 1)
                    if c >= 2:
                        act.wait_ge(job_dve, 2 + c - 1)
                    ins = nc.scalar.activation(halves(sig[:, c % 2, :]), pair(src), ACT.Sigmoid)
                ins.then_inc(job_act, 1)

            def rows_out(t):
                n = rows_of(t)
                act.wait_ge(row_ps, t + 1)
                nc.scalar.copy(v[0:n, t, :], ps[2 + t % 2][0:n, 0:512]).then_inc(row_act, 1)
                nc.scalar.activation(r[0:n, t, :], ps[2 + t % 2][0:n, 512:1024], ACT.Silu).then_inc(row_act, 1)

            for j in range(GLU_SECOND):
                channel_out(j)
            for t in range(ROWS_FIRST):
                rows_out(t)
            for j in range(GLU_SECOND, N_JOBS):
                channel_out(j)
            for t in range(ROWS_FIRST, NT + 1):
                rows_out(t)

            def level_exp(l):
                act.wait_ge(dec_ready, 2 * (l + 1))
                nc.scalar.activation(dec[:, l % 2, :], dec[:, l % 2, :], ACT.Exp).then_inc(exp_ready, 1)

            level_exp(0)
            level_exp(1)
            act.wait_ge(xc_ready, 1)
            nc.scalar.activation(xT[:, 0:4, :], conv[:], ACT.Square).then_inc(sq_ready, 1)
            act.wait_ge(var_ps, 1)
            nc.scalar.activation(halves(ln_inv), pair(ps[3]), ACT.Sqrt, bias=eps[:]).then_inc(lnroot_ready, 1)
            level_exp(2)
            act.wait_ge(ln_ready, 1)
            for c in range(4):
                nc.scalar.activation(xT[:, c, :], conv[:, c, :], ACT.Silu, scale=chan[:, 1, c:c + 1],
                                     bias=chan[:, 2, c:c + 1]).then_inc(conv_out, 1)
            act.wait_ge(conv_out, 4)
            for g in range(2):
                act.dma_start(s_smp[:, g], w["state_gla"][0, :, 2 * g:2 * g + 2].rearrange("b h k v -> (h k) b v")).then_inc(state_in, 16)
            act.wait_ge(tail_ps, 1)
            nc.scalar.copy(u_rows[:], ps[2][0:PAD, 0:512]).then_inc(tail_ready, 1)
            nc.scalar.copy(us_rows[:], ps[2][0:DEC_BATCH, 512:1024]).then_inc(tail_ready, 1)
            for l in range(3, LEVELS):
                level_exp(l)
            act.wait_ge(lev_ready, LEVELS)
            nc.scalar.activation(dec[:, 0, :], cum[:].rearrange("p g t -> p (g t)"), ACT.Exp).then_inc(exp_ready, 1)
            act.wait_ge(dec_ready, 2 * LEVELS + 1)
            nc.scalar.activation(dec[:, 1, :], dec[:, 1, :], ACT.Exp).then_inc(exp_ready, 1)
            nc.scalar.activation(bend[:], cum[:].rearrange("p g (c t) -> p g c t", c=NT)[:, :, :, 127], ACT.Exp).then_inc(exp_ready, 1)
            nc.scalar.activation(la[:, :, SEQ:TOK], la[:, :, SEQ:TOK], ACT.Exp).then_inc(exp_ready, 1)
            act.wait_ge(kdt_ps, 1)
            nc.scalar.copy(kDT[:].rearrange("p c g i -> p (c g i)"), ps[2][:, :]).then_inc(kdt_ready, 1)
            act.wait_ge(krow_ps, 1)
            nc.scalar.copy(k_rows[:], ps[2][0:DEC_BATCH, 0:D_BK]).then_inc(krow_ready, 1)
            for t in range(NT + 1):
                n = rows_of(t)
                if t < NT:
                    act.wait_ge(o_ps, t + 1)
                    src = o_heads(t)
                else:
                    act.wait_ge(so_used, H_B)
                    src = o_smp[:].rearrange("p (a b) v -> p a b v", b=2)
                if t >= 1:
                    act.wait_ge(hms_ready, t)
                nc.scalar.activation(dec[0:n, 0, 0:512].rearrange("p (a b v) -> p a b v", a=2, b=2), src, ACT.Square, scale=DV_B ** -0.5).then_inc(osq_ready, 1)
                act.wait_ge(hms_ready, t + 1)
                nc.scalar.activation(hrs[0:n, t, :], hms[0:n, t, :], ACT.Sqrt, bias=eps[0:n, :]).then_inc(hroot_ready, 1)
                act.wait_ge(bT_ps, t + 1)
                nc.scalar.copy(xT[:, 4:8, cols_of(t)], ps[2][:, 0:4 * n].rearrange("p (c n) -> p c n", c=4)).then_inc(bT_ready, 1)

        @block.vector
        def _(dve):
            steps = [0]

            def step(ins):
                steps[0] += 1
                ins.then_inc(dve_step, 1)
                dve.wait_ge(dve_step, steps[0])

            dve.wait_ge(consts, 5)
            for t in range(NT + 1):
                n = rows_of(t)
                nc.vector.tensor_tensor_reduce(u[0:n, 2 * (t % 2):2 * (t % 2) + 2, PAD:PAD + 512], x_sb[0:n, t, :].rearrange("p (a b) -> p a b", a=2),
                                               x_sb[0:n, t, :].rearrange("p (a b) -> p a b", a=2), 1.0 / D_MODEL, 0.0,
                                               ALU.mult, ALU.add, ms[0:n, t:t + 1]).then_inc(ms_ready, 1)
                dve.wait_ge(ms_ready, t + 1)
            dve.wait_ge(root_ready, 1)
            step(nc.vector.reciprocal(rstd[:], rstd[:]))
            dve.wait_ge(small_in, 16 * N_SMALL)

            def xT_out(t):
                n = rows_of(t)
                dve.wait_ge(xT_ps, t + 1)
                nc.vector.tensor_tensor(xT[:, :, cols_of(t)], ps[2 + t % 2][:, :].rearrange("p (k n) -> p k n", k=KC)[:, :, 0:n],
                                        bc(norm_col[:].unsqueeze(2), [128, KC, n]), ALU.mult).then_inc(xT_ready, 1)

            for t in range(NT + 1):
                n = rows_of(t)
                if t >= 2:
                    dve.wait_ge(xT_ps, t - 1)
                nc.vector.tensor_scalar(xs[0:n, t % 2, :], x_sb[0:n, t, :], rstd[0:n, t:t + 1], None, ALU.mult).then_inc(xs_ready, 1)
                if t:
                    xT_out(t - 1)
            xT_out(NT)
            for g in range(2):
                dve.wait_ge(job_ps, L0 + g + 1)
                nc.vector.tensor_scalar(halves(la[:, g, :]), pair(ps[(L0 + g) % 2]), gate_b[:, g:g + 1], None, ALU.add).then_inc(job_dve, 1)
            dve.wait_ge(log_ready, 1)
            step(nc.vector.scalar_tensor_tensor(out=la[:], in0=la[:], scalar=0.0, in1=absl, op0=ALU.min, op1=ALU.subtract))
            step(nc.vector.tensor_scalar(la[:], la[:], 1.0 / GATE_TAU, None, ALU.mult))
            for g in range(2):
                for c in range(NT):
                    last = nc.vector.tensor_tensor_scan(cum[:, g, 128 * c:128 * c + 128], ones[:], la[:, g, 128 * c:128 * c + 128],
                                                        0.0, ALU.mult, ALU.add)
                last.then_inc(la_ready, 1)
            for c0 in (0, 2):
                for c in (c0, c0 + 1):
                    dve.wait_ge(job_act, evacuated(7 + 2 * c)[1])
                    dve.wait_ge(job_ps, 8 + 2 * c + 1)
                    nc.vector.tensor_tensor(halves(u[:, c, PAD:PAD + TOK]), pair(ps[(8 + 2 * c) % 2]), halves(sig[:, c % 2, :]), ALU.mult).then_inc(job_dve, 1)
                dve.wait_ge(job_dve, 2 + c0 + 2)
                for tap in range(CONV_W):
                    for c in (c0, c0 + 1):
                        if tap == 0:
                            ins = nc.vector.tensor_scalar(conv[:, c, 0:SEQ], u[:, c, 0:SEQ], conv_wc[:, c, 0:1], chan[:, 0, c:c + 1], ALU.mult, ALU.add)
                        else:
                            dve.wait_ge(conv_ready, c0 * CONV_W + 2 * (tap - 1) + (c - c0) + 1)
                            ins = nc.vector.scalar_tensor_tensor(out=conv[:, c, 0:SEQ], in0=u[:, c, tap:tap + SEQ], scalar=conv_wc[:, c, tap:tap + 1],
                                                                 in1=conv[:, c, 0:SEQ], op0=ALU.mult, op1=ALU.add)
                        ins.then_inc(conv_ready, 1)
            dve.wait_ge(ubuf_ready, 1)
            step(nc.vector.tensor_copy(ubuf[:, :, :, PAD], u[:, :, PAD + SEQ:PAD + TOK]))
            for c in range(4):
                last = nc.vector.tensor_tensor(ubuf[:, c], ubuf[:, c], bc(conv_wc[:, c, :].unsqueeze(1), [128, DEC_BATCH, CONV_W]), ALU.mult)
            step(last)
            step(nc.vector.tensor_reduce(conv[:, :, SEQ:TOK], ubuf[:], AX.X, ALU.add))
            nc.vector.tensor_tensor(conv[:, :, SEQ:TOK], conv[:, :, SEQ:TOK], bc(chan[:, 0, :].unsqueeze(2), [128, 4, DEC_BATCH]), ALU.add).then_inc(conv_ready, 1)
            dve.wait_ge(conv_ready, 4 * CONV_W + 1)
            dve.wait_ge(masks_in, 16)
            dve.wait_ge(consts, 6)
            qk = (qT[:, :, 0:SEQ], kT[:, :, 0:SEQ])
            dve.wait_ge(job_act, evacuated(Q1)[1])

            def level_decay(l):
                hf = 64 >> l
                b4 = cum[:].rearrange("p g (n s) -> p (g n) s", s=2 * hf)
                d4 = dec[:, l % 2, :].rearrange("p (n s) -> p n s", s=2 * hf)
                edge = bc(b4[:, :, hf - 1:hf], [128, SEQ // hf, hf])
                if l >= 2:
                    dve.wait_ge(lev_ready, l - 1)
                nc.vector.tensor_tensor(d4[:, :, hf:], b4[:, :, hf:], edge, ALU.subtract).then_inc(dec_ready, 1)
                nc.vector.tensor_tensor(d4[:, :, 0:hf], edge, b4[:, :, 0:hf], ALU.subtract).then_inc(dec_ready, 1)

            def level_scale(l):
                dve.wait_ge(exp_ready, l + 1)
                if l >= 2:
                    dve.wait_ge(lev_ps, 2 * (l - 1))
                d3 = dec[:, l % 2, :].rearrange("p (g t) -> p g t", g=2)
                nc.vector.tensor_tensor(qE[:, l % 2], qk[0], d3, ALU.mult).then_inc(dve_lev, 1)
                nc.vector.tensor_tensor(kE[:, l % 2], qk[1], d3, ALU.mult).then_inc(lev_ready, 1)

            def level_keep(l):
                for cp in range(2):
                    i = 2 * l + cp
                    dve.wait_ge(lev_ps, i + 1)
                    if l:
                        dve.wait_ge(lev_used, i - 1)
                    nc.vector.copy_predicated(attn[:, cp].rearrange("p b c n -> p (b c n)").rearrange("p (n i) -> p n i", i=128),
                                              bc(masks[:, l, :].unsqueeze(1), [128, 8, 128]),
                                              ps[i % 2][:, :].rearrange("p (n i) -> p n i", i=128)).then_inc(lev_used, 1)

            dve.wait_ge(la_ready, 2)
            level_decay(0)
            level_decay(1)
            dve.wait_ge(mean_ps, 1)
            for c in range(4):
                last = nc.vector.tensor_tensor(halves(conv[:, c, :]), halves(conv[:, c, :]), pair(ps[2]), ALU.subtract)
            last.then_inc(xc_ready, 1)
            for l in range(LEVELS):
                if 1 <= l < LEVELS - 1:
                    level_decay(l + 1)
                level_scale(l)
                if l:
                    level_keep(l - 1)
                if l == 1:
                    dve.wait_ge(lnroot_ready, 1)
                    step(nc.vector.reciprocal(ln_inv, ln_inv))
                    dve.wait_ge(xc_ready, 1)
                    nc.vector.tensor_tensor(conv[:], conv[:], bc(ln_inv.unsqueeze(1), [128, 4, TOK]), ALU.mult).then_inc(ln_ready, 1)
            level_keep(LEVELS - 1)
            level_keep(LEVELS)
            c4 = cum[:].rearrange("p g (c t) -> p (g c) t", c=NT)
            nc.vector.tensor_tensor(dec[:, 1, :].rearrange("p (n t) -> p n t", t=128), bc(c4[:, :, 127:128], [128, 2 * NT, 128]), c4, ALU.subtract).then_inc(dec_ready, 1)
            dve.wait_ge(exp_ready, LEVELS + 4)
            nc.vector.tensor_tensor(qB, qk[0], dec[:, 0, :].rearrange("p (g t) -> p g t", g=2), ALU.mult).then_inc(qk_dec, 1)
            nc.vector.tensor_tensor(kD, qk[1], dec[:, 1, :].rearrange("p (g t) -> p g t", g=2), ALU.mult).then_inc(qk_dec, 1)
            for c in range(NT):
                dve.wait_ge(kv_ps, c + 1)
                if c:
                    dve.wait_ge(st_ready, c)
                for g in range(2):
                    for h in range(2):
                        rows = slice(64 * h, 64 * h + 64)
                        src = kv_bank(c)[rows, 256 * g + 128 * h:256 * g + 128 * h + 128]
                        if c == 0:
                            last = nc.vector.tensor_copy(state[rows, 1, g, :], src)
                        else:
                            last = nc.vector.scalar_tensor_tensor(out=state[rows, c + 1, g, :], in0=state[rows, c, g, :], scalar=bend[rows, g, c:c + 1],
                                                                  in1=src, op0=ALU.mult, op1=ALU.add)
                last.then_inc(st_ready, 1)

            def head_norm(t):
                n = rows_of(t)
                src = o_heads(t) if t < NT else o_smp[:].rearrange("p (a b) v -> p a b v", b=2)
                dve.wait_ge(osq_ready, t + 1)
                nc.vector.tensor_reduce(hms[0:n, t, :], dec[0:n, 0, 0:512].rearrange("p (h v) -> p h v", h=H_B), AX.X, ALU.add).then_inc(hms_ready, 1)
                dve.wait_ge(hroot_ready, t + 1)
                step(nc.vector.reciprocal(hrs[0:n, t, :], hrs[0:n, t, :]))
                if t >= 2:
                    dve.wait_ge(bT_ps, t - 1)
                dst = b_rows[0:n, t % 2, :].rearrange("p (a b v) -> p a b v", a=2, b=2)
                step(nc.vector.tensor_tensor(dst, src, bc(hrs[0:n, t, :].rearrange("p (a b) -> p a b", b=2).unsqueeze(3), [n, 2, 2, DV_B]), ALU.mult))
                dve.wait_ge(r_gained, t + 1)
                nc.vector.tensor_tensor(b_rows[0:n, t % 2, :], b_rows[0:n, t % 2, :], r[0:n, t, :], ALU.mult).then_inc(b_ready, 1)

            for t in range(NT):
                head_norm(t)
            dve.wait_ge(state_in, 48)
            dve.wait_ge(tail_ps, 1)
            for g in range(2):
                nc.vector.tensor_tensor(s_smp[:, g], s_smp[:, g], bc(la[:, g, SEQ:TOK].unsqueeze(2), [128, DEC_BATCH, DV_B]), ALU.mult).then_inc(s_decayed, 1)

            def v_block(h):
                if h >= 2:
                    dve.wait_ge(skv_ps, h - 1)
                nc.vector.tensor_tensor(vblk[:, h % 2], bc(v[0:DEC_BATCH, NT, DV_B * h:DV_B * h + DV_B].unsqueeze(1), [DEC_BATCH, DEC_BATCH, DV_B]),
                                        bc(own_seq[:].unsqueeze(2), [DEC_BATCH, DEC_BATCH, DV_B]), ALU.mult).then_inc(vblk_ready, 1)

            v_block(0)
            v_block(1)
            for h in range(H_B):
                rows = slice(64 * (h % 2), 64 * (h % 2) + 64)
                dve.wait_ge(skv_ps, h + 1)
                dve.wait_ge(s_decayed, 2)
                nc.vector.tensor_tensor(s_smp[rows, h // 2], s_smp[rows, h // 2], ps[0][rows, :].rearrange("p (b v) -> p b v", b=DEC_BATCH), ALU.add).then_inc(skv_used, 1)
                if h + 2 < H_B:
                    v_block(h + 2)
            for h in range(H_B):
                dve.wait_ge(so_ps, h + 1)
                step(nc.vector.tensor_tensor(vblk[:, 0], ps[3][0:DEC_BATCH, :].rearrange("p (b v) -> p b v", b=DEC_BATCH),
                                             bc(own_seq[:].unsqueeze(2), [DEC_BATCH, DEC_BATCH, DV_B]), ALU.mult))
                nc.vector.tensor_reduce(o_smp[:, h, :], vblk[:, 0].rearrange("p b v -> p v b"), AX.X, ALU.add).then_inc(so_used, 1)
                dve.wait_ge(so_used, h + 1)
            head_norm(NT)
            for t in range(NT + 1):
                n = rows_of(t)
                dve.wait_ge(y_ps, t + 1)
                nc.vector.tensor_tensor(x_sb[0:n, t, :], x_sb[0:n, t, :], ps[t % 2][0:n, :], ALU.add).then_inc(y_used, 1)

        @block.tensor
        def _(pe):
            for t in range(NT + 1):
                n = rows_of(t)
                pe.wait_ge(xs_ready, t + 1)
                if t >= 2:
                    pe.wait_ge(xT_ready, t - 1)
                for k in range(KC):
                    last = nc.tensor.transpose(ps[2 + t % 2][:, 128 * k:128 * k + n], xs[0:n, t % 2, 128 * k:128 * k + 128], ident[0:n, 0:n])
                last.then_inc(xT_ps, 1)
            pe.wait_ge(xT_ready, NT + 1)

            def channel_job(j):
                if j in (GLOW, K0, 7):
                    pe.wait_ge(w_in_in[(GLOW, K0, 7).index(j)], 16 * KC)
                if j >= 2:
                    on_dve, n = evacuated(j - 2)
                    pe.wait_ge(job_dve if on_dve else job_act, n)
                rows = GATE_RANK if j == GLOW else 128
                if j in (L0, L1):
                    pe.wait_ge(job_act, evacuated(GLOW)[1])
                for b in range(2):
                    dst = ps[j % 2][0:rows, 512 * b:512 * b + half]
                    if j in (L0, L1):
                        last = nc.tensor.matmul(dst, w_gate[:, 128 * (j - L0):128 * (j - L0) + 128], glow[:, half * b:half * b + half], start=True, stop=True)
                        continue
                    for k in range(KC):
                        last = nc.tensor.matmul(dst, w_in[:, k, JOB_COLS[j]:JOB_COLS[j] + rows], xT[:, k, half * b:half * b + half],
                                                start=(k == 0), stop=(k == KC - 1))
                last.then_inc(job_ps, 1)
            V_COL = 2 * D_A + 2 * D_BK

            def rows_job(t):
                n = rows_of(t)
                if t == 0:
                    pe.wait_ge(w_in_in[3], 16 * KC)
                if t >= 2:
                    pe.wait_ge(row_act, 2 * (t - 1))
                for b in range(2):
                    for k in range(KC):
                        last = nc.tensor.matmul(ps[2 + t % 2][0:n, 512 * b:512 * b + 512], xT[:, k, cols_of(t)],
                                                w_in[:, k, V_COL + 512 * b:V_COL + 512 * b + 512], start=(k == 0), stop=(k == KC - 1))
                last.then_inc(row_ps, 1)

            for j in range(GLU_SECOND):
                channel_job(j)
            for t in range(ROWS_FIRST):
                rows_job(t)
            for j in range(GLU_SECOND, N_JOBS):
                channel_job(j)
            for t in range(ROWS_FIRST, NT + 1):
                rows_job(t)
            pe.wait_ge(row_act, 2 * (NT + 1))
            pe.wait_ge(conv_ready, 4 * CONV_W + 1)
            for b in range(2):
                for c in range(4):
                    last = nc.tensor.matmul(ps[2][:, 512 * b:512 * b + half], mean_w[:], conv[:, c, half * b:half * b + half], start=(c == 0), stop=(c == 3))
            last.then_inc(mean_ps, 1)
            pe.wait_ge(job_dve, evacuated(14)[1])
            pe.wait_ge(job_act, evacuated(13)[1])

            def variance():
                pe.wait_ge(sq_ready, 1)
                for b in range(2):
                    for c in range(4):
                        last = nc.tensor.matmul(ps[3][:, 512 * b:512 * b + half], mean_w[:], xT[:, c, half * b:half * b + half], start=(c == 0), stop=(c == 3))
                last.then_inc(var_ps, 1)

            def last_rows():
                pe.wait_ge(xc_ready, 1)
                for c in range(4):
                    nc.tensor.transpose(ps[2][0:PAD, 128 * c:128 * c + 128], u[:, c, SEQ:SEQ + PAD], ident[:])
                    last = nc.tensor.transpose(ps[2][0:DEC_BATCH, 512 + 128 * c:512 + 128 * c + 128], u[:, c, PAD + SEQ:PAD + TOK], ident[:])
                last.then_inc(tail_ps, 1)

            for l in range(LEVELS + 1):
                if l < LEVELS:
                    pe.wait_ge(lev_ready, l + 1)
                    pe.wait_ge(dve_lev, l + 1)
                    q_, k_ = qE[:, l % 2], kE[:, l % 2]
                else:
                    q_, k_ = qT, kT
                for cp in range(2):
                    i = 2 * l + cp
                    if i >= 2:
                        pe.wait_ge(lev_used, i - 1)
                    for c in (2 * cp, 2 * cp + 1):
                        for h in range(H_B):
                            rows = slice(64 * (h % 2), 64 * (h % 2) + 64)
                            last = nc.tensor.matmul(by_head(i % 2, c, h), k_[rows, h // 2, 128 * c:128 * c + 128],
                                                    q_[rows, h // 2, 128 * c:128 * c + 128], start=True, stop=True)
                    last.then_inc(lev_ps, 1)
                if l == 0:
                    variance()
                if l == 1:
                    last_rows()
            pe.wait_ge(tail_ready, 2)
            pe.wait_ge(qk_dec, 2)
            pe.wait_ge(row_act, 2 * (NT + 1))
            for c in range(NT):
                for g in range(2):
                    last = nc.tensor.transpose(ps[2][:, 256 * c + 128 * g:256 * c + 128 * g + 128], kD[:, g, 128 * c:128 * c + 128], ident[:])
            last.then_inc(kdt_ps, 1)
            pe.wait_ge(kdt_ready, 1)
            for g in range(2):
                last = nc.tensor.transpose(ps[2][0:DEC_BATCH, 128 * g:128 * g + 128], kT[:, g, SEQ:TOK], ident[:])
            last.then_inc(krow_ps, 1)
            pe.wait_ge(lev_used, 2 * (LEVELS + 1))
            for c in range(NT):
                for g in range(2):
                    last = nc.tensor.matmul(kv_bank(c)[:, 256 * g:256 * g + 256], kDT[:, c, g, :], v[:, c, 256 * g:256 * g + 256], start=True, stop=True)
                last.then_inc(kv_ps, 1)

            def b_transposed(t):
                n = rows_of(t)
                pe.wait_ge(b_ready, t + 1)
                if t:
                    pe.wait_ge(bT_ready, t)
                else:
                    pe.wait_ge(krow_ready, 1)
                for c in range(4):
                    last = nc.tensor.transpose(ps[2][:, n * c:n * c + n], b_rows[0:n, t % 2, 128 * c:128 * c + 128], ident[0:n, 0:n])
                last.then_inc(bT_ps, 1)

            for t in range(NT):
                if t:
                    pe.wait_ge(st_ready, max(t, 2))
                if t >= 2:
                    pe.wait_ge(b_ready, t - 1)
                for h in range(H_B):
                    rows = slice(64 * (h % 2), 64 * (h % 2) + 64)
                    dst = by_head(1 + 2 * (t % 2), 0, h)
                    last = nc.tensor.matmul(dst, attn[:, t // 2, h % 2, t % 2, 128 * (h // 2):128 * (h // 2) + 128], v[:, t, 128 * h:128 * h + 128], start=True, stop=(t == 0))
                    if t:
                        last = nc.tensor.matmul(dst, qB[rows, h // 2, 128 * t:128 * t + 128], state[rows, t, h // 2, :], start=False, stop=True)
                last.then_inc(o_ps, 1)
                if t:
                    b_transposed(t - 1)
            b_transposed(NT - 1)
            pe.wait_ge(krow_ready, 1)
            pe.wait_ge(st_ready, NT)
            for h in range(H_B):
                rows = slice(64 * (h % 2), 64 * (h % 2) + 64)
                pe.wait_ge(vblk_ready, h + 1)
                if h:
                    pe.wait_ge(skv_used, h)
                for b in range(2):
                    last = nc.tensor.matmul(ps[0][rows, 512 * b:512 * b + 512], k_rows[:, 64 * h:64 * h + 64],
                                            vblk[:, h % 2, 4 * b:4 * b + 4, :].rearrange("p b v -> p (b v)"), start=True, stop=True)
                last.then_inc(skv_ps, 1)
            pe.wait_ge(skv_used, H_B)
            for h in range(H_B):
                rows = slice(64 * (h % 2), 64 * (h % 2) + 64)
                if h:
                    pe.wait_ge(so_used, h)
                for b in range(2):
                    last = nc.tensor.matmul(ps[3][0:DEC_BATCH, 512 * b:512 * b + 512], qT[rows, h // 2, SEQ:TOK],
                                            s_smp[rows, h // 2, 4 * b:4 * b + 4, :].rearrange("p b v -> p (b v)"), start=True, stop=True)
                last.then_inc(so_ps, 1)
            b_transposed(NT)
            pe.wait_ge(w_out_in, 16)
            pe.wait_ge(conv_out, 4)
            pe.wait_ge(bT_ready, NT + 1)
            for t in range(NT + 1):
                n = rows_of(t)
                if t >= 2:
                    pe.wait_ge(y_used, t - 1)
                for b in range(2):
                    for k in range(KC):
                        last = nc.tensor.matmul(ps[t % 2][0:n, 512 * b:512 * b + 512], xT[:, k, cols_of(t)], w_out[:, k, 512 * b:512 * b + 512],
                                                start=(k == 0), stop=(k == KC - 1))
                last.then_inc(y_ps, 1)


RING = 8
GROUP = 2
GROUPS = TOPK // GROUP
NEG = -3.0e38


def peer_layer(nc, w, layer, ident, x_sb):
    with ExitStack() as ctx:
        def sb(name, shape, dt=F32):
            return ctx.enter_context(nc.sbuf_tensor(f"p{layer}_{name}", shape, dt))

        def psum(name, shape):
            return ctx.enter_context(nc.psum_tensor(f"p{layer}_{name}", shape, F32))

        sem = signals(nc, ctx, f"p{layer}_")

        rows = sb("rows", [128, RING, 2 * D_MODEL])
        w_q = sb("w_q", [128, KC, H_P * D_KEY])
        keysT = sb("keysT", [128, 2 * H_P * N_KEYS])
        gain = sb("gain", [128, D_MODEL])
        zero = sb("zero", [128, 128])
        eps = sb("eps", [128, 1])
        iota16 = sb("iota16", [128, TOPK])
        spread = sb("spread", [DEC_BATCH, 128])
        gatherT = sb("gatherT", [128, DEC_BATCH])
        own_k = sb("own_k", [128, TOPK])
        x_cur = sb("x_cur", [128, D_MODEL])
        x_next = sb("x_next", [128, D_MODEL])
        xT = sb("xT", [128, KC, 128])
        xT_first = sb("xT_first", [128, KC, 128])
        sq = sb("sq", [128, D_MODEL])
        rstd = sb("rstd", [128, 1])
        qT = sb("qT", [128, 2, 128])
        q_rows = sb("q_rows", [128, D_KEY])
        s = sb("s", [128, 2, N_KEYS])
        s2 = sb("s2", [128, 2, N_KEYS])
        top = sb("top", [128, 2, TOPK])
        topi = sb("topi", [128, 2, TOPK], U32)
        topf = sb("topf", [128, 2, TOPK])
        cand = sb("cand", [128, TOPK, TOPK])
        cand2 = sb("cand2", [128, TOPK, TOPK])
        best = sb("best", [128, TOPK])
        besti = sb("besti", [128, TOPK], U32)
        split = sb("split", [128, 2, TOPK], U32)
        splitf = sb("splitf", [128, 2, TOPK])
        hit = sb("hit", [128, 2, TOPK, TOPK])
        sel = sb("sel", [128, 2, TOPK])
        rel = sb("rel", [128, TOPK])
        ex = sb("ex", [128, TOPK])
        ex_sum = sb("ex_sum", [128, 1])
        ex_inv = sb("ex_inv", [128, 1])
        ids = sb("ids", [128, NT * H_P * TOPK], U32)
        gates = sb("gates", [128, NT * H_P * TOPK])
        smp = sb("smp", [DEC_BATCH, 2, H_P * TOPK])
        smp_hit = sb("smp_hit", [128, 2 * H_P, TOPK])
        smp_own = sb("smp_own", [128, 2 * H_P])
        ids_lo = sb("ids_lo", [128, TOPK // 2], U32)
        ids_hi = sb("ids_hi", [128, TOPK // 2], U32)
        gate = sb("gate", [128, TOPK])
        dots = sb("dots", [128, 4, GROUP])
        acts = sb("acts", [128, 4, GROUP])
        diag = sb("diag", [128, 4, GROUP, 128])

        acc = psum("acc", [128, D_MODEL])
        turn = psum("turn", [128, D_MODEL])
        q_bank = psum("q_bank", [128, 512])
        s_bank = psum("s_bank", [128, 512])

        loaded, w_q_first, w_q_in, zeroed = sem("loaded"), sem("w_q_first"), sem("w_q_in"), sem("zeroed")
        sq_ready, root_ready, xn_ready, xT_ps, xT_ready, xcur_ready = (sem("sq_ready"), sem("root_ready"), sem("xn_ready"), sem("xT_ps"), sem("xT_ready"), sem("xcur_ready"))
        q_ps, q_ready, s_ps, s_ready, routed, rel_ready, ex_ready = (sem("q_ps"), sem("q_ready"), sem("s_ps"), sem("s_ready"), sem("routed"), sem("rel_ready"), sem("ex_ready"))
        qT_ps, qT_ready, looked = sem("qT_ps"), sem("qT_ready"), sem("looked")
        rt, inv_ready, gates_ready, gate_copied = sem("rt"), sem("inv_ready"), sem("gates_ready"), sem("gate_copied")
        lo_ready, hi_ready, paced = sem("lo_ready"), sem("hi_ready"), sem("paced")
        paced_dve, paced_pe, paced_act = sem("paced_dve"), sem("paced_pe"), sem("paced_act")
        rows_in = [sem(f"rows_in{i}") for i in range(RING)]
        dotted, gelud, diag_ready, rows_used, acc_ready, acc_used = (sem("dotted"), sem("gelud"), sem("diag_ready"), sem("rows_used"), sem("acc_ready"), sem("acc_used"))
        spread_ps, smp_step = sem("spread_ps"), sem("smp_step")
        N_LOADED = 16 * 6
        R_STEPS = 18

        block = ctx.enter_context(nc.Block())

        @block.sync
        def _(sp):
            sp.dma_start(gain[:], w["ffn_norm"][layer:layer + 1, :].to_broadcast([128, D_MODEL])).then_inc(loaded, 16)
            sp.dma_start(iota16[:], w["iota16"]).then_inc(loaded, 16)
            sp.dma_start(spread[:], w["spread"]).then_inc(loaded, 16)
            sp.dma_start(gatherT[:], w["gatherT"]).then_inc(loaded, 16)
            sp.dma_start(own_k[:], w["own_k"]).then_inc(loaded, 16)
            sp.dma_start(keysT[:], w["keysT"][layer]).then_inc(loaded, 16)
            for heads, arrived in (((0, 1), w_q_first), ((1, H_P), w_q_in)):
                cols = slice(D_KEY * heads[0], D_KEY * heads[1])
                for k in range(KC):
                    sp.dma_start(w_q[:, k, cols], w["peer_w_q"][layer, 128 * k:128 * k + 128, cols]).then_inc(arrived, 16)

        @block.gpsimd
        def _(pool):
            nc.gpsimd.memset(zero[:], 0.0).then_inc(zeroed, 1)
            nc.gpsimd.memset(eps[:], EPS).then_inc(zeroed, 1)

            def gather(k, table_ids):
                nc.gpsimd.indirect_dma_start(out=rows[:, k % RING, :], out_offset=None, in_=w[f"peer_uv{layer}"],
                                             in_offset=bass.IndirectOffsetOnAxis(ap=table_ids[:, k % 8:k % 8 + 1], axis=0)
                                             ).then_inc(rows_in[k % RING], 16)

            def slot_free(n, k):
                pool.wait_ge(rows_used, n * TOPK + k - RING + 1)
                pool.sem_inc(paced, 1)

            pool.wait_ge(lo_ready, 1)
            for k in range(TOPK):
                if k == 8:
                    pool.wait_ge(hi_ready, 1)
                if k >= RING:
                    pool.wait_ge(rows_used, k - RING + 1)
                gather(k, ids_lo if k < 8 else ids_hi)
            with pool.Fori(1, NT * H_P) as n:
                for k in range(TOPK):
                    if k % 8 == 0:
                        pool.wait_ge(lo_ready if k == 0 else hi_ready, n + 1)
                        pool.sem_inc(paced, 1)
                    slot_free(n, k)
                    gather(k, ids_lo if k < 8 else ids_hi)
            pool.wait_ge(lo_ready, NT * H_P + 1)
            for k in range(H_P):
                pool.wait_ge(rows_used, NT * H_P * TOPK + k - RING + 1)
                gather(k, ids_lo)

        @block.scalar
        def _(act):
            def prepare(t, first=False):
                n = rows_of(t) if isinstance(t, int) else 128
                if not first:
                    act.wait_ge(xn_ready, t)
                    act.sem_inc(paced_act, 1)
                nc.scalar.activation(sq[0:n, :], x_sb[0:n, t, :] if isinstance(t, int) else x_sb[:, bass.ds(t, 1), :].rearrange("p a n -> p (a n)"),
                                     ACT.Square, scale=D_MODEL ** -0.5, accum_out=rstd[0:n, :]).then_inc(sq_ready, 1)
                act.wait_ge(sq_ready, t + 1)
                nc.scalar.activation(rstd[0:n, :], rstd[0:n, :], ACT.Sqrt, bias=eps[0:n, :]).then_inc(root_ready, 1)
                act.wait_ge(xT_ps, t + 1)
                nc.scalar.copy((xT_first if first else xT)[:, :, 0:n], turn[:, :].rearrange("p (k n) -> p k n", k=KC)[:, :, 0:n]).then_inc(xT_ready, 1)

            def q_out(m, n):
                act.wait_ge(q_ps, m + 1)
                nc.scalar.copy(q_rows[0:n, :], q_bank[0:n, 0:D_KEY]).then_inc(q_ready, 1)

            def qT_out(m, n):
                act.wait_ge(qT_ps, m + 1)
                nc.scalar.copy(qT[:, :, 0:n], q_bank[:, 256:512].rearrange("p (c n) -> p c n", c=2)[:, :, 0:n]).then_inc(qT_ready, 1)

            def s_out(m, n, first=False):
                act.wait_ge(s_ps, m + 1)
                if not first:
                    act.wait_ge(routed, m)
                nc.scalar.copy(s[0:n].rearrange("p c n -> p (c n)"), s_bank[0:n, 0:256]).then_inc(s_ready, 1)

            def exps(m, n):
                act.wait_ge(rel_ready, m + 1)
                nc.scalar.activation(ex[0:n, :], rel[0:n, :], ACT.Exp, accum_out=ex_sum[0:n, :]).then_inc(ex_ready, 1)

            def gelu(i, g):
                act.wait_ge(dotted, i + 1)
                nc.scalar.activation(acts[:, g % 4, :], dots[:, g % 4, :], ACT.Gelu).then_inc(gelud, 1)

            def first_window(h):
                a, b = 2 * h + 1, 2 * h + 2
                i = h * GROUPS
                q_out(a, 128)
                qT_out(a, 128)
                s_out(a, 128)
                for g in range(3):
                    gelu(i + g, g)
                q_out(b, 128)
                gelu(i + 3, 3)
                exps(a, 128)
                qT_out(b, 128)
                gelu(i + 4, 4)
                s_out(b, 128)
                for g in range(5, GROUPS):
                    gelu(i + g, g)
                exps(b, 128)

            def window(t, h, n, opens=False):
                m = (t + 1) * H_P + h
                i = (t * H_P + h) * GROUPS
                if opens:
                    gelu(i, 0)
                q_out(m, n)
                if not opens:
                    gelu(i, 0)
                gelu(i + 1, 1)
                qT_out(m, n)
                if opens:
                    s_out(m, n)
                gelu(i + 2, 2)
                if not opens:
                    s_out(m, n)
                for g in range(3, GROUPS - 1):
                    gelu(i + g, g)
                exps(m, n)
                gelu(i + GROUPS - 1, GROUPS - 1)

            act.wait_ge(zeroed, 2)
            prepare(0, first=True)
            q_out(0, 128)
            qT_out(0, 128)
            s_out(0, 128, first=True)
            exps(0, 128)
            prepare(1)
            with act.Fori(0, H_P - 1) as h:
                first_window(h)
            window(0, H_P - 1, 128)
            with act.Fori(1, NT - 1) as t:
                prepare(t + 1)
                window(t, 0, 128, opens=True)
                with act.Fori(1, H_P) as h:
                    window(t, h, 128)
            prepare(NT)
            window(NT - 1, 0, DEC_BATCH, opens=True)
            with act.Fori(1, H_P) as h:
                window(NT - 1, h, DEC_BATCH)
            for g in range(H_P // GROUP):
                gelu(NT * H_P * GROUPS + g, g)

        @block.vector
        def _(dve):
            def after(sem_, value):
                dve.wait_ge(sem_, value)
                dve.sem_inc(paced_dve, 1)

            def prepare(t, inverses, first=False):
                n = rows_of(t) if isinstance(t, int) else 128
                dve.wait_ge(root_ready, t + 1)
                nc.vector.reciprocal(rstd[0:n, :], rstd[0:n, :]).then_inc(inv_ready, 1)
                dve.wait_ge(inv_ready, inverses)
                if not first:
                    dve.wait_ge(xcur_ready, t)
                nc.vector.scalar_tensor_tensor(out=x_next[0:n, :], in0=x_sb[0:n, t, :] if isinstance(t, int) else x_sb[:, bass.ds(t, 1), :].rearrange("p a n -> p (a n)"),
                                               scalar=rstd[0:n, :], in1=gain[0:n, :], op0=ALU.mult, op1=ALU.mult).then_inc(xn_ready, 1)

            def route(r, m, n, h, inverses):
                parts = []
                R = R_STEPS

                def need(i):
                    after(rt, r * R + i)

                def first8():
                    after(s_ready, r + 1)
                    for c in range(2):
                        nc.vector.max(top[0:n, c, 0:8], s[0:n, c, :]).then_inc(rt, 1)
                    for c in range(2):
                        need(1 + c)
                        nc.vector.max_index(topi[0:n, c, 0:8], top[0:n, c, 0:8], s[0:n, c, :]).then_inc(rt, 1)
                    for c in range(2):
                        nc.vector.match_replace(s2[0:n, c, :], top[0:n, c, 0:8], s[0:n, c, :], NEG).then_inc(rt, 1)

                def next8():
                    for c in range(2):
                        need(5 + c)
                        nc.vector.max(top[0:n, c, 8:16], s2[0:n, c, :]).then_inc(rt, 1)
                    for c in range(2):
                        need(7 + c)
                        nc.vector.max_index(topi[0:n, c, 8:16], top[0:n, c, 8:16], s2[0:n, c, :]).then_inc(rt, 1)

                def pairs():
                    nc.vector.tensor_tensor(cand[0:n], bc(top[0:n, 0, :].unsqueeze(2), [n, TOPK, TOPK]),
                                            bc(top[0:n, 1, :].unsqueeze(1), [n, TOPK, TOPK]), ALU.add).then_inc(rt, 1)
                    need(10)
                    nc.vector.tensor_copy(topf[0:n], topi[0:n]).then_inc(rt, 1)
                    need(11)
                    nc.vector.max(best[0:n, 0:8], cand[0:n]).then_inc(rt, 1)
                    need(13)
                    cflat, c2flat = cand[0:n].rearrange("p a b -> p (a b)"), cand2[0:n].rearrange("p a b -> p (a b)")
                    nc.vector.max_index(besti[0:n, 0:8], best[0:n, 0:8], cflat).then_inc(rt, 1)
                    nc.vector.match_replace(c2flat, best[0:n, 0:8], cflat, NEG).then_inc(rt, 1)
                    need(15)
                    nc.vector.max(best[0:n, 8:16], c2flat).then_inc(rt, 1)
                    need(16)
                    nc.vector.max_index(besti[0:n, 8:16], best[0:n, 8:16], c2flat).then_inc(rt, 1)
                    nc.vector.tensor_scalar(rel[0:n, :], best[0:n, :], best[0:n, 0:1], None, ALU.subtract).then_inc(rel_ready, 1)

                def lookup():
                    need(17)
                    nc.vector.tensor_scalar(split[0:n, 0, :], besti[0:n, :], 4, None, ALU.logical_shift_right)
                    nc.vector.tensor_scalar(split[0:n, 1, :], besti[0:n, :], 15, None, ALU.bitwise_and).then_inc(rt, 1)
                    dve.wait_ge(rt, r * R + 18)
                    nc.vector.tensor_copy(splitf[0:n], split[0:n]).then_inc(looked, 1)
                    dve.wait_ge(looked, 4 * r + 1)
                    nc.vector.tensor_tensor(hit[0:n].rearrange("p c k j -> p (c k) j"), bc(splitf[0:n].rearrange("p c k -> p (c k)").unsqueeze(2), [n, 2 * TOPK, TOPK]),
                                            bc(iota16[0:n, :].unsqueeze(1), [n, 2 * TOPK, TOPK]), ALU.is_equal).then_inc(looked, 1)
                    dve.wait_ge(looked, 4 * r + 2)
                    nc.vector.tensor_tensor(hit[0:n], hit[0:n], bc(topf[0:n].unsqueeze(2), [n, 2, TOPK, TOPK]), ALU.mult).then_inc(looked, 1)
                    dve.wait_ge(looked, 4 * r + 3)
                    nc.vector.tensor_reduce(sel[0:n].rearrange("p c k -> p (c k)"), hit[0:n].rearrange("p c k j -> p (c k) j"), AX.X, ALU.add).then_inc(looked, 1)
                    dve.wait_ge(looked, 4 * r + 4)
                    if n == 128:
                        dst = ids[:, bass.ds(m * TOPK, TOPK)] if not isinstance(m, int) else ids[:, m * TOPK:m * TOPK + TOPK]
                    else:
                        dst = smp[0:n, 0, bass.ds(h * TOPK, TOPK)]
                    nc.vector.scalar_tensor_tensor(out=dst, in0=sel[0:n, 0, :], scalar=float(N_KEYS), in1=sel[0:n, 1, :], op0=ALU.mult, op1=ALU.add).then_inc(routed, 1)

                def softmax():
                    dve.wait_ge(ex_ready, r + 1)
                    nc.vector.reciprocal(ex_inv[0:n, :], ex_sum[0:n, :]).then_inc(inv_ready, 1)
                    dve.wait_ge(inv_ready, inverses)
                    if n == 128:
                        dst = gates[:, bass.ds(m * TOPK, TOPK)] if not isinstance(m, int) else gates[:, m * TOPK:m * TOPK + TOPK]
                    else:
                        dst = smp[0:n, 1, bass.ds(h * TOPK, TOPK)]
                    nc.vector.tensor_scalar(dst, ex[0:n, :], ex_inv[0:n, :], None, ALU.mult).then_inc(gates_ready, 1)

                return [first8, next8, pairs, lookup], softmax

            def dot(n, g, table=TOPK // RING):
                for j in range(GROUP):
                    k = g * GROUP + j
                    dve.wait_ge(rows_in[k % RING], (n * table + k // RING + 1) * 16)
                    last = nc.vector.tensor_tensor_reduce(rows[:, k % RING, 0:D_MODEL], rows[:, k % RING, 0:D_MODEL], x_cur[:], 1.0, 0.0,
                                                          ALU.mult, ALU.add, dots[:, g % 4, j:j + 1])
                last.then_inc(dotted, 1)

            def weigh(i, g, wide=True):
                dve.wait_ge(gelud, i + 1)
                for j in range(GROUP):
                    k = g * GROUP + j
                    dst, unit = (diag[:, g % 4, j, :], ident[:]) if wide else (diag[:, g % 4, j, 0:DEC_BATCH], gatherT[:])
                    last = nc.vector.tensor_scalar(dst, unit, acts[:, g % 4, j:j + 1], gate[:, k:k + 1], ALU.mult, ALU.mult)
                last.then_inc(diag_ready, 1)

            def copy_ids(dst, n, at, sem_):
                if not isinstance(n, int):
                    dve.sem_inc(paced_dve, 1)
                src = ids[:, n * TOPK + at:n * TOPK + at + 8] if isinstance(n, int) else ids[:, bass.ds(n * TOPK + at, 8)]
                nc.vector.tensor_copy(dst[:], src).then_inc(sem_, 1)

            def take_gate(n, made):
                dve.wait_ge(gates_ready, made)
                after(diag_ready, n * GROUPS + 1)
                src = gates[:, n * TOPK:n * TOPK + TOPK] if isinstance(n, int) else gates[:, bass.ds(n * TOPK, TOPK)]
                nc.vector.tensor_copy(gate[:], src).then_inc(gate_copied, 1)
                dve.wait_ge(gate_copied, n + 1)

            def first_window(h):
                a, b = 2 * h + 1, 2 * h + 2
                parts_a, softmax_a = route(a, h + 1, 128, h, a + 3)
                parts_b, softmax_b = route(b, h + H_P, 128, h, b + 3)
                take_gate(h, b - 1)
                for g in range(GROUPS):
                    dot(h, g)
                    if g == 0:
                        copy_ids(ids_hi, h, 8, hi_ready)
                    else:
                        weigh(h * GROUPS + g - 1, g - 1)
                    if 1 <= g < 5:
                        parts_a[g - 1]()
                    if g == 4:
                        dve.wait_ge(routed, b)
                        copy_ids(ids_lo, h + 1, 0, lo_ready)
                        softmax_a()
                    if 5 <= g:
                        parts_b[g - 5]()
                parts_b[3]()
                weigh(h * GROUPS + GROUPS - 1, GROUPS - 1)
                softmax_b()

            def window(t, h, rows_next, last_head=False, made=None):
                n = t * H_P + h
                m = n + H_P
                parts, softmax = route(m, m, rows_next, h, (t + 1) * (H_P + 1) + h + 2)
                take_gate(n, n + 1 if made is None else made)
                for g in range(GROUPS):
                    dot(n, g)
                    if g == 0:
                        copy_ids(ids_hi, n, 8, hi_ready)
                    if g == 3 and not last_head:
                        dve.wait_ge(routed, n + 2)
                        copy_ids(ids_lo, n + 1, 0, lo_ready)
                    if g:
                        weigh(n * GROUPS + g - 1, g - 1)
                    if 3 <= g < 7:
                        parts[g - 3]()
                softmax()
                weigh(n * GROUPS + GROUPS - 1, GROUPS - 1)

            def next_x(t):
                dve.wait_ge(dotted, t * H_P * GROUPS)
                nc.vector.tensor_copy(x_cur[:], x_next[:]).then_inc(xcur_ready, 1)
                dve.wait_ge(xcur_ready, t + 1)

            def add_to_x(t):
                n = rows_of(t) if isinstance(t, int) else 128
                xt = x_sb[0:n, t, :] if isinstance(t, int) else x_sb[:, bass.ds(t, 1), :].rearrange("p a n -> p (a n)")
                dve.wait_ge(acc_ready, t + 1)
                nc.vector.tensor_tensor(xt, xt, acc[0:n, :], ALU.add).then_inc(acc_used, 1)

            dve.sem_inc(diag_ready, 1)
            dve.sem_inc(acc_used, 1)
            dve.wait_ge(loaded, N_LOADED)
            prepare(0, 1, first=True)
            dve.wait_ge(xn_ready, 1)
            nc.vector.tensor_copy(x_cur[:], x_next[:]).then_inc(xcur_ready, 1)
            parts, softmax = route(0, 0, 128, 0, 2)
            for part in parts:
                part()
            dve.wait_ge(routed, 1)
            copy_ids(ids_lo, 0, 0, lo_ready)
            softmax()
            prepare(1, 3)
            with dve.Fori(0, H_P - 1) as h:
                first_window(h)
            window(0, H_P - 1, 128, made=2 * H_P - 1)
            next_x(1)
            add_to_x(0)
            with dve.Fori(1, NT - 1) as t:
                prepare(t + 1, (t + 1) * (H_P + 1) + 1)
                with dve.Fori(0, H_P) as h:
                    window(t, h, 128)
                next_x(t + 1)
                add_to_x(t)
            prepare(NT, NT * (H_P + 1) + 1)
            with dve.Fori(0, H_P - 1) as h:
                window(NT - 1, h, DEC_BATCH)
            window(NT - 1, H_P - 1, DEC_BATCH, last_head=True)
            dve.wait_ge(spread_ps, 1)
            nc.vector.tensor_tensor(smp_hit[:], q_bank[:, 0:256].rearrange("p (a k) -> p a k", k=TOPK), bc(own_k[:].unsqueeze(1), [128, 2 * H_P, TOPK]), ALU.mult).then_inc(smp_step, 1)
            dve.wait_ge(smp_step, 1)
            nc.vector.tensor_reduce(smp_own[:], smp_hit[:], AX.X, ALU.add).then_inc(smp_step, 1)
            dve.wait_ge(smp_step, 2)
            nc.vector.tensor_copy(ids_lo[:], smp_own[:, 0:H_P]).then_inc(lo_ready, 1)
            dve.wait_ge(diag_ready, NT * H_P * GROUPS + 1)
            nc.vector.tensor_copy(gate[:, 0:H_P], smp_own[:, H_P:2 * H_P]).then_inc(gate_copied, 1)
            dve.wait_ge(dotted, NT * H_P * GROUPS)
            nc.vector.tensor_copy(x_cur[:], turn[:, :]).then_inc(xcur_ready, 1)
            add_to_x(NT - 1)
            dve.wait_ge(xcur_ready, NT + 1)
            dve.wait_ge(gate_copied, NT * H_P + 1)
            for g in range(H_P // GROUP):
                dot(NT * H_P, g)
                if g:
                    weigh(NT * H_P * GROUPS + g - 1, g - 1, wide=False)
            weigh(NT * H_P * GROUPS + 3, 3, wide=False)
            add_to_x(NT)

        @block.tensor
        def _(pe):
            def transpose_x(t):
                n = rows_of(t) if isinstance(t, int) else 128
                pe.wait_ge(xn_ready, t + 1)
                for k in range(KC):
                    last = nc.tensor.transpose(turn[:, 128 * k:128 * k + n], x_next[0:n, 128 * k:128 * k + 128], ident[0:n, 0:n])
                last.then_inc(xT_ps, 1)
                pe.wait_ge(xT_ready, t + 1)

            def queries(m, h, n, first=False, src=xT):
                if not first:
                    pe.wait_ge(qT_ready, m)
                for k in range(KC):
                    cols = w_q[:, k, bass.ds(h * D_KEY, D_KEY)]
                    last = nc.tensor.matmul(q_bank[0:n, 0:D_KEY], src[:, k, 0:n], cols, start=(k == 0), stop=(k == KC - 1))
                last.then_inc(q_ps, 1)

            def transpose_q(m, n):
                pe.wait_ge(q_ready, m + 1)
                pe.sem_inc(paced_pe, 1)
                for c in range(2):
                    last = nc.tensor.transpose(q_bank[:, 256 + 128 * c:256 + 128 * c + n], q_rows[0:n, 128 * c:128 * c + 128], ident[0:n, 0:n])
                last.then_inc(qT_ps, 1)

            def scores(m, h, n, first=False):
                if not first:
                    pe.wait_ge(s_ready, m)
                pe.wait_ge(qT_ready, m + 1)
                for c in range(2):
                    last = nc.tensor.matmul(s_bank[0:n, 128 * c:128 * c + 128], qT[:, c, 0:n], keysT[:, bass.ds((2 * h + c) * N_KEYS, N_KEYS)], start=True, stop=True)
                last.then_inc(s_ps, 1)

            def open_acc(t, n):
                pe.wait_ge(acc_used, t + 1)
                for b in range(2):
                    nc.tensor.matmul(acc[0:n, 512 * b:512 * b + 512], zero[:, 0:n], keysT[:, 0:512], start=True, stop=False)

            def close_acc(n):
                for b in range(2):
                    last = nc.tensor.matmul(acc[0:n, 512 * b:512 * b + 512], zero[:, 0:n], keysT[:, 0:512], start=False, stop=True)
                last.then_inc(acc_ready, 1)

            def experts(i, g, n):
                pe.wait_ge(diag_ready, i + 2)
                for j in range(GROUP):
                    k = g * GROUP + j
                    for b in range(2):
                        last = nc.tensor.matmul(acc[0:n, 512 * b:512 * b + 512], diag[:, g % 4, j, 0:n], rows[:, k % RING, D_MODEL + 512 * b:D_MODEL + 512 * b + 512],
                                                start=False, stop=False)
                    last.then_inc(rows_used, 1)

            def first_window(h):
                a, b = 2 * h + 1, 2 * h + 2
                i = h * GROUPS
                queries(a, h + 1, 128, src=xT_first)
                transpose_q(a, 128)
                scores(a, h + 1, 128)
                experts(i, 0, 128)
                experts(i + 1, 1, 128)
                queries(b, h, 128)
                experts(i + 2, 2, 128)
                transpose_q(b, 128)
                experts(i + 3, 3, 128)
                scores(b, h, 128)
                for g in range(4, GROUPS):
                    experts(i + g, g, 128)

            def spread_sample():
                pe.wait_ge(gates_ready, (NT + 1) * H_P)
                pe.wait_ge(routed, (NT + 1) * H_P)
                nc.tensor.matmul(q_bank[:, 0:256], spread[:], smp[:].rearrange("p c n -> p (c n)"), start=True, stop=True)
                for b in range(2):
                    last = nc.tensor.matmul(turn[:, 512 * b:512 * b + 512], spread[:], x_next[0:DEC_BATCH, 512 * b:512 * b + 512], start=True, stop=True)
                last.then_inc(spread_ps, 1)

            def window(t, h, n, opens=False, before_last=None):
                m = (t + 1) * H_P + h
                i = (t * H_P + h) * GROUPS
                if opens:
                    experts(i, 0, 128)
                queries(m, h, n)
                if not opens:
                    experts(i, 0, 128)
                    transpose_q(m, n)
                experts(i + 1, 1, 128)
                if opens:
                    transpose_q(m, n)
                scores(m, h, n)
                for g in range(2, GROUPS):
                    if g == GROUPS - 1 and before_last:
                        before_last()
                    experts(i + g, g, 128)

            pe.wait_ge(zeroed, 2)
            pe.wait_ge(loaded, N_LOADED)
            transpose_x(0)
            pe.wait_ge(w_q_first, 16 * KC)
            queries(0, 0, 128, first=True, src=xT_first)
            transpose_q(0, 128)
            scores(0, 0, 128, first=True)
            transpose_x(1)
            open_acc(0, 128)
            pe.wait_ge(w_q_in, 16 * KC)
            with pe.Fori(0, H_P - 1) as h:
                first_window(h)
            window(0, H_P - 1, 128)
            close_acc(128)
            with pe.Fori(1, NT - 1) as t:
                transpose_x(t + 1)
                open_acc(t, 128)
                window(t, 0, 128, opens=True)
                with pe.Fori(1, H_P) as h:
                    window(t, h, 128)
                close_acc(128)
            transpose_x(NT)
            open_acc(NT - 1, 128)
            window(NT - 1, 0, DEC_BATCH, opens=True)
            with pe.Fori(1, H_P - 1) as h:
                window(NT - 1, h, DEC_BATCH)
            window(NT - 1, H_P - 1, DEC_BATCH, before_last=spread_sample)
            close_acc(128)
            open_acc(NT, DEC_BATCH)
            for g in range(H_P // GROUP):
                experts(NT * H_P * GROUPS + g, g, DEC_BATCH)
            close_acc(DEC_BATCH)


def latent_projections(nc, w, out, ident, x_sb, smp):
    with ExitStack() as ctx:
        def sb(name, shape, dt=F32):
            return ctx.enter_context(nc.sbuf_tensor("c_" + name, shape, dt))

        sem = signals(nc, ctx, "c_")

        w_in = sb("w_in", [128, KC, D_IN_C])
        w_qb = sb("w_qb", [128, 3, H_C * 96])
        w_uk = sb("w_uk", [128, 2, H_C * D_NOPE])
        w_uv = sb("w_uv", [128, 2, H_C * D_V])
        w_out = sb("w_out", [128, KC, D_MODEL])
        norm_col = sb("norm_col", [128, KC])
        qn_col = sb("qn_col", [128, 3])
        kv_gain = sb("kv_gain", [128, R_KV])
        cos2 = sb("cos2", [128, NT + 1, D_ROPE])
        sin2 = sb("sin2", [128, NT + 1, D_ROPE])
        eps = sb("eps", [128, 1])
        causal = sb("causal", [128, 128])
        o = sb("o", [128, D_MODEL])
        rstd = sb("rstd", [128, 1])
        rstd2 = sb("rstd2", [128, 2])
        xs = sb("xs", [128, D_MODEL])
        xT = sb("xT", [128, KC, 128])
        cqT = sb("cqT", [128, 3, 128])
        ckv = sb("ckv", [128, 2, R_KV])
        ckvT = sb("ckvT", [128, 2, 128])
        kz = sb("kz", [128, 2, 96])
        kraw = sb("kraw", [128, D_ROPE])
        q = sb("q", [128, H_C, 96])
        cq = q[:, :, :].rearrange("p h d -> p (h d)")[:, 0:R_Q]
        rot = sb("rot", [128, 2, H_C, D_ROPE])
        qT = sb("qT", [96, H_C, 128])
        kT = sb("kT", [96, H_C, SEQ])
        v = sb("v", [128, NT, H_C * D_V])
        nmax = sb("nmax", [128, 2, 2])
        prob = rot[:, :, :, :].rearrange("p b h d -> p b (h d)")
        rot_k = sb("rot_k", [128, 2, 1, D_ROPE])
        probT = q[:, :, :].rearrange("p h d -> p (h d)")[:, 0:2 * SEQ].rearrange("p (b n) -> p b n", b=2)
        sums = sb("sums", [128, H_C])
        oT = rot[:, :, :, :].rearrange("p b h d -> p (b h d)").rearrange("p (k n) -> p k n", k=KC)
        ps = [ctx.enter_context(nc.psum_tensor(f"c_ps{i}", [128, 1024], F32)) for i in range(4)]

        small_in, w_in_in, wqb_in, wuk_in, wout_in = sem("small_in"), sem("w_in_in"), sem("wqb_in"), sem("wuk_in"), sem("wout_in")
        consts, sq_ready, root_ready, dve_step, xs_ready, xT_ps, xT_ready, z_ps = (sem("consts"), sem("sq_ready"), sem("root_ready"), sem("dve_step"), sem("xs_ready"), sem("xT_ps"), sem("xT_ready"), sem("z_ps"))
        zsq_ready, zroot_ready, lat_ready, latT_ps, cqT_ready, ckvT_ready = (sem("zsq_ready"), sem("zroot_ready"), sem("lat_ready"), sem("latT_ps"), sem("cqT_ready"), sem("ckvT_ready"))
        q_ps, q_ready, k_ps, k_used, v_ps, v_ready, rope_ready, qT_ps, qT_act, qT_dve = (sem("q_ps"), sem("q_ready"), sem("k_ps"), sem("k_used"), sem("v_ps"), sem("v_ready"), sem("rope_ready"), sem("qT_ps"), sem("qT_act"), sem("qT_dve"))
        s_ps, max_ready, neg_ready, p_ready, pT_ps, pT_ready, o_ps, o_ready, oT_ps, oT_ready, y_ps, y_used = (sem(n) for n in (
            "s_ps", "max_ready", "neg_ready", "p_ready", "pT_ps", "pT_ready", "o_ps", "o_ready", "oT_ps", "oT_ready", "y_ps", "y_used"))
        stores = sem("stores")
        block = ctx.enter_context(nc.Block())
        N_SMALL = 6

        @block.sync
        def _(sp):
            for dst, name in ((norm_col, "c_norm_cols"), (qn_col, "q_norm_cols"), (cos2, "cos2"), (sin2, "sin2"), (causal, "causal")):
                sp.dma_start(dst[:], w[name]).then_inc(small_in, 16)
            sp.dma_start(kv_gain[:], w["c_kv_norm"].to_broadcast([128, R_KV])).then_inc(small_in, 16)
            sp.dma_start(w_in[:], w["c_w_in"][0].rearrange("(k p) n -> p k n", p=128)).then_inc(w_in_in, 16)
            sp.dma_start(w_qb[:], w["c_w_q_b"][0].rearrange("(k p) n -> p k n", p=128)).then_inc(wqb_in, 16)
            sp.dma_start(w_uk[:], w["c_w_uk"][0].rearrange("(k p) h n -> p k (h n)", p=128)).then_inc(wuk_in, 16)
            sp.dma_start(w_uv[:], w["c_w_uv"][0].rearrange("(k p) h n -> p k (h n)", p=128)).then_inc(wuk_in, 16)
            sp.dma_start(w_out[:], w["c_w_out"][0].rearrange("(k p) n -> p k n", p=128)).then_inc(wout_in, 16)
            for t in range(NT + 1):
                n = rows_of(t)
                sp.wait_ge(lat_ready, t + 1)
                if t < NT:
                    ckv_dst, kpe_dst = out["new_ckv_prompt"][0, 0, 128 * t:128 * t + 128, :], out["new_kpe_prompt"][0, 0, 128 * t:128 * t + 128, :]
                else:
                    ckv_dst, kpe_dst = out["new_ckv_sample"][0, :, 0, :], out["new_kpe_sample"][0, :, 0, :]
                sp.dma_start(ckv_dst, ckv[0:n, t % 2, :]).then_inc(stores, 16)
                sp.dma_start(kpe_dst, kz[0:n, t % 2, 64:96]).then_inc(stores, 16)
                sp.wait_ge(stores, 32 * (t + 1))

        @block.gpsimd
        def _(pool):
            nc.gpsimd.memset(eps[:], EPS).then_inc(consts, 1)
            nc.gpsimd.memset(kz[:], 0.0).then_inc(consts, 1)

        @block.scalar
        def _(act):
            def mean_square(t):
                n = rows_of(t)
                if t:
                    act.wait_ge(xs_ready, t)
                if t >= 2:
                    act.wait_ge(oT_ps, t - 1)
                nc.scalar.activation(o[0:n, :], x_sb[0:n, t, :], ACT.Square, scale=D_MODEL ** -0.5, accum_out=rstd[0:n, :]).then_inc(sq_ready, 1)
                act.wait_ge(sq_ready, t + 1)
                nc.scalar.activation(rstd[0:n, :], rstd[0:n, :], ACT.Sqrt, bias=eps[0:n, :]).then_inc(root_ready, 1)

            act.wait_ge(consts, 2)
            mean_square(0)
            for t in range(NT + 1):
                n = rows_of(t)
                act.wait_ge(z_ps, t + 1)
                junk = q[0:n, :, :].rearrange("p h d -> p (h d)")
                nc.scalar.activation(junk[:, 512:512 + R_Q], ps[0][0:n, 0:R_Q], ACT.Square, scale=R_Q ** -0.5, accum_out=rstd2[0:n, 0:1])
                nc.scalar.activation(junk[:, 1024:1024 + R_KV], ps[0][0:n, 512:512 + R_KV], ACT.Square, scale=R_KV ** -0.5, accum_out=rstd2[0:n, 1:2]).then_inc(zsq_ready, 1)
                act.wait_ge(zsq_ready, t + 1)
                nc.scalar.activation(rstd2[0:n, :], rstd2[0:n, :], ACT.Sqrt, bias=eps[0:n, :]).then_inc(zroot_ready, 1)
                act.wait_ge(latT_ps, t + 1)
                if t < NT:
                    nc.scalar.copy(ckvT[:, :, 0:n], ps[3][:, 512:768].rearrange("p (c n) -> p c n", c=2))
                    nc.scalar.copy(kT[64:96, :, cols_of(t)], bc(ps[3][64:96, 768:896].unsqueeze(1), [32, H_C, 128])).then_inc(ckvT_ready, 1)
                else:
                    nc.scalar.copy(smp["ckvT"][:], ps[3][:, 512:768].rearrange("p (c n) -> p c n", c=2)[:, :, 0:n])
                    nc.scalar.copy(smp["kpeT"][64:96, :], ps[3][64:96, 768:768 + n]).then_inc(ckvT_ready, 1)
                act.wait_ge(q_ps, t + 1)
                if t:
                    act.wait_ge(qT_ps, t)
                q_flat = q[0:n].rearrange("p h d -> p (h d)")
                nc.scalar.copy(q_flat[:, 0:1024], ps[0][0:n, :]).then_inc(q_ready, 1)
                nc.scalar.copy(q_flat[:, 1024:1536], ps[1][0:n, 0:512]).then_inc(q_ready, 1)
                if t == NT:
                    break
                act.wait_ge(v_ps, t + 1)
                nc.scalar.copy(v[:, t, :], ps[3][:, :]).then_inc(v_ready, 1)
                act.wait_ge(qT_ps, t + 1)
                nc.scalar.copy(qT[:, 0:8, :], ps[0][0:96, :].rearrange("p (h n) -> p h n", h=8)).then_inc(qT_act, 1)
                mean_square(t + 1)
                keys = 128 * (t + 1)
                for h in range(H_C):
                    i = H_C * t + h
                    act.wait_ge(neg_ready, i + 1)
                    if i >= 2:
                        act.wait_ge(pT_ps, i - 1)
                    if h == 0 and t:
                        act.wait_ge(o_ready, t)
                    nc.scalar.activation(prob[:, i % 2, 0:keys], ps[0][:, 512 * (i % 2):512 * (i % 2) + keys], ACT.Exp, scale=MLA_SCALE,
                                         bias=nmax[:, 1, i % 2:i % 2 + 1], accum_out=sums[:, h:h + 1]).then_inc(p_ready, 1)
                act.wait_ge(oT_ps, t + 1)
                nc.scalar.copy(oT.rearrange("p k n -> p (k n)"), ps[3][:, :]).then_inc(oT_ready, 1)

        @block.vector
        def _(dve):
            steps = [0]

            def step(ins):
                steps[0] += 1
                ins.then_inc(dve_step, 1)
                dve.wait_ge(dve_step, steps[0])

            def rotate(dst, src, n, heads, t, tmp):
                c = bc(cos2[0:n, t, :].unsqueeze(1), [n, heads, D_ROPE])
                nc.vector.tensor_tensor(tmp[0:n, 1, 0:heads, 0:16], src[:, :, 16:32], bc(sin2[0:n, t, 0:16].unsqueeze(1), [n, heads, 16]), ALU.mult)
                nc.vector.tensor_tensor(tmp[0:n, 1, 0:heads, 16:32], src[:, :, 0:16], bc(sin2[0:n, t, 16:32].unsqueeze(1), [n, heads, 16]), ALU.mult)
                step(nc.vector.tensor_tensor(tmp[0:n, 0, 0:heads, :], src, c, ALU.mult))
                return nc.vector.tensor_tensor(dst, tmp[0:n, 0, 0:heads, :], tmp[0:n, 1, 0:heads, :], ALU.add)

            dve.wait_ge(small_in, 16 * N_SMALL)
            dve.wait_ge(consts, 2)

            def scale_rows(t):
                n = rows_of(t)
                dve.wait_ge(root_ready, t + 1)
                step(nc.vector.reciprocal(rstd[0:n, :], rstd[0:n, :]))
                nc.vector.tensor_scalar(xs[0:n, :], x_sb[0:n, t, :], rstd[0:n, :], None, ALU.mult).then_inc(xs_ready, 1)

            def turn_in(t):
                n = rows_of(t)
                dve.wait_ge(xT_ps, t + 1)
                nc.vector.tensor_tensor(xT[:, :, 0:n], ps[3][:, :].rearrange("p (k n) -> p k n", k=KC)[:, :, 0:n], bc(norm_col[:].unsqueeze(2), [128, KC, n]), ALU.mult).then_inc(xT_ready, 1)

            scale_rows(0)
            turn_in(0)
            for t in range(NT + 1):
                n = rows_of(t)
                dve.wait_ge(zroot_ready, t + 1)
                step(nc.vector.reciprocal(rstd2[0:n, :], rstd2[0:n, :]))
                if t:
                    dve.wait_ge(latT_ps, t)
                nc.vector.tensor_scalar(cq[0:n, :], ps[0][0:n, 0:R_Q], rstd2[0:n, 0:1], None, ALU.mult)
                if t >= 2:
                    dve.wait_ge(stores, 32 * (t - 1))
                nc.vector.scalar_tensor_tensor(out=ckv[0:n, t % 2, :], in0=ps[0][0:n, 512:512 + R_KV], scalar=rstd2[0:n, 1:2], in1=kv_gain[0:n, :], op0=ALU.mult, op1=ALU.mult)
                step(nc.vector.tensor_copy(kraw[0:n, :], ps[0][0:n, 512 + R_KV:512 + R_KV + D_ROPE]))
                rotate(kz[0:n, t % 2, 64:96].unsqueeze(1), kraw[0:n, :].unsqueeze(1), n, 1, t, rot_k).then_inc(lat_ready, 1)
                if t:
                    dve.wait_ge(y_ps, t)
                    nc.vector.tensor_tensor(x_sb[:, t - 1, :], x_sb[:, t - 1, :], ps[2][:, :], ALU.add).then_inc(y_used, 1)
                dve.wait_ge(latT_ps, t + 1)
                nc.vector.tensor_tensor(cqT[:, :, 0:n], ps[3][:, 0:384].rearrange("p (c n) -> p c n", c=3)[:, :, 0:n], bc(qn_col[:].unsqueeze(2), [128, 3, n]), ALU.mult).then_inc(cqT_ready, 1)
                if t < NT:
                    dve.wait_ge(k_ps, t + 1)
                    nc.vector.tensor_copy(kT[0:64, 0:8, cols_of(t)], ps[3][0:64, :].rearrange("p (h n) -> p h n", h=8)).then_inc(k_used, 1)
                    nc.vector.tensor_copy(kT[0:64, 8:16, cols_of(t)], ps[2][0:64, :].rearrange("p (h n) -> p h n", h=8)).then_inc(k_used, 1)
                dve.wait_ge(q_ready, 2 * (t + 1))
                if t == NT:
                    dve.wait_ge(lat_ready, NT + 1)
                    nc.vector.tensor_copy(smp["ckv"][:], ckv[0:n, t % 2, :])
                    rotate(q[0:n, :, 64:96], q[0:n, :, 64:96], n, H_C, t, rot).then_inc(rope_ready, 1)
                    dve.wait_ge(rope_ready, t + 1)
                    nc.vector.tensor_copy(smp["qn"][:], q[0:n, :, 0:64])
                    nc.vector.tensor_copy(smp["qp"][:], bc(q[0:n, :, 64:96].unsqueeze(2), [n, H_C, 4, D_ROPE]))
                    break
                rotate(q[0:n, :, 64:96], q[0:n, :, 64:96], n, H_C, t, rot).then_inc(rope_ready, 1)
                dve.wait_ge(qT_ps, t + 1)
                nc.vector.tensor_copy(qT[:, 8:16, :], ps[1][0:96, :].rearrange("p (h n) -> p h n", h=8)).then_inc(qT_dve, 1)
                keys = 128 * (t + 1)

                def turn_out(i):
                    dve.wait_ge(pT_ps, i + 1)
                    if i >= 2:
                        dve.wait_ge(o_ps, i - 1)
                    nc.vector.tensor_copy(probT[:, i % 2, 0:keys], ps[1][:, 512 * (i % 2):512 * (i % 2) + keys]).then_inc(pT_ready, 1)

                for h in range(H_C):
                    i = H_C * t + h
                    dve.wait_ge(s_ps, i + 1)
                    if i >= 2:
                        dve.wait_ge(p_ready, i - 1)
                    nc.vector.tensor_reduce(nmax[:, 0, i % 2:i % 2 + 1], ps[0][:, 512 * (i % 2):512 * (i % 2) + keys], AX.X, ALU.max).then_inc(max_ready, 1)
                    dve.wait_ge(max_ready, i + 1)
                    nc.vector.tensor_scalar(nmax[:, 1, i % 2:i % 2 + 1], nmax[:, 0, i % 2:i % 2 + 1], -MLA_SCALE, None, ALU.mult).then_inc(neg_ready, 1)
                    if h:
                        turn_out(i - 1)
                    if h == 4:
                        scale_rows(t + 1)
                    if h == 8:
                        turn_in(t + 1)
                turn_out(H_C * t + H_C - 1)
                dve.wait_ge(p_ready, H_C * (t + 1))
                step(nc.vector.reciprocal(sums[:], sums[:]))
                dve.wait_ge(o_ps, H_C * (t + 1))
                nc.vector.tensor_tensor(o[:].rearrange("p (h v) -> p h v", h=H_C), ps[2][:, :].rearrange("p (h v) -> p h v", h=H_C),
                                        bc(sums[:].unsqueeze(2), [128, H_C, D_V]), ALU.mult).then_inc(o_ready, 1)

        @block.tensor
        def _(pe):
            def turn_rows(t):
                n = rows_of(t)
                pe.wait_ge(xs_ready, t + 1)
                for k in range(KC):
                    last = nc.tensor.transpose(ps[3][:, 128 * k:128 * k + n], xs[0:n, 128 * k:128 * k + 128], ident[0:n, 0:n])
                last.then_inc(xT_ps, 1)

            def project(t, part):
                n = rows_of(t)
                at, lo, hi = ((0, 0, R_Q), (512, R_Q, D_IN_C))[part]
                if part == 0:
                    pe.wait_ge(xT_ready, t + 1)
                for k in range(KC):
                    last = nc.tensor.matmul(ps[0][0:n, at:at + hi - lo], xT[:, k, 0:n], w_in[:, k, lo:hi], start=(k == 0), stop=(k == KC - 1))
                if part:
                    last.then_inc(z_ps, 1)

            turn_rows(0)
            pe.wait_ge(w_in_in, 16)
            project(0, 0)
            project(0, 1)
            for t in range(NT + 1):
                n = rows_of(t)
                pe.wait_ge(lat_ready, t + 1)
                for c in range(3):
                    nc.tensor.transpose(ps[3][:, 128 * c:128 * c + n], cq[0:n, 128 * c:128 * c + 128], ident[0:n, 0:n])
                for c in range(2):
                    nc.tensor.transpose(ps[3][:, 512 + 128 * c:512 + 128 * c + n], ckv[0:n, t % 2, 128 * c:128 * c + 128], ident[0:n, 0:n])
                nc.tensor.transpose(ps[3][0:96, 768:768 + n], kz[0:n, t % 2, :], ident[0:n, 0:n]).then_inc(latT_ps, 1)
                pe.wait_ge(cqT_ready, t + 1)
                pe.wait_ge(wqb_in, 16)
                for b in range(3):
                    for k in range(3):
                        last = nc.tensor.matmul(ps[b // 2][0:n, 512 * (b % 2):512 * (b % 2) + 512], cqT[:, k, 0:n], w_qb[:, k, 512 * b:512 * b + 512], start=(k == 0), stop=(k == 2))
                last.then_inc(q_ps, 1)
                if t == NT:
                    break
                pe.wait_ge(ckvT_ready, t + 1)
                pe.wait_ge(wuk_in, 32)
                if t:
                    pe.wait_ge(y_used, t)
                for h in range(H_C):
                    dst = ps[3 - h // 8][0:64, 128 * (h % 8):128 * (h % 8) + 128]
                    for c in range(2):
                        last = nc.tensor.matmul(dst, w_uk[:, c, 64 * h:64 * h + 64], ckvT[:, c, :], start=(c == 0), stop=(c == 1))
                last.then_inc(k_ps, 1)
                pe.wait_ge(k_used, 2 * (t + 1))
                for b in range(2):
                    for c in range(2):
                        last = nc.tensor.matmul(ps[3][:, 512 * b:512 * b + 512], ckvT[:, c, :], w_uv[:, c, 512 * b:512 * b + 512], start=(c == 0), stop=(c == 1))
                last.then_inc(v_ps, 1)
                pe.wait_ge(q_ready, 2 * (t + 1))
                pe.wait_ge(rope_ready, t + 1)
                for h in range(H_C):
                    last = nc.tensor.transpose(ps[h // 8][0:96, 128 * (h % 8):128 * (h % 8) + 128], q[:, h, :], ident[:])
                last.then_inc(qT_ps, 1)
                pe.wait_ge(qT_act, t + 1)
                pe.wait_ge(qT_dve, t + 1)
                pe.wait_ge(v_ready, t + 1)
                keys = 128 * (t + 1)

                def scores(h):
                    i = H_C * t + h
                    if h >= 2:
                        pe.wait_ge(p_ready, i - 1)
                    dst = ps[0][:, 512 * (i % 2):512 * (i % 2) + keys]
                    nc.tensor.matmul(dst, qT[:, h, :], kT[:, h, 0:keys], start=True, stop=False)
                    nc.tensor.matmul(dst[:, 128 * t:128 * t + 128], ident[:], causal[:], start=False, stop=True).then_inc(s_ps, 1)

                def turn(h):
                    i = H_C * t + h
                    pe.wait_ge(p_ready, i + 1)
                    if h >= 2:
                        pe.wait_ge(pT_ready, i - 1)
                    for b in range(t + 1):
                        last = nc.tensor.transpose(ps[1][:, 512 * (i % 2) + 128 * b:512 * (i % 2) + 128 * b + 128], prob[:, i % 2, 128 * b:128 * b + 128], ident[:])
                    last.then_inc(pT_ps, 1)

                def weighted(h):
                    i = H_C * t + h
                    pe.wait_ge(pT_ready, i + 1)
                    for b in range(t + 1):
                        last = nc.tensor.matmul(ps[2][:, 64 * h:64 * h + 64], probT[:, i % 2, 128 * b:128 * b + 128], v[:, b, 64 * h:64 * h + 64], start=(b == 0), stop=(b == t))
                    last.then_inc(o_ps, 1)

                scores(0)
                for h in range(H_C):
                    if h + 1 < H_C:
                        scores(h + 1)
                    turn(h)
                    if h:
                        weighted(h - 1)
                    if h == 6:
                        turn_rows(t + 1)
                weighted(H_C - 1)
                project(t + 1, 0)
                pe.wait_ge(o_ready, t + 1)
                for k in range(KC):
                    last = nc.tensor.transpose(ps[3][:, 128 * k:128 * k + 128], o[:, 128 * k:128 * k + 128], ident[:])
                last.then_inc(oT_ps, 1)
                project(t + 1, 1)
                pe.wait_ge(oT_ready, t + 1)
                pe.wait_ge(wout_in, 16)
                for b in range(2):
                    for k in range(KC):
                        last = nc.tensor.matmul(ps[2][:, 512 * b:512 * b + 512], oT[:, k, :], w_out[:, k, 512 * b:512 * b + 512], start=(k == 0), stop=(k == KC - 1))
                last.then_inc(y_ps, 1)


def latent_sample(nc, w, ident, x_sb, smp):
    B, NQ = DEC_BATCH, 4
    BUFS = 3
    KEYS_8 = 8
    PIECES = NP // KEYS_8
    NB = B * PIECES
    with ExitStack() as ctx:
        def sb(name, shape, dt=F32):
            return ctx.enter_context(nc.sbuf_tensor("d_" + name, shape, dt))

        sem = signals(nc, ctx, "d_")

        w_ukT = sb("w_ukT", [128, H_C // 2, R_KV])
        w_uv = sb("w_uv", [128, 2, H_C * D_V])
        table = sb("table", [KEYS_8, NB], I32)
        table_f = sb("table_f", [KEYS_8, NB])
        spread = sb("spread", [KEYS_8, 128])
        part = sb("part", [128, 1])
        row_ids = sb("row_ids", [128, NB], I32)
        four = sb("four", [128, NQ])
        ones = sb("ones", [128, 128])
        past = sb("past", [128, BUFS, PIECES, KEYS_8 * (R_KV + D_ROPE)])

        def latent(b, slot, c=None):
            at, n = (R_KV * (slot % KEYS_8), R_KV) if c is None else (R_KV * (slot % KEYS_8) + 128 * c, 128)
            return past[:, b % BUFS, slot // KEYS_8, at:at + n]

        W_OUT_IN = (B - 3) % BUFS
        w_out = past[:, W_OUT_IN].rearrange("p s r -> p (s r)")[:, 0:KC * D_MODEL].rearrange("p (k n) -> p k n", k=KC)
        qnT = sb("qnT", [128, H_C // 2, B])
        qlT = sb("qlT", [128, 2, B, H_C])
        qpT = sb("qpT", [128, B, NQ, H_C])
        qp_self = sb("qp_self", [32, B, H_C])
        kp_self = sb("kp_self", [32, B])
        self_s = sb("self_s", [1, B * H_C])
        self_row = sb("self_row", [1, B, R_KV])
        ckvT = sb("ckvT", [128, 2, NQ * 2 * 128])
        kpeT = sb("kpeT", [128, NP // NQ, 128])
        sc = sb("sc", [128, 2, NP + 1, H_C])
        m1 = sb("m1", [128, H_C])
        mx = sb("mx", [H_C, 1])
        dmx = sb("dmx", [H_C, H_C])
        sums = sb("sums", [128, H_C])
        inv = sb("inv", [H_C, 1])
        o_n = sb("o_n", [H_C, R_KV])
        olT = sb("olT", [128, 2, H_C, B])
        oT = sb("oT", [128, KC, B])
        turn = [ctx.enter_context(nc.psum_tensor(f"d_turn{i}", [128, 1024], F32)) for i in range(2)]
        s_bank = ctx.enter_context(nc.psum_tensor("d_s", [128, 512], F32))
        m_bank = ctx.enter_context(nc.psum_tensor("d_m", [128, 512], F32))
        o_bank = [ctx.enter_context(nc.psum_tensor(f"d_o{i}", [128, 512], F32)) for i in range(2)]

        loaded, wout_in, table_in, consts = sem("loaded"), sem("wout_in"), sem("table_in"), sem("consts")
        table_ready, ids_ps, ids_ready = sem("table_ready"), sem("ids_ps"), sem("ids_ready")
        past_in = [[sem(f"past_in{b}_{g}") for g in range(PIECES)] for b in range(BUFS)]
        qnT_ps, qnT_ready, ql_ps, ql_ready, qp_ps, qp_ready, self_ps, self_ready, row_in, kps_ready = (sem(n) for n in (
            "qnT_ps", "qnT_ready", "ql_ps", "ql_ready", "qp_ps", "qp_ready", "self_ps", "self_ready", "row_in", "kps_ready"))
        kpeT_ps, kpeT_ready, turn_ps, turn_act, turn_dve, turn_used, sc_ready = (sem(n) for n in (
            "kpeT_ps", "kpeT_ready", "turn_ps", "turn_act", "turn_dve", "turn_used", "sc_ready"))
        self_put, m1_ready, m1T_ps, mx_ready, dmx_ready, mb_ps, rel_ready, p_ready, sum_ready, sumb_ps, inv_ready, o_ps, o_used, masked, olT_ps, olT_ready = (sem(n) for n in (
            "self_put", "m1_ready", "m1T_ps", "mx_ready", "dmx_ready", "mb_ps", "rel_ready", "p_ready", "sum_ready", "sumb_ps", "inv_ready", "o_ps", "o_used", "masked", "olT_ps", "olT_ready"))
        oT_ps, oT_ready, y_ps, y_used = sem("oT_ps"), sem("oT_ready"), sem("y_ps"), sem("y_used")
        block = ctx.enter_context(nc.Block())
        G = NP // NQ
        RELATIVE_AT = 3

        @block.sync
        def _(sp):
            sp.dma_start(table[:], w["page_cols"]).then_inc(table_in, 16)
            sp.dma_start(spread[:], w["spread"]).then_inc(table_in, 16)
            sp.dma_start(part[:], w["sixteenth"]).then_inc(table_in, 16)
            sp.dma_start(w_ukT[:], w["w_ukT"]).then_inc(loaded, 16)
            sp.dma_start(four[:], w["four"]).then_inc(loaded, 16)
            sp.dma_start(self_row[:].rearrange("a b r -> a (b r)"), smp["ckv"][:]).then_inc(row_in, 16)
            sp.dma_start(w_uv[:], w["c_w_uv"][0].rearrange("(k p) h n -> p k (h n)", p=128)).then_inc(wout_in, 16)
            sp.wait_ge(o_ps, B - 2)
            sp.dma_start(w_out, w["c_w_out"][0].rearrange("(k p) n -> p k n", p=128)).then_inc(wout_in, 16)

        @block.gpsimd
        def _(pool):
            nc.gpsimd.memset(ones[:], 1.0).then_inc(consts, 1)
            nc.gpsimd.memset(sc[:, :, NP, :], NEG_MASK).then_inc(consts, 1)
            pool.wait_ge(ids_ready, 1)
            for b in range(B):
                if b >= BUFS:
                    pool.wait_ge(o_ps, b - BUFS + 1)
                for g in range(PIECES):
                    nc.gpsimd.indirect_dma_start(out=past[:, b % BUFS, g, :], out_offset=None, in_=w["cache_rows"],
                                                 in_offset=bass.IndirectOffsetOnAxis(ap=row_ids[:, PIECES * b + g:PIECES * b + g + 1], axis=0)
                                                 ).then_inc(past_in[b % BUFS][g], 16)

        @block.scalar
        def _(act):
            nc.scalar.copy(kp_self[:], smp["kpeT"][64:96, :]).then_inc(kps_ready, 1)
            act.wait_ge(qnT_ps, 1)
            nc.scalar.copy(qnT[:].rearrange("p h b -> p (h b)"), m_bank[:, 0:64]).then_inc(qnT_ready, 1)
            act.wait_ge(ql_ps, 1)
            for odd in range(2):
                nc.scalar.copy(qlT[:].rearrange("p c b (a o) -> p o c a b", o=2)[:, odd], turn[0][:, 512 * odd:512 * odd + 128].rearrange("p (c a b) -> p c a b", c=2, a=8)).then_inc(ql_ready, 1)
            act.wait_ge(self_ps, 1)
            nc.scalar.copy(self_s[:], m_bank[0:1, 0:B * H_C]).then_inc(self_ready, 1)

            def exps(b):
                act.wait_ge(rel_ready, b + 1)
                nc.scalar.activation(sc[:, b % 2], sc[:, b % 2], ACT.Exp, scale=MLA_SCALE).then_inc(p_ready, 1)

            for b in range(B):
                act.wait_ge(kpeT_ps, b + 1)
                nc.scalar.copy(kpeT[:].rearrange("p g n -> p (g n)"), turn[0][:, :]).then_inc(kpeT_ready, 1)
                for g in range(1, G, 2):
                    i = b * G + g
                    act.wait_ge(turn_ps, i + 1)
                    if i >= 2:
                        act.wait_ge(turn_used, i - 1)
                    nc.scalar.copy(ckvT[:, i % 2, :], turn[1 - i % 2][:, :]).then_inc(turn_act, 1)
                    if b and g == RELATIVE_AT:
                        exps(b - 1)
            exps(B - 1)
            act.wait_ge(oT_ps, 1)
            nc.scalar.copy(oT[:].rearrange("p k b -> p (k b)"), m_bank[:, 0:64]).then_inc(oT_ready, 1)

        @block.vector
        def _(dve):
            dve.wait_ge(table_in, 48)
            nc.vector.tensor_copy(table_f[:], table[:]).then_inc(table_ready, 1)
            dve.wait_ge(ids_ps, 1)
            nc.vector.tensor_scalar(row_ids[:], m_bank[:, 256:256 + NB], 128.0 / KEYS_8, part[:], ALU.mult, ALU.add).then_inc(ids_ready, 1)
            dve.wait_ge(loaded, 32)
            dve.wait_ge(qp_ps, 1)
            src = turn[1][:, 0:128].rearrange("p (h b) -> p b h", b=B)
            nc.vector.tensor_copy(qp_self[:], src[0:32]).then_inc(qp_ready, 1)
            nc.vector.tensor_tensor(qpT[:], bc(src.unsqueeze(2), [128, B, NQ, H_C]), bc(four[:].unsqueeze(1).unsqueeze(3), [128, B, NQ, H_C]), ALU.mult).then_inc(qp_ready, 1)
            dve.wait_ge(self_ready, 1)
            dve.wait_ge(consts, 2)

            def largest(b):
                dve.wait_ge(m1T_ps, b + 1)
                nc.vector.tensor_reduce(mx[:], m_bank[0:H_C, 0:128], AX.X, ALU.max).then_inc(mx_ready, 1)
                dve.wait_ge(mx_ready, b + 1)
                nc.vector.tensor_scalar(dmx[:], ident[0:H_C, 0:H_C], mx[:], None, ALU.mult).then_inc(dmx_ready, 1)

            def relative(b):
                dve.wait_ge(mb_ps, b + 1)
                nc.vector.tensor_tensor(sc[:, b % 2], sc[:, b % 2], bc(m_bank[:, 256:256 + H_C].unsqueeze(1), [128, NP + 1, H_C]), ALU.subtract).then_inc(rel_ready, 1)

            def partial_sums(b):
                dve.wait_ge(p_ready, b + 1)
                nc.vector.tensor_reduce(sums[:], sc[:, b % 2].rearrange("p g h -> p h g"), AX.X, ALU.add).then_inc(sum_ready, 1)

            def normed(b):
                dve.wait_ge(sumb_ps, b + 1)
                nc.vector.reciprocal(inv[:], m_bank[0:H_C, 288:289]).then_inc(inv_ready, 1)
                dve.wait_ge(inv_ready, b + 1)
                dve.wait_ge(o_ps, b + 1)
                nc.vector.tensor_scalar(o_n[:], o_bank[b % 2][0:H_C, 0:R_KV], inv[:], None, ALU.mult).then_inc(o_used, 1)

            def turned_out(b):
                dve.wait_ge(olT_ps, b + 1)
                nc.vector.tensor_copy(olT[:, :, :, b], o_bank[b % 2][:, R_KV:R_KV + 2 * H_C].rearrange("p (c h) -> p c h", c=2)).then_inc(olT_ready, 1)

            for b in range(B):
                for g in range(0, G, 2):
                    i = b * G + g
                    dve.wait_ge(turn_ps, i + 1)
                    if i >= 2:
                        dve.wait_ge(turn_used, i - 1)
                    nc.vector.tensor_copy(ckvT[:, i % 2, :], turn[1 - i % 2][:, :]).then_inc(turn_dve, 1)
                    if b and g == 0:
                        largest(b - 1)
                    if b and g == 2:
                        relative(b - 1)
                    if b >= 2 and g == 4:
                        normed(b - 2)
                    if b and g == 4:
                        partial_sums(b - 1)
                    if b >= 2 and g == 6:
                        turned_out(b - 2)
                dve.wait_ge(turn_used, G * (b + 1))
                own = sc[:, b % 2]
                if b >= 2:
                    dve.wait_ge(o_ps, b - 1)
                nc.vector.tensor_copy(own[:, 0:NP, :].rearrange("p g h -> p (g h)"), s_bank[:, :]).then_inc(sc_ready, 1)
                if b >= 2:
                    nc.vector.memset(own[:, NP, :], NEG_MASK).then_inc(masked, 1)
                    dve.wait_ge(masked, b - 1)
                nc.vector.tensor_copy(own[0:1, NP, :], self_s[:, H_C * b:H_C * b + H_C]).then_inc(self_put, 1)
                dve.wait_ge(self_put, b + 1)
                dve.wait_ge(sc_ready, b + 1)
                nc.vector.tensor_reduce(m1[:], own.rearrange("p g h -> p h g"), AX.X, ALU.max).then_inc(m1_ready, 1)
            largest(B - 1)
            relative(B - 1)
            normed(B - 2)
            partial_sums(B - 1)
            turned_out(B - 2)
            normed(B - 1)
            turned_out(B - 1)
            dve.wait_ge(y_ps, 1)
            nc.vector.tensor_tensor(x_sb[0:B, NT, :], x_sb[0:B, NT, :], turn[0][0:B, :], ALU.add).then_inc(y_used, 1)

        @block.tensor
        def _(pe):
            pe.wait_ge(table_ready, 1)
            nc.tensor.matmul(m_bank[:, 256:256 + NB], spread[:], table_f[:], start=True, stop=True).then_inc(ids_ps, 1)
            pe.wait_ge(ids_ready, 1)
            qn = smp["qn"][:].rearrange("p h n -> p (h n)")
            for a in range(H_C // 2):
                last = nc.tensor.transpose(m_bank[:, 8 * a:8 * a + 8], qn[:, 128 * a:128 * a + 128], ident[0:B, 0:B])
            last.then_inc(qnT_ps, 1)
            for h in range(H_C):
                last = nc.tensor.transpose(turn[1][:, 8 * h:8 * h + 8], smp["qp"][:, h].rearrange("p a d -> p (a d)"), ident[0:B, 0:B])
            last.then_inc(qp_ps, 1)
            pe.wait_ge(qnT_ready, 1)
            pe.wait_ge(loaded, 32)
            for h in range(H_C):
                rows = slice(64 * (h % 2), 64 * (h % 2) + 64)
                for c in range(2):
                    at = 512 * (h % 2) + 64 * c + 8 * (h // 2)
                    last = nc.tensor.matmul(turn[0][:, at:at + 8], w_ukT[rows, h // 2, 128 * c:128 * c + 128], qnT[rows, h // 2, :], start=True, stop=True)
            last.then_inc(ql_ps, 1)
            pe.wait_ge(ql_ready, 2)
            pe.wait_ge(qp_ready, 2)
            pe.wait_ge(kps_ready, 1)
            for b in range(B):
                dst = m_bank[0:1, H_C * b:H_C * b + H_C]
                for c in range(2):
                    nc.tensor.matmul(dst, smp["ckvT"][:, c, b:b + 1], qlT[:, c, b, :], start=(c == 0), stop=False)
                last = nc.tensor.matmul(dst, kp_self[:, b:b + 1], qp_self[:, b, :], start=False, stop=True)
            last.then_inc(self_ps, 1)
            pe.wait_ge(self_ready, 1)
            pe.wait_ge(row_in, 16)
            pe.wait_ge(consts, 1)

            def spread_max(b):
                pe.wait_ge(dmx_ready, b + 1)
                nc.tensor.matmul(m_bank[:, 256:256 + H_C], ones[0:H_C, :], dmx[:], start=True, stop=True).then_inc(mb_ps, 1)

            def turn_max(b):
                pe.wait_ge(m1_ready, b + 1)
                nc.tensor.transpose(m_bank[0:H_C, 0:128], m1[:], ident[:]).then_inc(m1T_ps, 1)

            def weighted(b, first, end):
                if first == 0:
                    pe.wait_ge(p_ready, b + 1)
                    if b >= 2:
                        pe.wait_ge(olT_ready, b - 1)
                for p in range(first, end):
                    nc.tensor.matmul(o_bank[b % 2][0:H_C, 0:R_KV], sc[:, b % 2, p, :], latent(b, p), start=(p == 0), stop=False)
                if end < NP:
                    return
                nc.tensor.matmul(o_bank[b % 2][0:H_C, 0:R_KV], sc[0:1, b % 2, NP, :], self_row[:, b, :], start=False, stop=True).then_inc(o_ps, 1)
                pe.wait_ge(sum_ready, b + 1)
                pe.wait_ge(rel_ready, min(b + 2, B))
                nc.tensor.matmul(m_bank[0:H_C, 288:289], sums[:], ones[:, 0:1], start=True, stop=True).then_inc(sumb_ps, 1)

            def turn_out(b):
                pe.wait_ge(o_used, b + 1)
                for c in range(2):
                    last = nc.tensor.transpose(o_bank[b % 2][:, R_KV + H_C * c:R_KV + H_C * c + H_C], o_n[:, 128 * c:128 * c + 128], ident[0:H_C, 0:H_C])
                last.then_inc(olT_ps, 1)

            for b in range(B):
                def turn_pages(g):
                    i = b * G + g
                    if g >= 1 or b:
                        j = i - 2
                        if g == 1:
                            pe.wait_ge(kpeT_ready, b + 1)
                        if j >= 0:
                            pe.wait_ge(turn_act if j % 2 else turn_dve, j // 2 + 1)
                    for p in range(NQ):
                        for c in range(2):
                            last = nc.tensor.transpose(turn[1 - i % 2][:, 256 * p + 128 * c:256 * p + 128 * c + 128], latent(b, NQ * g + p, c), ident[:])
                    last.then_inc(turn_ps, 1)

                def group_scores(g):
                    i = b * G + g
                    pe.wait_ge(turn_act if i % 2 else turn_dve, i // 2 + 1)
                    at = NQ * H_C * g
                    nc.tensor.matmul(s_bank[:, at:at + NQ * H_C], kpeT[:, g, :], qpT[:, b].rearrange("p a h -> p (a h)"), start=True, stop=False)
                    for p in range(NQ):
                        for c in range(2):
                            last = nc.tensor.matmul(s_bank[:, at + H_C * p:at + H_C * p + H_C], ckvT[:, i % 2, 256 * p + 128 * c:256 * p + 128 * c + 128], qlT[:, c, b, :],
                                                    start=False, stop=(c == 1 and p == NQ - 1))
                    last.then_inc(turn_used, 1)

                if b:
                    pe.wait_ge(turn_act, b * G // 2)
                for g in range(G):
                    if g % 2 == 0:
                        pe.wait_ge(past_in[b % BUFS][g // 2], 16 * (b // BUFS + 1))
                    last = nc.tensor.transpose(turn[0][:, 128 * g:128 * g + 128], past[:, b % BUFS, g // 2, KEYS_8 * R_KV + 128 * (g % 2):KEYS_8 * R_KV + 128 * (g % 2) + 128], ident[:])
                last.then_inc(kpeT_ps, 1)
                turn_pages(0)
                if b:
                    turn_max(b - 1)
                pe.wait_ge(kpeT_ready, b + 1)
                if b:
                    pe.wait_ge(sc_ready, b)
                for g in range(G):
                    if g + 1 < G:
                        turn_pages(g + 1)
                    group_scores(g)
                    if b and g == 1:
                        spread_max(b - 1)
                    if b >= 2 and g < 4:
                        weighted(b - 2, 16 + 4 * g, 20 + 4 * g)
                    if b and g >= 4:
                        weighted(b - 1, 4 * g - 16, 4 * g - 12)
                    if b >= 2 and g == 5:
                        turn_out(b - 2)
            turn_max(B - 1)
            weighted(B - 2, 16, 28)
            spread_max(B - 1)
            weighted(B - 2, 28, NP)
            weighted(B - 1, 0, NP)
            turn_out(B - 2)
            turn_out(B - 1)
            pe.wait_ge(olT_ready, B)
            pe.wait_ge(wout_in, 32)
            for h in range(H_C):
                rows = slice(64 * (h % 2), 64 * (h % 2) + 64)
                for c in range(2):
                    last = nc.tensor.matmul(m_bank[rows, 8 * (h // 2):8 * (h // 2) + 8], w_uv[:, c, 64 * h:64 * h + 64], olT[:, c, h, :], start=(c == 0), stop=(c == 1))
            last.then_inc(oT_ps, 1)
            pe.wait_ge(oT_ready, 1)
            for n in range(2):
                for k in range(KC):
                    last = nc.tensor.matmul(turn[0][0:B, 512 * n:512 * n + 512], oT[:, k, :], w_out[:, k, 512 * n:512 * n + 512], start=(k == 0), stop=(k == KC - 1))
            last.then_inc(y_ps, 1)


def sample_buffers(nc, ctx):
    def sb(name, shape):
        return ctx.enter_context(nc.sbuf_tensor("smp_" + name, shape, F32))

    return {"ckv": sb("ckv", [DEC_BATCH, R_KV]), "ckvT": sb("ckvT", [128, 2, DEC_BATCH]), "kpeT": sb("kpeT", [96, DEC_BATCH]),
            "qn": sb("qn", [DEC_BATCH, H_C, D_NOPE]), "qp": sb("qp", [DEC_BATCH, H_C, 4, D_ROPE])}


def final_norm(nc, w, out, x_sb):
    with ExitStack() as ctx:
        gain = ctx.enter_context(nc.sbuf_tensor("f_gain", [128, D_MODEL], F32))
        eps = ctx.enter_context(nc.sbuf_tensor("f_eps", [128, 1], F32))
        sq = ctx.enter_context(nc.sbuf_tensor("f_sq", [128, D_MODEL], F32))
        rstd = ctx.enter_context(nc.sbuf_tensor("f_rstd", [128, NT + 1], F32))
        sem = signals(nc, ctx, "f_")
        gain_in, eps_set, sq_ready, root_ready, inv_ready, y_ready, y_out = (sem(n) for n in (
            "gain_in", "eps_set", "sq_ready", "root_ready", "inv_ready", "y_ready", "y_out"))
        block = ctx.enter_context(nc.Block())

        @block.gpsimd
        def _(pool):
            nc.gpsimd.memset(eps[:], EPS).then_inc(eps_set, 1)

        @block.sync
        def _(sp):
            sp.dma_start(gain[:], w["final_norm"].unsqueeze(0).to_broadcast([128, D_MODEL])).then_inc(gain_in, 16)
            for t in range(NT + 1):
                sp.wait_ge(y_ready, t + 1)
                dst = out["y_prompt"][0, 128 * t:128 * t + 128, :] if t < NT else out["y_sample"][:, 0, :]
                sp.dma_start(dst, x_sb[0:rows_of(t), t, :]).then_inc(y_out, 16)
            sp.wait_ge(y_out, 16 * (NT + 1))

        @block.scalar
        def _(act):
            act.wait_ge(eps_set, 1)
            for t in range(NT + 1):
                n = rows_of(t)
                if t:
                    act.wait_ge(sq_ready, t)
                nc.scalar.activation(sq[0:n, :], x_sb[0:n, t, :], ACT.Square, scale=D_MODEL ** -0.5, accum_out=rstd[0:n, t:t + 1]).then_inc(sq_ready, 1)
                act.wait_ge(sq_ready, t + 1)
                nc.scalar.activation(rstd[0:n, t:t + 1], rstd[0:n, t:t + 1], ACT.Sqrt, bias=eps[0:n, :]).then_inc(root_ready, 1)

        @block.vector
        def _(dve):
            dve.wait_ge(gain_in, 16)
            for t in range(NT + 1):
                n = rows_of(t)
                dve.wait_ge(root_ready, t + 1)
                nc.vector.reciprocal(rstd[0:n, t:t + 1], rstd[0:n, t:t + 1]).then_inc(inv_ready, 1)
                dve.wait_ge(inv_ready, t + 1)
                nc.vector.scalar_tensor_tensor(out=x_sb[0:n, t, :], in0=x_sb[0:n, t, :], scalar=rstd[0:n, t:t + 1], in1=gain[0:n, :],
                                               op0=ALU.mult, op1=ALU.mult).then_inc(y_ready, 1)


def constants():
    p = np.arange(128)
    masks = np.zeros((128, LEVELS + 1, 128), np.int32)
    for l in range(LEVELS):
        hf = 64 >> l
        masks[:, l, :] = ((p[:, None] // (2 * hf) == p[None, :] // (2 * hf))
                          & (p[:, None] // hf % 2 == 0) & (p[None, :] // hf % 2 == 1))
    masks[:, LEVELS, :] = np.eye(128)
    pos = np.full((128, NT + 1), PAST_LEN, np.float32)
    pos[:, 0:NT] = 128 * np.arange(NT)[None, :] + p[:, None]
    inv = np.power(np.float32(ROPE_BASE), -np.arange(D_ROPE // 2, dtype=np.float32) / np.float32(D_ROPE // 2)).astype(np.float32)
    ang = (pos[:, :, None] * inv).astype(np.float32)
    cos, sin = np.cos(ang).astype(np.float32), np.sin(ang).astype(np.float32)
    return {"cos2": np.concatenate([cos, cos], axis=2), "sin2": np.concatenate([-sin, sin], axis=2),
            "causal": np.where(p[None, :] <= p[:, None], 0.0, NEG_MASK).astype(np.float32),
            "four": (p[:, None] // D_ROPE == np.arange(4)[None, :]).astype(np.float32),
            "ident": np.eye(128, dtype=np.float32), "level_masks": masks,
            "own_seq": np.eye(DEC_BATCH, dtype=np.float32),
            "iota16": np.tile(np.arange(TOPK, dtype=np.float32), (128, 1)),
            "spread": (p[None, :] // TOPK == np.arange(DEC_BATCH)[:, None]).astype(np.float32),
            "gatherT": (p[:, None] // TOPK == np.arange(DEC_BATCH)[None, :]).astype(np.float32),
            "sixteenth": (p % TOPK).astype(np.float32)[:, None],
            "own_k": (p[:, None] % TOPK == np.arange(TOPK)[None, :]).astype(np.float32)}


def laid_out(a):
    def cols(v):
        return np.ascontiguousarray(v.reshape(-1, 128).T)

    return {
        "ab_norm_cols": lambda: cols(a["ab_norm"][0]),
        "conv_w_cols": lambda: np.ascontiguousarray(a["conv_w"][0].reshape(CONV_W, 4, 128).transpose(2, 1, 0)),
        "chan_cols": lambda: np.ascontiguousarray(np.stack([cols(a[n][0]) for n in ("conv_b", "conv_ln_g", "conv_ln_b")], axis=1)),
        "gate_b_cols": lambda: cols(a["gla_b_gate"][0]),
        "c_norm_cols": lambda: cols(a["c_norm"][0]),
        "q_norm_cols": lambda: cols(a["c_q_norm"][0]),
        "w_ukT": lambda: np.ascontiguousarray(a["c_w_uk"][0].reshape(R_KV, H_C // 2, 128).transpose(2, 1, 0)),
        "keysT": lambda: np.ascontiguousarray(a["peer_keys"].transpose(0, 4, 1, 2, 3)).reshape(2, N_KEYS, -1),
        "peer_uv0": lambda: np.concatenate([a["peer_u"][0], a["peer_v"][0]], axis=1),
        "peer_uv1": lambda: np.concatenate([a["peer_u"][1], a["peer_v"][1]], axis=1),
        "cache_rows": lambda: np.concatenate([a["cache_ckv"][0].reshape(-1, 8 * R_KV), a["cache_kpe"][0].reshape(-1, 8 * D_ROPE)], axis=1),
        "page_cols": lambda: np.ascontiguousarray(a["page_table"].reshape(-1, 8).T),
        "state_conv_cols": lambda: np.ascontiguousarray(a["state_conv"][0].reshape(DEC_BATCH, PAD, 4, 128).transpose(3, 2, 0, 1)),
    }


def program(nc, w, out):
    with ExitStack() as ctx:
        ident = ctx.enter_context(nc.sbuf_tensor("ident", [128, 128], F32))
        x_sb = ctx.enter_context(nc.sbuf_tensor("x_sb", [128, NT + 1, D_MODEL], F32))
        x_in = ctx.enter_context(nc.semaphore("x_in"))
        with nc.Block() as block:
            @block.sync
            def _(sp):
                sp.dma_start(ident[:], w["ident"]).then_inc(x_in, 16)
                for t in range(NT):
                    sp.dma_start(x_sb[:, t, :], w["x_prompt"][0, 128 * t:128 * t + 128, :]).then_inc(x_in, 16)
                sp.dma_start(x_sb[0:DEC_BATCH, NT, :], w["x_sample"][:, 0, :]).then_inc(x_in, 16)
                sp.wait_ge(x_in, 16 * (NT + 2))
        even_layer(nc, w, out, ident, x_sb)
        peer_layer(nc, w, 0, ident, x_sb)
        with ExitStack() as odd:
            smp = sample_buffers(nc, odd)
            latent_projections(nc, w, out, ident, x_sb, smp)
            latent_sample(nc, w, ident, x_sb, smp)
        peer_layer(nc, w, 1, ident, x_sb)
        final_norm(nc, w, out, x_sb)


_USED = ['ab_norm_cols', 'ab_w_in', 'ab_w_out', 'c_kv_norm', 'c_norm_cols', 'c_w_in', 'c_w_out', 'c_w_q_b', 'c_w_uk', 'c_w_uv', 'cache_rows', 'causal', 'chan_cols', 'conv_w_cols', 'cos2', 'ffn_norm', 'final_norm', 'four', 'gate_b_cols', 'gatherT', 'gla_head_g', 'gla_w_gate', 'ident', 'iota16', 'keysT', 'level_masks', 'own_k', 'own_seq', 'page_cols', 'peer_uv0', 'peer_uv1', 'peer_w_q', 'q_norm_cols', 'sin2', 'sixteenth', 'spread', 'state_conv', 'state_conv_cols', 'state_gla', 'w_ukT', 'x_prompt', 'x_sample']
_OUTS = {"y_prompt": (1, SEQ, D_MODEL), "y_sample": (DEC_BATCH, 1, D_MODEL),
         "new_ckv_prompt": (1, 1, SEQ, R_KV), "new_kpe_prompt": (1, 1, SEQ, D_ROPE),
         "new_ckv_sample": (1, DEC_BATCH, 1, R_KV), "new_kpe_sample": (1, DEC_BATCH, 1, D_ROPE),
         "new_conv_prompt": (1, 1, PAD, D_A), "new_conv_sample": (1, DEC_BATCH, PAD, D_A),
         "new_gla_prompt": (1, 1, H_B, DK_B, DV_B), "new_gla_sample": (1, DEC_BATCH, H_B, DK_B, DV_B)}


def kernel(**inputs):
    import concourse.bacc as _bacc
    from concourse import mybir as _mybir
    from concourse.bass_utils import run_bass_kernel_spmd as _run

    arrays = {name: np.ascontiguousarray(a) for name, a in inputs.items() if name in _USED}
    arrays.update((k, a) for k, a in constants().items() if k in _USED)
    arrays.update((k, f()) for k, f in laid_out({n: np.asarray(a) for n, a in inputs.items()}).items() if k in _USED)
    nc = _bacc.Bacc("TRN2", target_bir_lowering=False, num_devices=1)
    w = {n: nc.dram_tensor("in_" + n, a.shape, _mybir.dt.from_np(a.dtype), kind="ExternalInput").ap() for n, a in arrays.items()}
    out = {n: nc.dram_tensor("out_" + n, shape, F32, kind="ExternalOutput").ap() for n, shape in _OUTS.items()}
    program(nc, w, out)
    r = _run(nc, [{"in_" + n: a for n, a in arrays.items()}], core_ids=[0])
    return tuple(r.results[0]["out_" + n] for n in _OUTS)
```
